# Optimizing a Trainium2 kernel written in Bass

```python
import math
import jax, jax.numpy as jnp
from jax import lax
import numpy as np

D_MODEL = 1024
BATCH = 1
SEQ = 512
DEPTH = 1
DEC_BATCH = 1
DEC_SEQ = 32
PAST_LEN = 128

CHUNK = 64
QBLOCK = 128
H_D = 4
DK_D = 64
DV_D = 128
H_R = 4
DK_R = 128
DV_R = 128
MIX_WIDTH = H_D * DV_D + H_R * DV_R
IN_COLS = 2 * H_D * 2 * DK_D + H_D * DV_D + 2 * H_R * DK_R + 2 * H_R * DV_R
N_MEM = 256
H_X = 4
HD_X = D_MODEL // H_X
PEER_HEADS = 8
N_KEYS = 128
N_EXPERTS = N_KEYS * N_KEYS
PEER_TOPK = 16
D_KEY = 256
PEER_BLOCK = 256
EPS = 1e-6

kernel_name = 'hybrid_diffattn_retnet_peer_stream_step'

def rmsnorm(x, g):
    xf = x.astype(jnp.float32)
    y = xf * lax.rsqrt(jnp.mean(xf * xf, axis=-1, keepdims=True) + EPS)
    return (y * g.astype(jnp.float32)).astype(x.dtype)

def project_mixer(hn, w_in):
    B, T = hn.shape[0], hn.shape[1]
    y = hn @ w_in
    sizes = [H_D * 2 * DK_D, H_D * 2 * DK_D, H_D * DV_D, H_R * DK_R, H_R * DK_R, H_R * DV_R, H_R * DV_R]
    splits = np.cumsum(sizes)[:-1].tolist()
    qd, kd, vd, qr, kr, vr, gr = jnp.split(y, splits, axis=-1)
    return (qd.reshape(B, T, H_D, 2, DK_D), kd.reshape(B, T, H_D, 2, DK_D), vd.reshape(B, T, H_D, DV_D),
            qr.reshape(B, T, H_R, DK_R), kr.reshape(B, T, H_R, DK_R) * (DK_R ** -0.5),
            vr.reshape(B, T, H_R, DV_R), gr)

def alibi_slopes():
    return 2.0 ** (-8.0 * jnp.arange(1, H_D + 1, dtype=jnp.float32) / H_D)

def diff_lambda(lq1, lk1, lq2, lk2, lam_init):
    f = lambda a: a.astype(jnp.float32)
    return jnp.exp(jnp.sum(f(lq1) * f(lk1))) - jnp.exp(jnp.sum(f(lq2) * f(lk2))) + lam_init

def diff_core(q, k, v, qpos, kpos, lam, mask):
    s = jnp.einsum('bqhmd,bkhmd->mbhqk', q.astype(jnp.float32), k.astype(jnp.float32)) * (DK_D ** -0.5)
    dist = jnp.abs(qpos[:, None] - kpos[None, :]).astype(jnp.float32)
    s = s - alibi_slopes()[None, None, :, None, None] * dist
    if mask is not None:
        s = jnp.where(mask, s, -1e30)
    p = jax.nn.softmax(s, axis=-1)
    a = p[0] - lam * p[1]
    return jnp.einsum('bhqk,bkhe->bqhe', a, v.astype(jnp.float32))

def diff_post(o, lam_init, g):
    B, T = o.shape[0], o.shape[1]
    y = o * lax.rsqrt(jnp.mean(o * o, axis=-1, keepdims=True) + EPS) * g.astype(jnp.float32) * (1.0 - lam_init)
    return y.reshape(B, T, H_D * DV_D)

def ret_chunk(S, q, k, v):
    L = q.shape[1]
    log_g = jnp.log1p(-(2.0 ** (-5.0 - jnp.arange(H_R, dtype=jnp.float32))))
    i = jnp.arange(L, dtype=jnp.float32)
    diff = i[:, None] - i[None, :]
    decay = jnp.where(diff >= 0, jnp.exp(jnp.maximum(diff, 0.0)[None] * log_g[:, None, None]), 0.0)
    inner = jnp.einsum('bihd,bjhd->bhij', q, k) * decay[None]
    cross_scale = jnp.exp((i[:, None] + 1.0) * log_g[None, :])
    o = jnp.einsum('bhij,bjhe->bihe', inner, v) + jnp.einsum('bihd,bhde->bihe', q, S) * cross_scale[None, :, :, None]
    tail = jnp.exp((L - 1.0 - i)[:, None] * log_g[None, :])
    S_new = jnp.exp(L * log_g)[None, :, None, None] * S + jnp.einsum('bjhd,bjhe,jh->bhde', k, v, tail)
    return S_new, o

def ret_post(o, gate, g):
    B, T = o.shape[0], o.shape[1]
    mu = jnp.mean(o, axis=-1, keepdims=True)
    oc = o - mu
    y = oc * lax.rsqrt(jnp.mean(oc * oc, axis=-1, keepdims=True) + EPS) * g.astype(jnp.float32)
    return y.reshape(B, T, H_R * DV_R) * jax.nn.silu(gate.astype(jnp.float32))

def mem_kv(mem, g_mem, w_xk, w_xv):
    B = mem.shape[0]
    mn = rmsnorm(mem, g_mem)
    return (mn @ w_xk).reshape(B, N_MEM, H_X, HD_X), (mn @ w_xv).reshape(B, N_MEM, H_X, HD_X)

def cross_attn(hn, mk, mv, w_xq, w_xo):
    B, T = hn.shape[0], hn.shape[1]
    q = (hn @ w_xq).reshape(B, T, H_X, HD_X)
    s = jnp.einsum('bthd,bmhd->bhtm', q.astype(jnp.float32), mk.astype(jnp.float32)) * (HD_X ** -0.5)
    p = jax.nn.softmax(s, axis=-1)
    o = jnp.einsum('bhtm,bmhd->bthd', p, mv.astype(jnp.float32)).reshape(B, T, D_MODEL)
    return o.astype(hn.dtype) @ w_xo

def peer(h, w_pq, pk1, pk2, u_tab, v_tab):
    B, T, D = h.shape
    n = B * T
    pad = (-n) % PEER_BLOCK
    blocks = jnp.pad(h.reshape(n, D), ((0, pad), (0, 0))).reshape(-1, PEER_BLOCK, D)

    def one_block(hb):
        q = (hb @ w_pq).astype(jnp.float32).reshape(PEER_BLOCK, PEER_HEADS, 2, D_KEY // 2)
        s1 = jnp.einsum('tpd,pnd->tpn', q[:, :, 0], pk1.astype(jnp.float32))
        s2 = jnp.einsum('tpd,pnd->tpn', q[:, :, 1], pk2.astype(jnp.float32))
        v1, i1 = lax.top_k(s1, PEER_TOPK)
        v2, i2 = lax.top_k(s2, PEER_TOPK)
        cand = (v1[..., :, None] + v2[..., None, :]).reshape(PEER_BLOCK, PEER_HEADS, PEER_TOPK * PEER_TOPK)
        cidx = (i1[..., :, None] * N_KEYS + i2[..., None, :]).reshape(PEER_BLOCK, PEER_HEADS, PEER_TOPK * PEER_TOPK)
        sc, pos = lax.top_k(cand, PEER_TOPK)
        e = jnp.take_along_axis(cidx, pos, axis=-1)
        gate = jax.nn.softmax(sc, axis=-1)
        u = jnp.take(u_tab, e, axis=0).astype(jnp.float32)
        act = jax.nn.gelu(jnp.einsum('tpkd,td->tpk', u, hb.astype(jnp.float32)), approximate=False)
        vv = jnp.take(v_tab, e, axis=0).astype(jnp.float32)
        return jnp.einsum('tpk,tpkd->td', gate * act, vv).astype(h.dtype)

    out = lax.map(one_block, blocks).reshape(-1, D)[:n]
    return out.reshape(B, T, D)

def setup_inputs(seed: int = 0) -> dict:
    key = jax.random.key(seed)
    ks = jax.random.split(key, 32)
    nrm = lambda k, shape, s: jax.random.normal(k, shape, jnp.float32) * s
    gain = lambda k, shape: 1.0 + 0.01 * jax.random.normal(k, shape, jnp.float32)
    return {
        'x_prompt': nrm(ks[0], (BATCH, SEQ, D_MODEL), 1.0),
        'x_sample': nrm(ks[1], (DEC_BATCH, DEC_SEQ, D_MODEL), 1.0),
        'mem_prompt': nrm(ks[2], (BATCH, N_MEM, D_MODEL), 1.0),
        'cache_da_k': nrm(ks[3], (DEPTH, DEC_BATCH, PAST_LEN, H_D, 2, DK_D), 1.0),
        'cache_da_v': nrm(ks[4], (DEPTH, DEC_BATCH, PAST_LEN, H_D, DV_D), 1.0),
        'state_ret': nrm(ks[5], (DEPTH, DEC_BATCH, H_R, DK_R, DV_R), 1.0),
        'cache_mem_k': nrm(ks[6], (DEPTH, DEC_BATCH, N_MEM, H_X, HD_X), 1.0),
        'cache_mem_v': nrm(ks[7], (DEPTH, DEC_BATCH, N_MEM, H_X, HD_X), 1.0),
        'g_mix': gain(ks[8], (DEPTH, D_MODEL)),
        'w_in': nrm(ks[9], (DEPTH, D_MODEL, IN_COLS), D_MODEL ** -0.5),
        'lam_q1': nrm(ks[10], (DEPTH, DK_D), 0.1),
        'lam_k1': nrm(ks[11], (DEPTH, DK_D), 0.1),
        'lam_q2': nrm(ks[12], (DEPTH, DK_D), 0.1),
        'lam_k2': nrm(ks[13], (DEPTH, DK_D), 0.1),
        'g_da': gain(ks[14], (DEPTH, H_D, DV_D)),
        'g_ret': gain(ks[15], (DEPTH, H_R, DV_R)),
        'w_out': nrm(ks[16], (DEPTH, MIX_WIDTH, D_MODEL), MIX_WIDTH ** -0.5),
        'g_cross': gain(ks[17], (DEPTH, D_MODEL)),
        'g_mem': gain(ks[18], (DEPTH, D_MODEL)),
        'w_xq': nrm(ks[19], (DEPTH, D_MODEL, D_MODEL), D_MODEL ** -0.5),
        'w_xk': nrm(ks[20], (DEPTH, D_MODEL, D_MODEL), D_MODEL ** -0.5),
        'w_xv': nrm(ks[21], (DEPTH, D_MODEL, D_MODEL), D_MODEL ** -0.5),
        'w_xo': nrm(ks[22], (DEPTH, D_MODEL, D_MODEL), D_MODEL ** -0.5),
        'g_ffn': gain(ks[23], (DEPTH, D_MODEL)),
        'w_pq': nrm(ks[24], (DEPTH, D_MODEL, PEER_HEADS * D_KEY), D_MODEL ** -0.5),
        'peer_k1': nrm(ks[25], (DEPTH, PEER_HEADS, N_KEYS, D_KEY // 2), (D_KEY // 2) ** -0.5),
        'peer_k2': nrm(ks[26], (DEPTH, PEER_HEADS, N_KEYS, D_KEY // 2), (D_KEY // 2) ** -0.5),
        'peer_u': nrm(ks[27], (DEPTH, N_EXPERTS, D_MODEL), D_MODEL ** -0.5),
        'peer_v': nrm(ks[28], (DEPTH, N_EXPERTS, D_MODEL), PEER_HEADS ** -0.5),
        'g_final': gain(ks[29], (D_MODEL,)),
    }

def reference(x_prompt, x_sample, mem_prompt, cache_da_k, cache_da_v, state_ret, cache_mem_k, cache_mem_v,
              g_mix, w_in, lam_q1, lam_k1, lam_q2, lam_k2, g_da, g_ret, w_out, g_cross, g_mem,
              w_xq, w_xk, w_xv, w_xo, g_ffn, w_pq, peer_k1, peer_k2, peer_u, peer_v, g_final):
    x = x_prompt
    B, T = x.shape[0], x.shape[1]
    pos = jnp.arange(T)
    kp_list, vp_list, sp_list, mkp_list, mvp_list = [], [], [], [], []
    for l in range(DEPTH):
        lam_init = 0.8 - 0.6 * math.exp(-0.3 * l)
        lam = diff_lambda(lam_q1[l], lam_k1[l], lam_q2[l], lam_k2[l], lam_init)
        hn = rmsnorm(x, g_mix[l])
        qd, kd, vd, qr, kr, vr, gr = project_mixer(hn, w_in[l])

        def attn_block(i, qd=qd, kd=kd, vd=vd, lam=lam):
            qb = lax.dynamic_slice_in_dim(qd, i * QBLOCK, QBLOCK, axis=1)
            qpos = i * QBLOCK + jnp.arange(QBLOCK)
            mask = (qpos // CHUNK)[:, None] >= (pos // CHUNK)[None, :]
            return diff_core(qb, kd, vd, qpos, pos, lam, mask)

        od = lax.map(attn_block, jnp.arange(T // QBLOCK))
        od = jnp.moveaxis(od, 0, 1).reshape(B, T, H_D, DV_D)

        to_chunks = lambda a: jnp.moveaxis(a.astype(jnp.float32).reshape(B, T // CHUNK, CHUNK, a.shape[2], a.shape[3]), 1, 0)
        S0 = jnp.zeros((B, H_R, DK_R, DV_R), jnp.float32)
        S_fin, orr = lax.scan(lambda S, qkv: ret_chunk(S, qkv[0], qkv[1], qkv[2]), S0,
                              (to_chunks(qr), to_chunks(kr), to_chunks(vr)))
        orr = jnp.moveaxis(orr, 0, 1).reshape(B, T, H_R, DV_R)

        mixed = jnp.concatenate([diff_post(od, lam_init, g_da[l]), ret_post(orr, gr, g_ret[l])], axis=-1)
        x = x + mixed.astype(x.dtype) @ w_out[l]
        mk, mv = mem_kv(mem_prompt, g_mem[l], w_xk[l], w_xv[l])
        x = x + cross_attn(rmsnorm(x, g_cross[l]), mk, mv, w_xq[l], w_xo[l])
        x = x + peer(rmsnorm(x, g_ffn[l]), w_pq[l], peer_k1[l], peer_k2[l], peer_u[l], peer_v[l])
        kp_list.append(kd)
        vp_list.append(vd)
        sp_list.append(S_fin)
        mkp_list.append(mk)
        mvp_list.append(mv)
    y_prompt = rmsnorm(x, g_final)

    xs = x_sample
    Bs, Ts = xs.shape[0], xs.shape[1]
    qpos_s = PAST_LEN + jnp.arange(Ts)
    kpos_s = jnp.arange(PAST_LEN + Ts)
    ks_list, vs_list, ss_list = [], [], []
    for l in range(DEPTH):
        lam_init = 0.8 - 0.6 * math.exp(-0.3 * l)
        lam = diff_lambda(lam_q1[l], lam_k1[l], lam_q2[l], lam_k2[l], lam_init)
        hn = rmsnorm(xs, g_mix[l])
        qd, kd, vd, qr, kr, vr, gr = project_mixer(hn, w_in[l])
        k_all = jnp.concatenate([cache_da_k[l].astype(kd.dtype), kd], axis=1)
        v_all = jnp.concatenate([cache_da_v[l].astype(vd.dtype), vd], axis=1)
        od = diff_core(qd, k_all, v_all, qpos_s, kpos_s, lam, None)
        S_new, orr = ret_chunk(state_ret[l].astype(jnp.float32), qr.astype(jnp.float32),
                               kr.astype(jnp.float32), vr.astype(jnp.float32))
        mixed = jnp.concatenate([diff_post(od, lam_init, g_da[l]), ret_post(orr, gr, g_ret[l])], axis=-1)
        xs = xs + mixed.astype(xs.dtype) @ w_out[l]
        xs = xs + cross_attn(rmsnorm(xs, g_cross[l]), cache_mem_k[l], cache_mem_v[l], w_xq[l], w_xo[l])
        xs = xs + peer(rmsnorm(xs, g_ffn[l]), w_pq[l], peer_k1[l], peer_k2[l], peer_u[l], peer_v[l])
        ks_list.append(kd)
        vs_list.append(vd)
        ss_list.append(S_new)
    y_sample = rmsnorm(xs, g_final)

    new_da_k_prompt = jnp.stack(kp_list)
    new_da_v_prompt = jnp.stack(vp_list)
    new_ret_state_prompt = jnp.stack(sp_list)
    new_mem_k_prompt = jnp.stack(mkp_list)
    new_mem_v_prompt = jnp.stack(mvp_list)
    new_da_k_sample = jnp.stack(ks_list)
    new_da_v_sample = jnp.stack(vs_list)
    new_ret_state_sample = jnp.stack(ss_list)
    return (y_prompt, y_sample, new_da_k_prompt, new_da_v_prompt, new_ret_state_prompt, new_mem_k_prompt, new_mem_v_prompt, new_da_k_sample, new_da_v_sample, new_ret_state_sample)


_drawn_inputs = setup_inputs


def setup_inputs(seed=0):
    import zlib

    import numpy as np

    out = dict(_drawn_inputs(seed))
    spreads = {}
    factors = {'g_mix': 2.877,
     'lam_q1': 5.719,
     'g_da': 19.953,
     'g_ret': 5.601,
     'g_cross': 8.0,
     'g_mem': 5.785,
     'g_ffn': 29.264,
     'g_final': 34.167,
     'cache_da_k': 7.273,
     'cache_da_v': 8.0}
    for name, (base, spread) in spreads.items():
        noise = np.random.default_rng([zlib.crc32(name.encode()), seed]).standard_normal(out[name].shape)
        drawn = base * np.exp(spread * noise) if base else spread * noise
        out[name] = __import__('jax').numpy.asarray(drawn.astype(out[name].dtype))
    for name, factor in factors.items():
        out[name] = (out[name] * factor).astype(out[name].dtype)
    return out
```

```python
from contextlib import ExitStack

import numpy as np

import concourse.bass as bass
from concourse import mybir

ALU = mybir.AluOpType
ACT = mybir.ActivationFunctionType
AX_X = mybir.AxisListType.X
F32 = mybir.dt.float32
U32 = mybir.dt.uint32

P = 128
D = 1024
C = D // P
TP, TS = 512, 32
T = TP + TS
HT = T // 2
TILES = [(0, 128), (128, 128), (256, 128), (384, 128), (512, 32)]
NT = len(TILES)
HEADS = 4
DK = 64
PAST = 128
CHUNK = 64
MEM = 256
PH = 8
KEYS = 128
TOPK = 16
EPS = 1e-6
LAM_INIT = 0.8 - 0.6
NEG = -1e30
FLOOR = -3.0e38

SLOPE8, G_DA, G_RET, GAMMA_L, GAMMA_LS, TAIL, TAIL_S = range(7)
NPAR = 8
QD, KD, VD, QR, KR, VR, GR = range(7)
NB_IN = 7
NB_X = 6

GROUP = 4
TOK8 = 8
CTOK = GROUP * TOK8
NCHUNK = T // CTOK
U2_GROUPS = NCHUNK
U1_GROUPS = KEYS // GROUP - U2_GROUPS


class Steps:

    def __init__(self, eng, sem):
        self.eng, self.sem, self.here = eng, sem, 0

    def restart(self):
        self.eng.sem_clear(self.sem)
        self.here = 0

    def link(self, ins):
        ins.then_inc(self.sem, 1)
        self.here += 1
        self.eng.wait_ge(self.sem, self.here)


def encoder_step(nc, d):
    with ExitStack() as whole:
        def sem(name):
            return whole.enter_context(nc.semaphore(name))

        def keep(name, shape, dt=F32):
            return whole.enter_context(nc.sbuf_tensor(name, shape, dt))

        xT = keep("xT", [P, C, T])
        hT = keep("hT", [P, C, T])
        sq = keep("sq", [P, 2, T])
        rms = keep("rms", [P, T])
        ident = keep("ident", [P, P])
        ones = keep("ones", [P, P])
        eps = keep("eps", [P, 2])
        gains = keep("gains", [P, 5, C])
        par = keep("par", [P, HEADS, NPAR])
        iota = keep("iota", [P, P])
        lam_in = keep("lam_in", [P, 4, DK])
        lam = keep("lam", [P, 4])
        bank = [whole.enter_context(nc.psum_tensor(f"bank{b}", [P, 512], F32)) for b in range(8)]

        x_landed, const_landed = sem("x_landed"), sem("const_landed")
        w_landed = [sem(f"w_landed{s}") for s in range(NB_IN)]
        sq_ready, sq_used, rms_ready = sem("sq_ready"), sem("sq_used"), sem("rms_ready")
        h_ready = sem("h_ready")
        vec, passed = sem("vec_steps"), sem("waits_passed")
        lam_ready = sem("lam_ready")
        out_stored = sem("out_stored")
        in_done, in_taken = sem("in_done"), sem("in_taken")
        cache_landed = sem("cache_landed")
        s_ready, s_taken, max_ready, e_ready = sem("s_ready"), sem("s_taken"), sem("max_ready"), sem("e_ready")
        a_ready, at_ready, at_taken, pv_ready, pv_taken = (
            sem("a_ready"), sem("at_ready"), sem("at_taken"), sem("pv_ready"), sem("pv_taken"))
        par_ready = sem("par_ready")
        dsq_ready, dss_ready, drms_ready, mixed_ready = (
            sem("dsq_ready"), sem("dss_ready"), sem("drms_ready"), sem("mixed_ready"))
        kt_ready, kn_ready, inner_ready, im_ready = (
            sem("kt_ready"), sem("kn_ready"), sem("inner_ready"), sem("im_ready"))
        qs_ready, u_ready, st_ready, ro_ready, ro_copied, mean_ready, oc_ready = (
            sem("qs_ready"), sem("u_ready"), sem("st_ready"), sem("ro_ready"), sem("ro_copied"),
            sem("mean_ready"), sem("oc_ready"))
        kd_stored, vd_stored, st_stored = sem("kd_stored"), sem("vd_stored"), sem("st_stored")
        wo_done, wo_taken = sem("wo_done"), sem("wo_taken")
        xo_done, xo_taken = sem("xo_done"), sem("xo_taken")
        mem_landed = sem("mem_landed")
        x_done, x_taken = sem("x_done"), sem("x_taken")
        cm_landed = sem("cm_landed")
        xs_ready, xmax_ready, xe_ready, xp_ready, xt_ready, xt_taken, xpv_ready, xpv_taken = (
            sem("xs_ready"), sem("xmax_ready"), sem("xe_ready"), sem("xp_ready"), sem("xt_ready"),
            sem("xt_taken"), sem("xpv_ready"), sem("xpv_taken"))
        mk_stored, mv_stored = sem("mk_stored"), sem("mv_stored")
        pq_done, pq_taken = sem("pq_done"), sem("pq_taken")
        pk_landed = [sem("pk_landed0"), sem("pk_landed1")]
        sc_ready, sc_taken, sc_used = sem("sc_ready"), sem("sc_taken"), sem("sc_used")
        dif_ready, gexp_ready, sel_ready, selT_ready, selT_taken = (
            sem("dif_ready"), sem("gexp_ready"), sem("sel_ready"), sem("selT_ready"), sem("selT_taken"))
        u_landed = [sem(f"u_landed{j}") for j in range(GROUP)]
        z_ready, z_taken = sem("z_ready"), sem("z_taken")
        act_stored = [sem(f"act_stored{j}") for j in range(GROUP)]
        hot_ready, g_ready, g_taken = sem("hot_ready"), sem("g_ready"), sem("g_taken")
        kd_free, vd_free, st_free, mk_free, mv_free = (
            sem("kd_free"), sem("vd_free"), sem("st_free"), sem("mk_free"), sem("mv_free"))
        g_free = [sem("g_free0"), sem("g_free1")]
        g_stored = [sem("g_stored0"), sem("g_stored1")]
        v_landed = [sem("v_landed0"), sem("v_landed1")]
        ag_landed = [sem("ag_landed0"), sem("ag_landed1")]
        w_ready, y_ready, y_taken = sem("w_ready"), sem("y_ready"), sem("y_taken")

        front = ExitStack()

        def fr(name, shape, dt=F32):
            return front.enter_context(nc.sbuf_tensor(name, shape, dt))

        wring = fr("wring", [P, NB_IN, C, P])
        dist = fr("dist", [P, TP])
        dist_s = fr("dist_s", [P, PAST + TS])
        decay = fr("decay", [P, HEADS, P])
        cross_scale = fr("cross_scale", [P, HEADS, P])
        mixedT = fr("mixedT", [P, C, T])
        memT = fr("memT", [P, C, MEM])
        memn = fr("memn", [P, C, MEM])
        hp = fr("hp", [P, NPAR])
        qdT, kdT, qrT, krT, grT = (fr(n, [P, T]) for n in ("qdT", "kdT", "qrT", "krT", "grT"))
        vd, vr, kn = (fr(n, [P, NT, P]) for n in ("vd", "vr", "kn"))
        ck, cv, st_in = fr("ck", [P, PAST]), fr("cv", [P, P]), fr("st_in", [P, P])
        S = fr("S", [P, 2, 2, TP])
        mx, nmx, rs, ri = (fr(n, [P, 2, 2]) for n in ("mx", "nmx", "rs", "ri"))
        aT = fr("aT", [P, TP])
        od = fr("od", [P, T])
        sqo = fr("sqo", [P, T])
        rmo = fr("rmo", [P, T])
        qs = fr("qs", [P, T])
        im = fr("im", [P, TP + TS])
        st = fr("st", [P, NT, P])
        ro = fr("ro", [P, T])
        mkT, mv = fr("mkT", [P, 2, MEM]), fr("mv", [P, 2, MEM])
        cmk, cmv = fr("cmk", [P, 2, MEM]), fr("cmv", [P, 2, MEM])
        xqT = fr("xqT", [P, 2, T])
        E = fr("E", [P, 2, MEM])
        eT = fr("eT", [P, MEM])
        xm, xn, xr = (fr(n, [P, 2]) for n in ("xm", "xn", "xr"))
        front.close()

        peer = ExitStack()

        def pe_(name, shape, dt=F32):
            return peer.enter_context(nc.sbuf_tensor(name, shape, dt))

        pring = pe_("pring", [P, 4, C, P])
        pk = pe_("pk", [P, 2, 2, KEYS])
        qpT = pe_("qpT", [P, 2, T])
        sc = pe_("sc", [P, 2, 2, NT, KEYS])
        scr = pe_("scr", [P, TOPK * TOPK])
        v16 = pe_("v16", [P, 2, NT, TOPK])
        i16 = pe_("i16", [P, 2, NT, TOPK], U32)
        cand = pe_("cand", [P, TOPK, TOPK])
        c16 = pe_("c16", [P, NT, TOPK])
        p16 = pe_("p16", [P, NT, TOPK], U32)
        best = pe_("best", [P, NT, PH, TOPK])
        pos = pe_("pos", [P, NT, PH, TOPK], U32)
        key1 = pe_("key1", [P, NT, PH, TOPK])
        key2 = pe_("key2", [P, NT, PH, TOPK])
        rank = pe_("rank", [P, 2, PH * TOPK], U32)
        rankf = pe_("rankf", [P, 2, PH * TOPK])
        hit = pe_("hit", [P, PH * TOPK, TOPK])
        dif = pe_("dif", [P, PH, TOPK])
        gsum = pe_("gsum", [P, PH])
        sel = pe_("sel", [P, NT, 3, P])
        selT = pe_("selT", [P, 3, NT * P])
        uring = pe_("uring", [P, GROUP, C, P])
        actb = pe_("actb", [P, GROUP, T])
        hot2 = pe_("hot2", [P, 2, TOK8, KEYS])
        hot1 = pe_("hot1", [P, 2, TOK8, KEYS])
        gst = pe_("gst", [P, 2, KEYS, CTOK])
        peer.close()

        last = ExitStack()

        def la(name, shape, dt=F32):
            return last.enter_context(nc.sbuf_tensor(name, shape, dt))

        vring = la("vring", [P, 2, GROUP, D])
        aring = la("aring", [P, 2, GROUP, T])
        gring = la("gring", [P, 2, NCHUNK, GROUP * CTOK])
        wb = la("wb", [P, 2, GROUP, T])
        last.close()

        block = whole.enter_context(nc.Block())

        def half(h):
            return slice(h * HT, (h + 1) * HT)

        def tile_cols(t):
            return slice(TILES[t][0], TILES[t][0] + TILES[t][1])

        CONSTS = [(ident, "ident"), (ones, "ones"), (eps, "eps"), (gains, "gains"), (par, "par"),
                  (iota, "iota"), (lam_in, "lam"), (dist, "dist"), (decay, "decay"),
                  (cross_scale, "cross_scale")]
        NCONST = 16 * (len(CONSTS) + 1)
        NORM_MIX, NORM_MEM, NORM_CROSS, NORM_FFN, NORM_FINAL = range(5)

        X_DONE = [1, 2, 4, 4, 6, 8]


        def results_stored(eng):
            eng.wait_ge(kd_stored, 16 * HEADS)
            eng.wait_ge(vd_stored, 32 * HEADS)
            eng.wait_ge(st_stored, 32 * HEADS)
            eng.wait_ge(mk_stored, 16 * HEADS)
            eng.wait_ge(mv_stored, 16 * HEADS)

        @block.sync
        def _(sp):
            for j in range(GROUP):
                sp.sem_inc(act_stored[j], 16)
            sp.dma_start(xT[:], d["x"]).then_inc(x_landed, 16)
            for tile, name in CONSTS:
                sp.dma_start(tile[:], d[name]).then_inc(const_landed, 16)
            sp.dma_start(dist_s[0:TS, :], d["dist_s"]).then_inc(const_landed, 16)

            def weights(slot, src):
                sp.dma_start(wring[:, slot], src).then_inc(w_landed[slot], 16)

            for b in range(NB_IN):
                weights(b, d["w_in"][0, b])
            sp.dma_start(memT[:], d["mem"]).then_inc(mem_landed, 16)

            def head_cache(h):
                sp.dma_start(ck[:], d["cache_k"][h]).then_inc(cache_landed, 16)
                sp.dma_start(cv[:], d["cache_v"][h]).then_inc(cache_landed, 16)
                sp.dma_start(st_in[:], d["state"][h]).then_inc(cache_landed, 16)

            head_cache(0)
            with sp.Fori(0, HEADS - 1) as i:
                for b in range(NB_IN):
                    sp.wait_ge(in_done, i * 14 + 2 * (b + 1))
                    weights(b, d["w_in"][i + 1, b])
                sp.wait_ge(ro_ready, i + 1)
                head_cache(i + 1)
            for b in range(4):
                sp.wait_ge(in_done, (HEADS - 1) * 14 + 2 * (b + 1))
                weights(b, d["w_out"][b])
            for b in range(4):
                sp.wait_ge(wo_done, 2 * (b + 1))
                weights(b, d["w_out"][4 + b])
            for b in range(NB_X):
                if b < 4:
                    sp.wait_ge(wo_done, 8 + 2 * (b + 1))
                else:
                    sp.wait_ge(in_done, (HEADS - 1) * 14 + 2 * (b + 1))
                weights(b, d["w_x"][0, b])
            def head_mem(h):
                sp.dma_start(cmk[:], d["cache_mem_k"][h]).then_inc(cm_landed, 16)
                sp.dma_start(cmv[:], d["cache_mem_v"][h]).then_inc(cm_landed, 16)

            head_mem(0)
            with sp.Fori(0, HEADS - 1) as i:
                for b in range(NB_X):
                    sp.wait_ge(x_done, i * 8 + X_DONE[b])
                    weights(b, d["w_x"][i + 1, b])
                sp.wait_ge(xpv_ready, (i + 1) * NT)
                head_mem(i + 1)
            for b in range(4):
                sp.wait_ge(x_done, (HEADS - 1) * 8 + X_DONE[b])
                weights(b, d["w_xo"][b])
            for b in range(4):
                sp.wait_ge(xo_done, 2 * (b + 1))
                weights(b, d["w_xo"][4 + b])

            sp.wait_ge(h_ready, C * (NORM_FFN + 1))
            results_stored(sp)

            def query_weights(slot, src):
                sp.dma_start(pring[:, slot], src).then_inc(w_landed[slot], 16)

            def load_keys(slot, src):
                sp.dma_start(pk[:, slot], src).then_inc(pk_landed[slot], 16)

            for b in range(4):
                query_weights(b, d["w_pq"][0, b])
            for j in range(2):
                load_keys(j, d["keys"][0, j])
            for j in range(GROUP):
                sp.dma_start(uring[:, j], d["u"][0, j]).then_inc(u_landed[j], 16)
            with sp.Fori(0, PH // 2 - 1) as i:
                for j in range(2):
                    for s in range(2):
                        sp.wait_ge(pq_done, i * 8 + (4 * j + 2 * s + 2))
                        query_weights(2 * j + s, d["w_pq"][i + 1, 2 * j + s])
                    sp.wait_ge(sc_ready, i * 2 + j + 1)
                    load_keys(j, d["keys"][i + 1, j])
            with sp.Fori(0, U1_GROUPS + U2_GROUPS - 1) as i:
                for j in range(GROUP):
                    sp.wait_ge(z_ready, (i * GROUP + j + 1) * 2)
                    sp.dma_start(uring[:, j], d["u"][i + 1, j]).then_inc(u_landed[j], 16)
                    sp.wait_ge(z_taken, 4 + (i * GROUP + j + 1) * 2)
                    sp.dma_start(d["act"][i, j], actb[:, j]).then_inc(act_stored[j], 16)
            for j in range(GROUP):
                n = KEYS - GROUP + j
                sp.wait_ge(z_taken, 4 + (n + 1) * 2)
                sp.dma_start(d["act"][KEYS // GROUP - 1, j], actb[:, j]).then_inc(act_stored[j], 16)

            for j in range(GROUP):
                sp.wait_ge(act_stored[j], 16 + 16 * (KEYS // GROUP))
            sp.wait_ge(g_stored[0], 16 * ((NCHUNK + 1) // 2))
            sp.wait_ge(g_stored[1], 16 * (NCHUNK // 2))

            def load_group(g, p):
                sp.dma_start(vring[:, p], d["v"][g].rearrange("j p n -> p j n")).then_inc(v_landed[p], 16)
                sp.dma_start(aring[:, p], d["act"][g].rearrange("j p t -> p j t")).then_inc(ag_landed[p], 16)
                sp.dma_start(gring[:, p], d["gates"][:, :, g].rearrange("c p k -> p c k")).then_inc(ag_landed[p], 16)

            load_group(0, 0)
            load_group(1, 1)
            with sp.Fori(0, KEYS // GROUP // 2 - 1) as i:
                for p in range(2):
                    sp.wait_ge(y_ready, 32 + (i * 2 + p + 1) * 16)
                    sp.sem_inc(passed, 1)
                    sp.wait_ge(w_ready, (i * 2 + p + 1) * GROUP)
                    sp.sem_inc(passed, 1)
                    load_group(i * 2 + (2 + p), p)

            sp.wait_ge(h_ready, C * (NORM_FINAL + 1))
            sp.dma_start(d["y"], hT[:]).then_inc(out_stored, 16)
            sp.wait_ge(out_stored, 16)
            results_stored(sp)

        @block.gpsimd
        def _(pool):
            for s in (kd_free, vd_free, st_free, mk_free, mv_free, g_free[0], g_free[1]):
                pool.sem_inc(s, 1)

            def ready(s, n):
                pool.wait_ge(s, n)
                pool.sem_inc(passed, 1)

            def stored(s, n, free):
                pool.wait_ge(s, n)
                pool.sem_inc(free, 1)

            with pool.Fori(0, HEADS) as i:
                ready(in_taken, 2 + i * 14 + 4)
                pool.dma_start(d["kd_out"][i], kdT[:]).then_inc(kd_stored, 16)
                ready(in_taken, 2 + i * 14 + 6)
                pool.dma_start(d["vd_out"][i], vd[:, 0:4]).then_inc(vd_stored, 16)
                pool.dma_start(d["vds_out"][i], vd[0:TS, 4]).then_inc(vd_stored, 16)
                stored(kd_stored, (i + 1) * 16, kd_free)
                stored(vd_stored, (i + 1) * 32, vd_free)
                ready(st_ready, i + 1)
                pool.dma_start(d["st_out"][i, 0], st[:, 3]).then_inc(st_stored, 16)
                pool.dma_start(d["st_out"][i, 1], st[:, 4]).then_inc(st_stored, 16)
                stored(st_stored, (i + 1) * 32, st_free)
            with pool.Fori(0, HEADS) as i:
                ready(x_taken, 2 + i * 8 + 2)
                pool.dma_start(d["mk_out"][i], mkT[:]).then_inc(mk_stored, 16)
                ready(x_taken, 2 + i * 8 + 4)
                pool.dma_start(d["mv_out"][i], mv[:]).then_inc(mv_stored, 16)
                stored(mk_stored, (i + 1) * 16, mk_free)
                stored(mv_stored, (i + 1) * 16, mv_free)

            def store_gates(c, p, n, turn):
                ready(g_taken, n)
                pool.dma_start(d["gates"][c].rearrange("p g k -> p (g k)"),
                               gst[:, p].rearrange("p k t -> p (k t)")).then_inc(g_stored[p], 16)
                stored(g_stored[p], turn * 16, g_free[p])

            with pool.Fori(0, NCHUNK // 2) as i:
                for p in range(2):
                    store_gates(i * 2 + p, p, 2 + (i * 2 + p + 1) * 8, i + 1)
            store_gates(NCHUNK - 1, 0, 2 + NCHUNK * 8, NCHUNK // 2 + 1)

        @block.tensor
        def _(pe):
            def norm_sums(k, n):
                for c in range(C):
                    pe.wait_ge(sq_ready, C * k + c + 1)
                    if c == 0 and k > 0:
                        pe.wait_ge(rms_ready, k)
                    if n == T:
                        pe.matmul(bank[6][:, 0:HT], ones[:], sq[:, c % 2, 0:HT], start=c == 0, stop=c == C - 1)
                        m = pe.matmul(bank[7][:, 0:HT], ones[:], sq[:, c % 2, HT:T], start=c == 0, stop=c == C - 1)
                    else:
                        m = pe.matmul(bank[6][:, 0:n], ones[:], sq[:, c % 2, 0:n], start=c == 0, stop=c == C - 1)
                    m.then_inc(sq_used, 1)

            pe.sem_inc(g_ready, 4)
            pe.sem_inc(y_ready, 32)
            pe.wait_ge(const_landed, NCONST)
            norm_sums(NORM_MIX, T)
            norm_sums(NORM_MEM, MEM)

            def project_T(i, k, slot):
                pe.wait_ge(w_landed[slot], (i + 1) * 16)
                for h in range(2):
                    pe.wait_ge(in_taken, i * 14 + (k + h + 1))
                    for c in range(C):
                        m = pe.matmul(bank[h][:, 0:HT], wring[:, slot, c], hT[:, c, half(h)],
                                      start=c == 0, stop=c == C - 1)
                    m.then_inc(in_done, 1)

            def project_rows(i, k, slot):
                pe.wait_ge(w_landed[slot], (i + 1) * 16)
                for u, tiles in enumerate((range(4), [4])):
                    pe.wait_ge(in_taken, i * 14 + (k + u + 1))
                    for t in tiles:
                        rows = TILES[t][1]
                        for c in range(C):
                            m = pe.matmul(bank[u][0:rows, (t % 4) * P:(t % 4 + 1) * P], hT[:, c, tile_cols(t)],
                                          wring[:, slot, c], start=c == 0, stop=c == C - 1)
                    m.then_inc(in_done, 1)

            def scores(i, t):
                q0, rows = TILES[t]
                pe.wait_ge(s_taken, i * NT + t + 1)
                if t == 4:
                    pe.wait_ge(cache_landed, (i + 1) * 48)
                    pe.sem_inc(passed, 1)
                for m_ in range(2):
                    ps = slice(DK * m_, DK * m_ + DK)
                    lhs = qdT[ps, q0:q0 + rows]
                    if t < 4:
                        m = pe.matmul(bank[2 + m_][0:rows, 0:q0 + rows], lhs, kdT[ps, 0:q0 + rows],
                                      start=True, stop=True)
                    else:
                        pe.matmul(bank[2 + m_][0:rows, 0:PAST], lhs, ck[ps, :], start=True, stop=True)
                        m = pe.matmul(bank[2 + m_][0:rows, PAST:PAST + TS], lhs, kdT[ps, q0:q0 + rows],
                                      start=True, stop=True)
                m.then_inc(s_ready, 1)

            def turn(i, t):
                rows = TILES[t][1]
                pe.wait_ge(a_ready, i * NT + t + 1)
                pe.wait_ge(at_taken, i * NT + t + 1)
                if t == 4:
                    pe.sem_inc(passed, 1)
                if t < 4:
                    for k in range(t + 1):
                        m = pe.transpose(bank[4][:, k * P:(k + 1) * P], S[:, t % 2, 0, k * P:(k + 1) * P], ident[:])
                else:
                    pe.transpose(bank[4][:, 0:rows], S[0:rows, 0, 0, 0:PAST], ident[0:rows, 0:rows])
                    m = pe.transpose(bank[4][0:TS, P:P + rows], S[0:rows, 0, 0, PAST:PAST + TS],
                                     ident[0:rows, 0:rows])
                m.then_inc(at_ready, 1)

            def values(i, t):
                rows = TILES[t][1]
                pe.wait_ge(at_taken, i * NT + t + 2)
                pe.wait_ge(pv_taken, i * NT + t + 1)
                o = bank[5 + t % 2][:, 0:rows]
                if t < 4:
                    for k in range(t + 1):
                        m = pe.matmul(o, vd[:, k], aT[:, k * P:(k + 1) * P], start=k == 0, stop=k == t)
                else:
                    pe.matmul(o, cv[:], aT[:, 0:rows], start=True, stop=False)
                    m = pe.matmul(o, vd[0:TS, 4], aT[0:TS, P:P + rows], start=False, stop=True)
                m.then_inc(pv_ready, 1)

            def sums(src, ready_sem, value, done):
                pe.wait_ge(ready_sem, value)
                pe.matmul(bank[6][:, 0:HT], ones[:], src[:, 0:HT], start=True, stop=True)
                pe.matmul(bank[7][:, 0:HT], ones[:], src[:, HT:T], start=True, stop=True).then_inc(done, 1)

            pe.wait_ge(h_ready, C)
            with pe.Fori(0, HEADS) as i:
                project_T(i, 0, QD)
                project_T(i, 2, KD)
                project_rows(i, 4, VD)
                pe.wait_ge(in_taken, i * 14 + 6 + 2)
                pe.wait_ge(ro_copied, i + 1)
                scores(i, 0)
                project_T(i, 6, QR)
                scores(i, 1)
                turn(i, 0)
                project_T(i, 8, KR)
                scores(i, 2)
                values(i, 0)
                turn(i, 1)
                project_rows(i, 10, VR)
                scores(i, 3)
                values(i, 1)
                turn(i, 2)
                project_T(i, 12, GR)
                scores(i, 4)
                values(i, 2)
                turn(i, 3)
                values(i, 3)
                turn(i, 4)
                for t in range(NT):
                    rows = TILES[t][1]
                    out = bank[0][:, t * P:(t + 1) * P] if t < 4 else bank[1][0:rows, 0:P]
                    if t == 0:
                        pe.wait_ge(in_taken, i * 14 + 14 + 2)
                    m = pe.transpose(out, krT[:, tile_cols(t)], ident[:])
                m.then_inc(kt_ready, 1)
                pe.wait_ge(s_taken, i * NT + 5 + 1)
                for t in range(NT):
                    rows = TILES[t][1]
                    out = bank[2][:, t * P:(t + 1) * P] if t < 4 else bank[3][0:rows, 0:rows]
                    m = pe.matmul(out, krT[:, tile_cols(t)], qrT[:, tile_cols(t)], start=True, stop=True)
                m.then_inc(inner_ready, 1)
                values(i, 4)
                pe.wait_ge(kn_ready, i + 1)
                for t in range(NT):
                    rows = TILES[t][1]
                    out = bank[0][:, t * P:(t + 1) * P] if t < 4 else bank[1][:, 0:P]
                    m = pe.matmul(out, kn[0:rows, t], vr[0:rows, t], start=True, stop=True)
                m.then_inc(u_ready, 1)
                sums(sqo, dsq_ready, i * 2 + 1, dss_ready)
                pe.wait_ge(im_ready, i + 1)
                pe.wait_ge(st_ready, i + 1)
                for t in range(NT):
                    q0, rows = TILES[t]
                    out = bank[2][:, q0:q0 + rows] if t < 4 else bank[3][:, 0:rows]
                    m = pe.matmul(out, vr[0:rows, t], im[0:rows, q0:q0 + rows], start=True, stop=t == 0)
                    if t:
                        before = st[:, t - 1] if t < 4 else st_in[:]
                        m = pe.matmul(out, before, qs[:, q0:q0 + rows], start=False, stop=True)
                m.then_inc(ro_ready, 1)
                pe.wait_ge(drms_ready, i * 2 + 1)
                sums(ro, ro_copied, i + 2, mean_ready)
                pe.wait_ge(oc_ready, i + 1)
                pe.wait_ge(dsq_ready, i * 2 + 2)
                pe.matmul(bank[6][:, 0:HT], ones[:], sqo[:, 0:HT], start=True, stop=True)
                pe.matmul(bank[7][:, 0:HT], ones[:], sqo[:, HT:T], start=True, stop=True).then_inc(dss_ready, 1)

            def output_projection(first, taken, done):
                with pe.Fori(0, 2) as i:
                    for b in range(4):
                        pe.wait_ge(w_landed[b], i * 16 + first[b])
                        for h in range(2):
                            pe.wait_ge(taken, i * 8 + (2 * b + h + 1))
                            for c in range(C):
                                m = pe.matmul(bank[h][:, 0:HT], wring[:, b, c], mixedT[:, c, half(h)],
                                              start=c == 0, stop=c == C - 1)
                            m.then_inc(done, 1)

            pe.wait_ge(mixed_ready, 2 + 2 * HEADS)
            output_projection([16 * (HEADS + 1)] * 4, wo_taken, wo_done)
            norm_sums(NORM_CROSS, T)

            pe.wait_ge(h_ready, C * (NORM_CROSS + 1))
            xw = [16 * (HEADS + 3)] * 4 + [16 * (HEADS + 1)] * 2
            with pe.Fori(0, HEADS) as i:
                def xland(b):
                    pe.wait_ge(w_landed[b], i * 16 + xw[b])

                def xunit(k):
                    pe.wait_ge(x_taken, i * 8 + (k + 1))
                    return bank[k % 2]

                for b in range(2):
                    xland(b)
                    o = xunit(b)
                    for c in range(C):
                        m = pe.matmul(o[:, 0:MEM], wring[:, b, c], memn[:, c], start=c == 0, stop=c == C - 1)
                    m.then_inc(x_done, 1)
                xland(2)
                xland(3)
                for mt in range(2):
                    o = xunit(2 + mt)
                    for b in range(2):
                        for c in range(C):
                            m = pe.matmul(o[:, b * P:(b + 1) * P], memn[:, c, mt * P:(mt + 1) * P],
                                          wring[:, 2 + b, c], start=c == 0, stop=c == C - 1)
                    m.then_inc(x_done, 1)
                for b in range(2):
                    xland(4 + b)
                    for h in range(2):
                        o = xunit(4 + 2 * b + h)
                        for c in range(C):
                            m = pe.matmul(o[:, 0:HT], wring[:, 4 + b, c], hT[:, c, half(h)],
                                          start=c == 0, stop=c == C - 1)
                        m.then_inc(x_done, 1)
                pe.wait_ge(x_taken, i * 8 + 8 + 2)

                def xscores(t):
                    rows = TILES[t][1]
                    if t >= 2:
                        pe.wait_ge(xe_ready, i * NT + (t - 1))
                    if t == 4:
                        pe.wait_ge(cm_landed, (i + 1) * 32)
                    src = mkT if t < 4 else cmk
                    for c in range(2):
                        m = pe.matmul(bank[2 + t % 2][0:rows, 0:MEM], xqT[:, c, tile_cols(t)], src[:, c],
                                      start=c == 0, stop=c == 1)
                    m.then_inc(xs_ready, 1)

                def xturn(t):
                    rows = TILES[t][1]
                    pe.wait_ge(xp_ready, i * NT + t + 1)
                    pe.wait_ge(xt_taken, i * NT + t + 1)
                    if t == 4:
                        pe.sem_inc(passed, 1)
                    for k in range(2):
                        m = pe.transpose(bank[4][:, k * P:k * P + rows], E[0:rows, t % 2, k * P:(k + 1) * P],
                                         ident[0:rows, 0:rows])
                    m.then_inc(xt_ready, 1)

                def xvalues(t):
                    rows = TILES[t][1]
                    pe.wait_ge(xt_taken, i * NT + t + 2)
                    pe.wait_ge(xpv_taken, i * NT + t + 1)
                    src = mv if t < 4 else cmv
                    for b in range(2):
                        o = bank[5 + t % 2][:, b * P:b * P + rows]
                        for k in range(2):
                            m = pe.matmul(o, src[:, k, b * P:(b + 1) * P], eT[:, k * P:k * P + rows],
                                          start=k == 0, stop=k == 1)
                    m.then_inc(xpv_ready, 1)

                xscores(0)
                xscores(1)
                for t in range(NT):
                    xturn(t)
                    xvalues(t)
                    if t + 2 < NT:
                        xscores(t + 2)

            pe.wait_ge(xpv_taken, 2 + HEADS * NT)
            wl = [16 * (2 * HEADS + 3)] * 4
            output_projection(wl, xo_taken, xo_done)
            norm_sums(NORM_FFN, T)

            pe.wait_ge(h_ready, C * (NORM_FFN + 1))
            pq0 = 16 * (2 * HEADS + 5)
            with pe.Fori(0, PH // 2) as i:
                for j in range(2):
                    for s in range(2):
                        pe.wait_ge(w_landed[2 * j + s], i * 16 + pq0)
                        for h in range(2):
                            pe.wait_ge(pq_taken, i * 8 + (4 * j + 2 * s + h + 1))
                            for c in range(C):
                                m = pe.matmul(bank[h][:, 0:HT], pring[:, 2 * j + s, c], hT[:, c, half(h)],
                                              start=c == 0, stop=c == C - 1)
                            m.then_inc(pq_done, 1)
                    pe.wait_ge(pk_landed[j], (i + 1) * 16)
                    pe.wait_ge(pq_taken, i * 8 + (4 * j + 4 + 2))
                    pe.wait_ge(sc_taken, i * 2 + (j + 1))
                    for s in range(2):
                        for t in range(NT):
                            rows = TILES[t][1]
                            o = bank[2 + s][:, t * P:(t + 1) * P] if t < 4 else bank[4][0:rows, s * P:(s + 1) * P]
                            m = pe.matmul(o, qpT[:, s, tile_cols(t)], pk[:, j, s], start=True, stop=True)
                    m.then_inc(sc_ready, 1)

            def first_products(i, g, j):
                pe.wait_ge(u_landed[j], (g + 1) * 16)
                for h in range(2):
                    pe.wait_ge(z_taken, (g * GROUP + j) * 2 + (h + 1))
                    for c in range(C):
                        m = pe.matmul(bank[(2 * j + h) % 4][:, 0:HT], uring[:, j, c], hT[:, c, half(h)],
                                      start=c == 0, stop=c == C - 1)
                    m.then_inc(z_ready, 1)

            pe.wait_ge(sc_taken, 1 + PH)
            pe.wait_ge(pq_taken, 2 + 4 * PH)
            with pe.Fori(0, U1_GROUPS) as i:
                for j in range(GROUP):
                    first_products(i, i, j)

            pe.wait_ge(sel_ready, NT)
            for t in range(NT):
                for k in range(3):
                    n = t * 3 + k
                    m = pe.transpose(bank[4 + n // 4][:, (n % 4) * P:(n % 4 + 1) * P], sel[:, t, k], ident[:])
            m.then_inc(selT_ready, 1)
            pe.wait_ge(selT_taken, 1)

            def gate_products(c, j):
                pe.wait_ge(hot_ready, (c * GROUP) + j + 1)
                for b in range(2):
                    pe.wait_ge(g_taken, (c * GROUP + j) * 2 + (b + 1))
                    for k in range(4):
                        m = pe.matmul(bank[4 + b][:, k * P:(k + 1) * P], hot2[:, j % 2, 4 * b + k],
                                      hot1[:, j % 2, 4 * b + k], start=True, stop=True)
                    m.then_inc(g_ready, 1)

            with pe.Fori(0, U2_GROUPS) as i:
                for j in range(GROUP):
                    first_products(i, i + U1_GROUPS, j)
                    gate_products(i, j)

            pe.wait_ge(z_taken, 4 + 2 * KEYS)
            pe.wait_ge(g_taken, 2 + 2 * GROUP * NCHUNK)
            with pe.Fori(0, KEYS // GROUP // 2) as i:
                for p in range(2):
                    pe.wait_ge(v_landed[p], (i + 1) * 16)
                    pe.wait_ge(w_ready, (i * 2 + p + 1) * GROUP)
                    for n in range(2 * C):
                        b, h = n // 2, n % 2
                        pe.wait_ge(y_taken, (i * 2 + p) * (2 * C) + (n + 1))
                        for j in range(GROUP):
                            m = pe.matmul(bank[n % 8][:, 0:HT], vring[:, p, j, b * P:(b + 1) * P],
                                          wb[:, p, j, half(h)], start=j == 0, stop=j == GROUP - 1)
                        m.then_inc(y_ready, 1)
            pe.wait_ge(y_taken, 8 + 2 * C * KEYS // GROUP)
            norm_sums(NORM_FINAL, T)

        @block.scalar
        def _(act):
            def norm_squares(k, src, n):
                for c in range(C):
                    if C * k + c >= 2:
                        act.wait_ge(sq_used, C * k + c - 1)
                    act.activation(sq[:, c % 2, 0:n], src[:, c], ACT.Square).then_inc(sq_ready, 1)
                act.wait_ge(sq_used, C * (k + 1))
                if k:
                    act.wait_ge(h_ready, C * k)
                if n == T:
                    act.activation(rms[:, 0:HT], bank[6][:, 0:HT], ACT.Sqrt, scale=1.0 / D, bias=eps[:, 0:1])
                    act.activation(rms[:, HT:T], bank[7][:, 0:HT], ACT.Sqrt, scale=1.0 / D,
                                   bias=eps[:, 0:1]).then_inc(rms_ready, 1)
                else:
                    act.activation(rms[:, 0:n], bank[6][:, 0:n], ACT.Sqrt, scale=1.0 / D,
                                   bias=eps[:, 0:1]).then_inc(rms_ready, 1)

            for s, n in ((in_taken, 2), (at_taken, 1), (ro_copied, 1), (x_taken, 2), (xt_taken, 1),
                         (pq_taken, 2), (sc_taken, 1), (z_taken, 4), (g_taken, 2)):
                act.sem_inc(s, n)
            act.wait_ge(x_landed, 16)
            act.wait_ge(const_landed, NCONST)
            norm_squares(NORM_MIX, xT, T)
            act.wait_ge(lam_ready, 1)
            act.activation(lam[:, 2:4], lam[:, 0:2], ACT.Exp).then_inc(lam_ready, 1)
            act.wait_ge(mem_landed, 16)
            norm_squares(NORM_MEM, memT, MEM)

            with act.Fori(0, HEADS) as i:
                def unit(k, dst, src, fn=ACT.Copy, scale=1.0):
                    act.wait_ge(in_done, i * 14 + (k + 1))
                    act.activation(dst, src, fn, scale=scale).then_inc(in_taken, 1)

                def unit_T(k, dst, fn=ACT.Copy, scale=1.0):
                    for h in range(2):
                        unit(k + h, dst[:, half(h)], bank[h][:, 0:HT], fn, scale)

                def unit_rows(k, dst):
                    unit(k, dst[:, 0:4].rearrange("p t n -> p (t n)"), bank[0][:])
                    unit(k + 1, dst[0:TS, 4], bank[1][0:TS, 0:P])

                def exps(t):
                    rows = TILES[t][1]
                    keys = (t + 1) * P if t < 4 else PAST + TS
                    act.wait_ge(max_ready, i * NT + (t + 1))
                    for m in range(2):
                        s = S[0:rows, t % 2, m, 0:keys]
                        a = act.activation(s, s, ACT.Exp, scale=DK ** -0.5, bias=nmx[0:rows, t % 2, m:m + 1],
                                           accum_out=rs[0:rows, t % 2, m:m + 1])
                    a.then_inc(e_ready, 1)

                def turned(t):
                    rows = TILES[t][1]
                    act.wait_ge(at_ready, i * NT + (t + 1))
                    if t < 4:
                        a = act.activation(aT[:, 0:(t + 1) * P], bank[4][:, 0:(t + 1) * P], ACT.Copy)
                    else:
                        act.activation(aT[:, 0:rows], bank[4][:, 0:rows], ACT.Copy)
                        a = act.activation(aT[0:TS, P:P + rows], bank[4][0:TS, P:P + rows], ACT.Copy)
                    a.then_inc(at_taken, 1)

                unit_T(0, qdT)
                act.wait_ge(kd_free, i + 1)
                unit_T(2, kdT)
                act.wait_ge(vd_free, i + 1)
                unit_rows(4, vd)
                exps(0)
                unit_T(6, qrT)
                exps(1)
                turned(0)
                unit_T(8, krT, scale=P ** -0.5)
                exps(2)
                turned(1)
                unit_rows(10, vr)
                exps(3)
                turned(2)
                act.wait_ge(mixed_ready, i * 2 + 2)
                unit_T(12, grT, fn=ACT.Silu)
                exps(4)
                turned(3)
                turned(4)
                act.wait_ge(kt_ready, i + 1)
                act.wait_ge(par_ready, i + 1)
                act.activation(kn[:, 0:4].rearrange("p t n -> p (t n)"), bank[0][:], ACT.Copy,
                               scale=hp[:, TAIL:TAIL + 1])
                act.activation(kn[0:TS, 4], bank[1][0:TS, 0:P], ACT.Copy,
                               scale=hp[0:TS, TAIL_S:TAIL_S + 1]).then_inc(kn_ready, 1)
                act.wait_ge(pv_taken, (i + 1) * NT + 2)
                act.activation(sqo[:], od[:], ACT.Square).then_inc(dsq_ready, 1)
                act.wait_ge(dss_ready, i * 2 + 1)
                sc2 = (1.0 - LAM_INIT) ** 2
                act.activation(rmo[:, 0:HT], bank[6][:, 0:HT], ACT.Sqrt, scale=1.0 / (P * sc2), bias=eps[:, 1:2])
                act.activation(rmo[:, HT:T], bank[7][:, 0:HT], ACT.Sqrt, scale=1.0 / (P * sc2),
                               bias=eps[:, 1:2]).then_inc(drms_ready, 1)
                act.wait_ge(ro_ready, i + 1)
                act.activation(ro[:, 0:TP], bank[2][:], ACT.Copy)
                act.activation(ro[:, TP:T], bank[3][:, 0:TS], ACT.Copy).then_inc(ro_copied, 1)
                act.wait_ge(oc_ready, i + 1)
                act.activation(sqo[:], ro[:], ACT.Square).then_inc(dsq_ready, 1)
                act.wait_ge(dss_ready, i * 2 + 2)
                act.wait_ge(mixed_ready, i * 2 + 3)
                act.activation(rmo[:, 0:HT], bank[6][:, 0:HT], ACT.Sqrt, scale=1.0 / P, bias=eps[:, 0:1])
                act.activation(rmo[:, HT:T], bank[7][:, 0:HT], ACT.Sqrt, scale=1.0 / P,
                               bias=eps[:, 0:1]).then_inc(drms_ready, 1)

            act.wait_ge(wo_taken, 2 + 16)
            norm_squares(NORM_CROSS, xT, T)

            with act.Fori(0, HEADS) as i:
                def xunit(k, dst, width):
                    act.wait_ge(x_done, i * 8 + (k + 1))
                    act.activation(dst, bank[k % 2][:, 0:width], ACT.Copy).then_inc(x_taken, 1)

                act.wait_ge(mk_free, i + 1)
                for b in range(2):
                    xunit(b, mkT[:, b], MEM)
                act.wait_ge(mv_free, i + 1)
                for mt in range(2):
                    xunit(2 + mt, mv[:, mt], MEM)
                for b in range(2):
                    for h in range(2):
                        xunit(4 + 2 * b + h, xqT[:, b, half(h)], HT)

                def xexp(t):
                    rows = TILES[t][1]
                    act.wait_ge(xmax_ready, i * NT + (t + 1))
                    act.activation(E[0:rows, t % 2], bank[2 + t % 2][0:rows, 0:MEM], ACT.Exp,
                                   scale=(D // HEADS) ** -0.5, bias=xn[0:rows, t % 2:t % 2 + 1],
                                   accum_out=xr[0:rows, t % 2:t % 2 + 1]).then_inc(xe_ready, 1)

                def xturned(t):
                    rows = TILES[t][1]
                    act.wait_ge(xt_ready, i * NT + (t + 1))
                    act.activation(eT[:].rearrange("p (k n) -> p k n", k=2)[:, :, 0:rows],
                                   bank[4][:, 0:2 * P].rearrange("p (k n) -> p k n", k=2)[:, :, 0:rows],
                                   ACT.Copy).then_inc(xt_taken, 1)

                xexp(0)
                for t in range(NT):
                    if t + 1 < NT:
                        xexp(t + 1)
                    xturned(t)

            act.wait_ge(xo_taken, 2 + 16)
            norm_squares(NORM_FFN, xT, T)

            with act.Fori(0, PH // 2) as i:
                for j in range(2):
                    for s in range(2):
                        for h in range(2):
                            act.wait_ge(pq_done, i * 8 + (4 * j + 2 * s + h + 1))
                            act.activation(qpT[:, s, half(h)], bank[h][:, 0:HT], ACT.Copy).then_inc(pq_taken, 1)
                    act.wait_ge(sc_ready, i * 2 + (j + 1))
                    act.wait_ge(sc_used, i * 2 + (j + 1))
                    for s in range(2):
                        act.activation(sc[:, j, s, 0:4].rearrange("p t n -> p (t n)"), bank[2 + s][:], ACT.Copy)
                    act.activation(sc[0:TS, j, :, 4], bank[4][0:TS, 0:2 * P].rearrange("p (s n) -> p s n", s=2),
                                   ACT.Copy).then_inc(sc_taken, 1)

            def activations(g, j):
                for h in range(2):
                    act.wait_ge(z_ready, (g * GROUP + j) * 2 + (h + 1))
                    if h == 0:
                        act.wait_ge(act_stored[j], (g + 1) * 16)
                    act.activation(actb[:, j, half(h)], bank[(2 * j + h) % 4][:, 0:HT],
                                   ACT.Gelu).then_inc(z_taken, 1)

            with act.Fori(0, U1_GROUPS) as i:
                for j in range(GROUP):
                    activations(i, j)

            act.wait_ge(dif_ready, 1)
            act.activation(best[:].rearrange("p t h k -> p (t h k)"), best[:].rearrange("p t h k -> p (t h k)"),
                           ACT.Exp).then_inc(gexp_ready, 1)
            act.wait_ge(selT_ready, 1)
            for t in range(NT):
                for k in range(3):
                    n = t * 3 + k
                    a = act.activation(selT[:, k, t * P:(t + 1) * P],
                                       bank[4 + n // 4][:, (n % 4) * P:(n % 4 + 1) * P], ACT.Copy)
            a.then_inc(selT_taken, 1)

            def gate_chunk(c, p, turn):
                for j in range(GROUP):
                    activations(c + U1_GROUPS, j)
                    for b in range(2):
                        act.wait_ge(g_ready, 4 + (c * GROUP + j) * 2 + (b + 1))
                        if j == 0 and b == 0:
                            act.wait_ge(g_free[p], turn)
                        t0 = j * TOK8 + 4 * b
                        act.activation(gst[:, p, :, t0:t0 + 4].rearrange("p k t -> p t k"),
                                       bank[4 + b][:].rearrange("p (t k) -> p t k", t=4),
                                       ACT.Copy).then_inc(g_taken, 1)

            with act.Fori(0, NCHUNK // 2) as i:
                for p in range(2):
                    gate_chunk(i * 2 + p, p, i + 1)
            gate_chunk(NCHUNK - 1, 0, NCHUNK // 2 + 1)

            act.wait_ge(y_taken, 8 + 2 * C * KEYS // GROUP)
            norm_squares(NORM_FINAL, xT, T)

        @block.vector
        def _(dve):
            step = Steps(dve, vec)

            def normed(k, src, dst, n):
                dve.wait_ge(rms_ready, k + 1)
                step.link(dve.reciprocal(rms[:, 0:n], rms[:, 0:n]))
                for c in range(C):
                    dve.scalar_tensor_tensor(out=dst[:, c], in0=src[:, c], scalar=gains[:, k, c:c + 1],
                                             in1=rms[:, 0:n], op0=ALU.mult, op1=ALU.mult).then_inc(h_ready, 1)

            for s, n in ((s_taken, 1), (pv_taken, 2), (mixed_ready, 2), (wo_taken, 2), (xo_taken, 2),
                         (xpv_taken, 2), (sc_used, 2), (y_taken, 8)):
                dve.sem_inc(s, n)
            dve.wait_ge(const_landed, NCONST)
            for m in range(2):
                a = dve.tensor_tensor_reduce(out=lam_in[:, 2 * m], in0=lam_in[:, 2 * m], in1=lam_in[:, 2 * m + 1],
                                             scale=1.0, scalar=0.0, op0=ALU.mult, op1=ALU.add,
                                             accum_out=lam[:, m:m + 1])
            a.then_inc(lam_ready, 1)
            dve.wait_ge(lam_ready, 2)
            step.link(dve.tensor_tensor(lam[:, 0:1], lam[:, 3:4], lam[:, 2:3], ALU.subtract))
            step.link(dve.tensor_scalar(lam[:, 0:1], lam[:, 0:1], -LAM_INIT, None, ALU.add))
            dve.wait_ge(x_landed, 16)
            normed(NORM_MIX, xT, hT, T)
            dve.wait_ge(mem_landed, 16)
            normed(NORM_MEM, memT, memn, MEM)

            with dve.Fori(0, HEADS) as i:
                step.restart()
                step.link(dve.tensor_copy(hp[:], par[:, i]))
                dve.sem_inc(par_ready, 1)

                def biased(t):
                    rows = TILES[t][1]
                    keys = (t + 1) * P if t < 4 else PAST + TS
                    far = dist[:, TP - keys:TP] if t < 4 else dist_s[0:rows, :]
                    dve.wait_ge(s_ready, i * NT + (t + 1))
                    for m in range(2):
                        a = dve.scalar_tensor_tensor(out=S[0:rows, t % 2, m, 0:keys], in0=far,
                                                     scalar=hp[0:rows, SLOPE8:SLOPE8 + 1],
                                                     in1=bank[2 + m][0:rows, 0:keys], op0=ALU.mult, op1=ALU.add)
                    a.then_inc(s_taken, 1)
                    dve.wait_ge(s_taken, i * NT + (t + 2))
                    step.link(dve.tensor_reduce(mx[0:rows, t % 2], S[0:rows, t % 2, :, 0:keys], AX_X, ALU.max))
                    dve.tensor_scalar(nmx[0:rows, t % 2], mx[0:rows, t % 2], -DK ** -0.5, None,
                                      ALU.mult).then_inc(max_ready, 1)

                def combined(t):
                    rows = TILES[t][1]
                    keys = (t + 1) * P if t < 4 else PAST + TS
                    dve.wait_ge(e_ready, i * NT + (t + 1))
                    r = ri[0:rows, t % 2]
                    step.link(dve.reciprocal(r, rs[0:rows, t % 2]))
                    step.link(dve.tensor_scalar(r[:, 1:2], r[:, 1:2], lam[0:rows, 0:1], None, ALU.mult))
                    s0, s1 = S[0:rows, t % 2, 0, 0:keys], S[0:rows, t % 2, 1, 0:keys]
                    step.link(dve.tensor_scalar(s0, s0, r[:, 0:1], None, ALU.mult))
                    dve.scalar_tensor_tensor(out=s0, in0=s1, scalar=r[:, 1:2], in1=s0, op0=ALU.mult,
                                             op1=ALU.add).then_inc(a_ready, 1)

                def output(t):
                    rows = TILES[t][1]
                    dve.wait_ge(pv_ready, i * NT + (t + 1))
                    dve.tensor_copy(od[:, tile_cols(t)],
                                    bank[5 + t % 2][:, 0:rows]).then_inc(pv_taken, 1)

                biased(0)
                biased(1)
                combined(0)
                biased(2)
                combined(1)
                output(0)
                biased(3)
                combined(2)
                output(1)
                biased(4)
                combined(3)
                output(2)
                combined(4)
                output(3)
                dve.wait_ge(in_taken, i * 14 + 8 + 2)
                dve.tensor_tensor(qs[:, 0:TP].rearrange("p (c n) -> p c n", c=4),
                                  qrT[:, 0:TP].rearrange("p (c n) -> p c n", c=4),
                                  cross_scale[:, i][:, None, :].to_broadcast([P, 4, P]), ALU.mult)
                dve.tensor_tensor(qs[:, TP:T], qrT[:, TP:T], cross_scale[:, i, 0:TS], ALU.mult)
                dve.wait_ge(inner_ready, i + 1)
                dve.tensor_tensor(im[:, 0:TP].rearrange("p (c n) -> p c n", c=4),
                                  bank[2][:].rearrange("p (c n) -> p c n", c=4),
                                  decay[:, i][:, None, :].to_broadcast([P, 4, P]), ALU.mult)
                dve.tensor_tensor(im[0:TS, TP:T], bank[3][0:TS, 0:TS], decay[0:TS, i, 0:TS],
                                  ALU.mult).then_inc(im_ready, 1)
                output(4)
                dve.wait_ge(u_ready, i + 1)
                dve.wait_ge(cache_landed, (i + 1) * 48)
                dve.wait_ge(st_free, i + 1)
                step.link(dve.tensor_copy(st[:, 0], bank[0][:, 0:P]))
                for t in range(1, 4):
                    step.link(dve.scalar_tensor_tensor(out=st[:, t], in0=st[:, t - 1],
                                                       scalar=hp[:, GAMMA_L:GAMMA_L + 1],
                                                       in1=bank[0][:, t * P:(t + 1) * P], op0=ALU.mult, op1=ALU.add))
                dve.scalar_tensor_tensor(out=st[:, 4], in0=st_in[:], scalar=hp[:, GAMMA_LS:GAMMA_LS + 1],
                                         in1=bank[1][:, 0:P], op0=ALU.mult, op1=ALU.add).then_inc(st_ready, 1)
                dve.wait_ge(drms_ready, i * 2 + 1)
                step.link(dve.reciprocal(rmo[:], rmo[:]))
                dve.scalar_tensor_tensor(out=mixedT[:, i], in0=od[:], scalar=hp[:, G_DA:G_DA + 1], in1=rmo[:],
                                         op0=ALU.mult, op1=ALU.mult).then_inc(mixed_ready, 1)
                dve.wait_ge(mean_ready, i + 1)
                for h in range(2):
                    a = dve.scalar_tensor_tensor(out=ro[:, half(h)], in0=bank[6 + h][:, 0:HT], scalar=-1.0 / P,
                                                 in1=ro[:, half(h)], op0=ALU.mult, op1=ALU.add)
                a.then_inc(oc_ready, 1)
                dve.wait_ge(drms_ready, i * 2 + 2)
                step.link(dve.reciprocal(rmo[:], rmo[:]))
                step.link(dve.scalar_tensor_tensor(out=ro[:], in0=ro[:], scalar=hp[:, G_RET:G_RET + 1], in1=rmo[:],
                                                   op0=ALU.mult, op1=ALU.mult))
                dve.tensor_tensor(mixedT[:, HEADS + i], ro[:], grT[:], ALU.mult).then_inc(mixed_ready, 1)

            def residual(done, taken):
                with dve.Fori(0, 2) as i:
                    for b in range(4):
                        for h in range(2):
                            dve.wait_ge(done, i * 8 + (2 * b + h + 1))
                            x = xT[:, i * 4 + b, half(h)]
                            dve.tensor_tensor(x, bank[h][:, 0:HT], x, ALU.add).then_inc(taken, 1)

            residual(wo_done, wo_taken)
            normed(NORM_CROSS, xT, hT, T)

            with dve.Fori(0, HEADS) as i:
                step.restart()

                def xmax(t):
                    rows = TILES[t][1]
                    dve.wait_ge(xs_ready, i * NT + (t + 1))
                    step.link(dve.tensor_reduce(xm[0:rows, t % 2:t % 2 + 1], bank[2 + t % 2][0:rows, 0:MEM],
                                                AX_X, ALU.max))
                    dve.tensor_scalar(xn[0:rows, t % 2:t % 2 + 1], xm[0:rows, t % 2:t % 2 + 1],
                                      -(D // HEADS) ** -0.5, None, ALU.mult).then_inc(xmax_ready, 1)

                def xnorm(t):
                    rows = TILES[t][1]
                    dve.wait_ge(xe_ready, i * NT + (t + 1))
                    r = xr[0:rows, t % 2:t % 2 + 1]
                    step.link(dve.reciprocal(r, r))
                    dve.tensor_scalar(E[0:rows, t % 2], E[0:rows, t % 2], r, None, ALU.mult).then_inc(xp_ready, 1)

                def xoutput(t):
                    rows = TILES[t][1]
                    dve.wait_ge(xpv_ready, i * NT + (t + 1))
                    dve.tensor_scalar(mixedT[:, bass.ds(i * 2, 2), tile_cols(t)],
                                      bank[5 + t % 2][:, 0:2 * P].rearrange("p (b n) -> p b n", b=2)[:, :, 0:rows],
                                      1.0, None, ALU.mult).then_inc(xpv_taken, 1)

                xmax(0)
                xmax(1)
                for t in range(NT):
                    xnorm(t)
                    xoutput(t)
                    if t + 2 < NT:
                        xmax(t + 2)

            residual(xo_done, xo_taken)
            normed(NORM_FFN, xT, hT, T)

            results_stored(dve)
            for x in (v16, i16, c16, p16):
                a = step.link(dve.memset(x[:], 0))

            def top16(vals, idx, src, spare):
                step.link(dve.max(vals[:, 0:8], src))
                step.link(dve.max_index(idx[:, 0:8], vals[:, 0:8], src))
                step.link(dve.match_replace(spare, vals[:, 0:8], src, FLOOR))
                step.link(dve.max(vals[:, 8:16], spare))
                step.link(dve.max_index(idx[:, 8:16], vals[:, 8:16], spare))

            with dve.Fori(0, PH // 2) as i:
                step.restart()
                for j in range(2):
                    dve.wait_ge(sc_taken, i * 2 + (j + 2))
                    dve.sem_inc(passed, 1)
                    for s in range(2):
                        for t in range(NT):
                            rows = TILES[t][1]
                            top16(v16[0:rows, s, t], i16[0:rows, s, t], sc[0:rows, j, s, t], scr[0:rows, 0:KEYS])
                    dve.sem_inc(sc_used, 1)
                    for t in range(NT):
                        rows = TILES[t][1]
                        step.link(dve.tensor_tensor(cand[0:rows],
                                                    v16[0:rows, 0, t][:, :, None].to_broadcast([rows, TOPK, TOPK]),
                                                    v16[0:rows, 1, t][:, None, :].to_broadcast([rows, TOPK, TOPK]),
                                                    ALU.add))
                        top16(c16[0:rows, t], p16[0:rows, t], cand[0:rows].rearrange("p a b -> p (a b)"),
                              scr[0:rows, :])
                    p = i * 2 + j
                    dve.tensor_copy(best[:, :, p], c16[:])
                    dve.tensor_copy(pos[:, :, p], p16[:])
                    dve.tensor_copy(key1[:, :, p], i16[:, 0])
                    step.link(dve.tensor_copy(key2[:, :, p], i16[:, 1]))

            with dve.Fori(0, NT) as i:
                step.restart()
                at = pos[:, i].rearrange("p h k -> p (h k)")
                dve.tensor_scalar(rank[:, 0], at, 4, None, ALU.logical_shift_right)
                step.link(dve.tensor_scalar(rank[:, 1], at, TOPK - 1, None, ALU.bitwise_and))
                step.link(dve.tensor_copy(rankf[:], rank[:]))
                for s, key in ((0, key1), (1, key2)):
                    step.link(dve.tensor_tensor(hit[:], rankf[:, s][:, :, None].to_broadcast([P, PH * TOPK, TOPK]),
                                                iota[:, 0:TOPK][:, None, :].to_broadcast([P, PH * TOPK, TOPK]),
                                                ALU.is_equal))
                    h4 = hit[:].rearrange("p (h k) a -> p h k a", h=PH)
                    step.link(dve.tensor_tensor(h4, h4, key[:, i][:, :, None, :].to_broadcast([P, PH, TOPK, TOPK]),
                                                ALU.mult))
                    step.link(dve.tensor_reduce(sel[:, i, s], hit[:], AX_X, ALU.add))
                step.link(dve.tensor_tensor(dif[:], best[:, i],
                                            best[:, i, :, 0:1].to_broadcast([P, PH, TOPK]), ALU.subtract))
                step.link(dve.tensor_copy(best[:, i], dif[:]))
            dve.sem_inc(dif_ready, 1)
            dve.wait_ge(gexp_ready, 1)
            for t in range(NT):
                step.link(dve.tensor_reduce(gsum[:], best[:, t], AX_X, ALU.add))
                step.link(dve.reciprocal(gsum[:], gsum[:]))
                dve.tensor_tensor(sel[:, t, 2].rearrange("p (h k) -> p h k", h=PH), best[:, t],
                                  gsum[:][:, :, None].to_broadcast([P, PH, TOPK]), ALU.mult).then_inc(sel_ready, 1)
                dve.wait_ge(sel_ready, t + 1)

            dve.wait_ge(selT_taken, 1)
            with dve.Fori(0, NCHUNK) as i:
                step.restart()
                for j in range(GROUP):
                    dve.wait_ge(g_ready, (i * GROUP + j) * 2 + 2)
                    tok = bass.ds(i * CTOK + j * TOK8, TOK8)

                    def spread(k):
                        return selT[:, k, tok][:, :, None].to_broadcast([P, TOK8, KEYS])

                    every = iota[:][:, None, :].to_broadcast([P, TOK8, KEYS])
                    step.link(dve.tensor_tensor(hot1[:, j % 2], every, spread(0), ALU.is_equal))
                    dve.tensor_tensor(hot2[:, j % 2], every, spread(1), ALU.is_equal)
                    dve.tensor_tensor(hot1[:, j % 2], hot1[:, j % 2], spread(2), ALU.mult).then_inc(hot_ready, 1)

            def weighted(g, p, turn):
                dve.wait_ge(ag_landed[p], turn)
                dve.wait_ge(y_ready, g * 16 + 16)
                for j in range(GROUP):
                    dve.tensor_tensor(wb[:, p, j].rearrange("p (c t) -> p c t", c=NCHUNK),
                                      aring[:, p, j].rearrange("p (c t) -> p c t", c=NCHUNK),
                                      gring[:, p, :, j * CTOK:(j + 1) * CTOK], ALU.mult).then_inc(w_ready, 1)

            def add_products(g):
                for n in range(2 * C):
                    b, h = n // 2, n % 2
                    dve.wait_ge(y_ready, g * 16 + (32 + n + 1))
                    dve.tensor_tensor(xT[:, b, half(h)], bank[n % 8][:, 0:HT], xT[:, b, half(h)],
                                      ALU.add).then_inc(y_taken, 1)

            pairs = KEYS // GROUP // 2
            weighted(0, 0, 32)
            with dve.Fori(0, pairs - 1) as i:
                weighted(i * 2 + 1, 1, (i + 1) * 32)
                add_products(i * 2)
                weighted(i * 2 + 2, 0, (i + 2) * 32)
                add_products(i * 2 + 1)
            weighted(2 * pairs - 1, 1, pairs * 32)
            add_products(2 * pairs - 2)
            add_products(2 * pairs - 1)
            dve.wait_ge(y_taken, 8 + 16 * 2 * pairs)
            normed(NORM_FINAL, xT, hT, T)


def kernel(**inputs):
    import concourse.bacc as _bacc
    from concourse.bass_utils import run_bass_kernel_spmd as _run

    a = {k: np.asarray(v) for k, v in inputs.items()}

    def chunked(w):
        k, n = w.shape
        return w.reshape(k // P, P, n // P, P).transpose(2, 1, 0, 3)

    def features(x):
        return x.T.reshape(-1, P, x.shape[0]).transpose(1, 0, 2)

    x = np.concatenate([a["x_prompt"][0], a["x_sample"][0]], 0)
    w_in = a["w_in"][0].reshape(C, P, NB_IN, HEADS, P).transpose(3, 2, 1, 0, 4)
    w_x = np.stack([chunked(a[n][0]).reshape(HEADS, 2, P, C, P) for n in ("w_xk", "w_xv", "w_xq")], 1)
    host = {
        "x": features(x),
        "mem": features(a["mem_prompt"][0]),
        "gains": np.stack([g.reshape(C, P).T for g in (a["g_mix"][0], a["g_mem"][0], a["g_cross"][0],
                                                       a["g_ffn"][0], a["g_final"])], 1),
        "lam": np.broadcast_to(np.stack([a[n][0] for n in ("lam_q1", "lam_k1", "lam_q2", "lam_k2")]),
                               (P, 4, DK)),
        "w_in": w_in,
        "w_out": chunked(a["w_out"][0]),
        "w_x": w_x.reshape(HEADS, NB_X, P, C, P),
        "w_xo": chunked(a["w_xo"][0]),
        "w_pq": chunked(a["w_pq"][0]).reshape(PH // 2, 4, P, C, P),
        "keys": np.stack([a["peer_k1"][0], a["peer_k2"][0]], 1).transpose(0, 3, 1, 2).reshape(
            PH // 2, 2, P, 2, KEYS),
        "cache_k": a["cache_da_k"][0, 0].reshape(PAST, HEADS, 2 * DK).transpose(1, 2, 0),
        "cache_v": a["cache_da_v"][0, 0].transpose(1, 0, 2),
        "state": a["state_ret"][0, 0],
        "cache_mem_k": a["cache_mem_k"][0, 0].transpose(1, 2, 0).reshape(HEADS, 2, P, MEM).transpose(0, 2, 1, 3),
        "cache_mem_v": a["cache_mem_v"][0, 0].reshape(2, P, HEADS, MEM).transpose(2, 1, 0, 3),
        "u": a["peer_u"][0].reshape(KEYS // GROUP, GROUP, KEYS, C, P).transpose(0, 1, 4, 3, 2),
        "v": a["peer_v"][0].reshape(KEYS // GROUP, GROUP, KEYS, D),
    }
    r = np.arange(P)
    far = -np.abs(r[:, None] - (np.arange(TP)[None, :] - (TP - P))).astype(np.float64)
    ahead = (np.arange(TP)[None, :] - (TP - P)) // CHUNK > r[:, None] // CHUNK
    log_g = np.log1p(-(2.0 ** (-5.0 - np.arange(HEADS))))
    gap = r[None, None, :] - r[:, None, None]
    par = np.zeros((P, HEADS, NPAR))
    par[:, :, SLOPE8] = 2.0 ** (-8.0 * np.arange(1, HEADS + 1) / HEADS) * DK ** 0.5
    par[:, :, GAMMA_L] = np.exp(P * log_g)
    par[:, :, GAMMA_LS] = np.exp(TS * log_g)
    par[:, :, TAIL] = np.exp((P - 1 - r)[:, None] * log_g)
    par[:, :, TAIL_S] = np.exp(np.maximum(TS - 1 - r, 0)[:, None] * log_g)
    par = par.astype(np.float32)
    par[:, :, G_DA] = a["g_da"][0].T
    par[:, :, G_RET] = a["g_ret"][0].T
    host.update({
        "ident": np.eye(P), "ones": np.ones((P, P)), "iota": np.broadcast_to(r, (P, P)),
        "eps": np.broadcast_to([EPS, EPS / (1.0 - LAM_INIT) ** 2], (P, 2)),
        "par": par,
        "dist": np.where(ahead, NEG, far),
        "dist_s": -np.abs(PAST + np.arange(TS)[:, None] - np.arange(PAST + TS)[None, :]),
        "decay": np.where(gap >= 0, np.exp(np.maximum(gap, 0) * log_g[None, :, None]), 0.0),
        "cross_scale": np.broadcast_to(np.exp((r + 1) * log_g[:, None]), (P, HEADS, P)),
    })
    outs = {
        "y": (P, C, T), "kd_out": (HEADS, P, T), "vd_out": (HEADS, P, 4, P), "vds_out": (HEADS, TS, P),
        "st_out": (HEADS, 2, P, P), "mk_out": (HEADS, P, 2, MEM), "mv_out": (HEADS, P, 2, MEM),
    }
    scratch = {"act": (KEYS // GROUP, GROUP, P, T), "gates": (NCHUNK, P, KEYS // GROUP, GROUP * CTOK)}

    nc = _bacc.Bacc("TRN2", target_bir_lowering=False, num_devices=1)
    arrays, d = {}, {}
    for name, v in host.items():
        arrays["in_" + name] = np.ascontiguousarray(v, dtype=np.float32)
        d[name] = nc.dram_tensor("in_" + name, arrays["in_" + name].shape, F32, kind="ExternalInput").ap()
    for name, shape in outs.items():
        d[name] = nc.dram_tensor("out_" + name, shape, F32, kind="ExternalOutput").ap()
    for name, shape in scratch.items():
        d[name] = nc.dram_tensor("scratch_" + name, shape, F32, kind="Internal").ap()
    encoder_step(nc, d)
    res = _run(nc, [arrays], core_ids=[0]).results[0]
    o = {name: np.asarray(res["out_" + name]) for name in outs}

    y = o["y"].transpose(2, 1, 0).reshape(T, D)
    kd = o["kd_out"].reshape(HEADS, 2, DK, T).transpose(3, 0, 1, 2)
    vd = o["vd_out"].transpose(2, 1, 0, 3).reshape(TP, HEADS, P)
    mk = o["mk_out"].transpose(3, 0, 2, 1).reshape(MEM, HEADS, 2 * P)
    mv = o["mv_out"].transpose(2, 1, 0, 3).reshape(MEM, HEADS, 2 * P)
    return (y[None, :TP], y[None, TP:], kd[None, None, :TP], vd[None, None], o["st_out"][None, None, :, 0],
            mk[None, None], mv[None, None], kd[None, None, TP:],
            o["vds_out"].transpose(1, 0, 2)[None, None], o["st_out"][None, None, :, 1])
```

```python
from contextlib import ExitStack

import numpy as np

import concourse.bass as bass
from concourse import mybir

ALU = mybir.AluOpType
ACT = mybir.ActivationFunctionType
AX_X = mybir.AxisListType.X
F32 = mybir.dt.float32
F32R = mybir.dt.float32r
U32 = mybir.dt.uint32

P = 128
D = 1024
C = D // P
TP, TS = 512, 32
T = TP + TS
HT = T // 2
TILES = [(0, 128), (128, 128), (256, 128), (384, 128), (512, 32)]
NT = len(TILES)
HEADS = 4
DK = 64
PAST = 128
CHUNK = 64
MEM = 256
PH = 8
KEYS = 128
TOPK = 16
EPS = 1e-6
LAM_INIT = 0.8 - 0.6
NEG = -1e30
FLOOR = -3.0e38

SLOPE8, G_DA, G_RET, GAMMA_L, GAMMA_LS, TAIL, TAIL_S = range(7)
NPAR = 8
QD, KD, VD, QR, KR, VR, GR = range(7)
NB_IN = 7
NB_X = 6

GROUP = 4
TOK8 = 8
CTOK = GROUP * TOK8
NCHUNK = T // CTOK
U2_GROUPS = NCHUNK
U3_GROUPS = 1
U1_GROUPS = KEYS // GROUP - U2_GROUPS - U3_GROUPS
NPQ = 2 * PH


class Plan:

    def __init__(self, nc, start):
        self.nc, self.end, self.start_of = nc, start, {}

    def place(self, name, shape, dt=F32):
        at = -(-self.end // 32) * 32
        self.start_of[name] = at
        self.end = at + 4 * int(np.prod(shape[1:]))
        return self.nc.alloc_sbuf_tensor_at(name, shape, dt, offset=at)


class Steps:

    def __init__(self, eng, sem):
        self.eng, self.sem, self.here = eng, sem, 0

    def restart(self):
        self.eng.sem_clear(self.sem)
        self.here = 0

    def link(self, ins):
        ins.then_inc(self.sem, 1)
        self.here += 1
        self.eng.wait_ge(self.sem, self.here)


def encoder_step(nc, d):
    with ExitStack() as whole:
        def sem(name):
            return whole.enter_context(nc.semaphore(name))

        plan = Plan(nc, nc.sbuf_base)
        xT = plan.place("xT", [P, C, T])
        sq = plan.place("sq", [P, 2, T])
        rms = plan.place("rms", [P, T])
        ident = plan.place("ident", [P, P])
        ones = plan.place("ones", [P, P])
        eps = plan.place("eps", [P, 2])
        gains = plan.place("gains", [P, 5, C])
        par = plan.place("par", [P, HEADS, NPAR])
        iota = plan.place("iota", [P, P])
        lam_in = plan.place("lam_in", [P, 4, DK])
        lam = plan.place("lam", [P, 4])
        wring = plan.place("wring", [P, NB_IN, C, P])
        bank = [whole.enter_context(nc.psum_tensor(f"bank{b}", [P, 512], F32)) for b in range(8)]

        x_landed, const_landed = sem("x_landed"), sem("const_landed")
        w_landed = [sem(f"w_landed{s}") for s in range(NB_IN)]
        sq_ready, sq_used, rms_ready = sem("sq_ready"), sem("sq_used"), sem("rms_ready")
        h_ready = sem("h_ready")
        vec, passed = sem("vec_steps"), sem("waits_passed")
        lam_ready = sem("lam_ready")
        out_stored = sem("out_stored")
        in_done, in_taken = sem("in_done"), sem("in_taken")
        cache_landed = sem("cache_landed")
        s_ready, s_taken, max_ready, e_ready = sem("s_ready"), sem("s_taken"), sem("max_ready"), sem("e_ready")
        a_ready, at_ready, at_taken, pv_ready, pv_taken = (
            sem("a_ready"), sem("at_ready"), sem("at_taken"), sem("pv_ready"), sem("pv_taken"))
        par_ready = sem("par_ready")
        dsq_ready, dss_ready, drms_ready, mixed_ready = (
            sem("dsq_ready"), sem("dss_ready"), sem("drms_ready"), sem("mixed_ready"))
        kt_ready, kn_ready, inner_ready, im_ready = (
            sem("kt_ready"), sem("kn_ready"), sem("inner_ready"), sem("im_ready"))
        qs_ready, u_ready, st_ready, ro_ready, ro_copied, mean_ready, oc_ready = (
            sem("qs_ready"), sem("u_ready"), sem("st_ready"), sem("ro_ready"), sem("ro_copied"),
            sem("mean_ready"), sem("oc_ready"))
        kd_stored, vd_stored, st_stored = sem("kd_stored"), sem("vd_stored"), sem("st_stored")
        wo_done, wo_taken = sem("wo_done"), sem("wo_taken")
        xo_done, xo_taken = sem("xo_done"), sem("xo_taken")
        mem_landed = sem("mem_landed")
        x_done, x_taken = sem("x_done"), sem("x_taken")
        cm_landed = sem("cm_landed")
        xs_ready, xmax_ready, xe_ready, xp_ready, xt_ready, xt_taken, xpv_ready, xpv_taken = (
            sem("xs_ready"), sem("xmax_ready"), sem("xe_ready"), sem("xp_ready"), sem("xt_ready"),
            sem("xt_taken"), sem("xpv_ready"), sem("xpv_taken"))
        mk_stored, mv_stored = sem("mk_stored"), sem("mv_stored")
        unit_done, unit_taken = sem("unit_done"), sem("unit_taken")
        hi_ready, lo_ready = sem("hi_ready"), sem("lo_ready")
        hc_ready, hhi_ready = sem("hc_ready"), sem("hhi_ready")
        pk_landed = [sem("pk_landed0"), sem("pk_landed1")]
        sc_ready, sc_taken = sem("sc_ready"), sem("sc_taken")
        dif_ready, gexp_ready, sel_ready, selT_ready, selT_taken = (
            sem("dif_ready"), sem("gexp_ready"), sem("sel_ready"), sem("selT_ready"), sem("selT_taken"))
        act_stored = [sem(f"act_stored{j}") for j in range(GROUP)]
        hot_ready, g_ready, g_taken = sem("hot_ready"), sem("g_ready"), sem("g_taken")
        kd_free, vd_free, st_free, mk_free, mv_free = (
            sem("kd_free"), sem("vd_free"), sem("st_free"), sem("mk_free"), sem("mv_free"))
        g_stored = [sem("g_stored0"), sem("g_stored1")]
        wf_ready, whi_ready = sem("wf_ready"), sem("whi_ready")
        ag_landed = [sem("ag_landed0"), sem("ag_landed1")]
        w_ready, y_ready, y_taken = sem("w_ready"), sem("y_ready"), sem("y_taken")

        front = Plan(nc, plan.end)

        def fr(name, shape, dt=F32):
            return front.place(name, shape, dt)

        hT = fr("hT", [P, C, T])
        dist = fr("dist", [P, TP])
        dist_s = fr("dist_s", [P, PAST + TS])
        decay = fr("decay", [P, HEADS, P])
        cross_scale = fr("cross_scale", [P, HEADS, P])
        mixedT = fr("mixedT", [P, C, T])
        memT = fr("memT", [P, C, MEM])
        memn = fr("memn", [P, C, MEM])
        hp = fr("hp", [P, NPAR])
        qdT, kdT, qrT, krT, grT = (fr(n, [P, T]) for n in ("qdT", "kdT", "qrT", "krT", "grT"))
        vd, vr, kn = (fr(n, [P, NT, P]) for n in ("vd", "vr", "kn"))
        ck, cv, st_in = fr("ck", [P, PAST]), fr("cv", [P, P]), fr("st_in", [P, P])
        S = fr("S", [P, 2, 2, TP])
        mx, nmx, rs, ri = (fr(n, [P, 2, 2]) for n in ("mx", "nmx", "rs", "ri"))
        aT = fr("aT", [P, TP])
        od = fr("od", [P, T])
        sqo = fr("sqo", [P, T])
        rmo = fr("rmo", [P, T])
        qs = fr("qs", [P, T])
        im = fr("im", [P, TP + TS])
        st = fr("st", [P, NT, P])
        ro = fr("ro", [P, T])
        mkT, mv = fr("mkT", [P, 2, MEM]), fr("mv", [P, 2, MEM])
        cmk, cmv = fr("cmk", [P, 2, MEM]), fr("cmv", [P, 2, MEM])
        xqT = fr("xqT", [P, 2, T])
        E = fr("E", [P, 2, MEM])
        eT = fr("eT", [P, MEM])
        xm, xn, xr = (fr(n, [P, 2]) for n in ("xm", "xn", "xr"))

        first = Plan(nc, plan.end)
        hs = [first.place(n, [P, C, T], F32R) for n in ("h_hi", "h_lo")]
        us = [first.place(n, [P, 2, C, P], F32R) for n in ("u_hi", "u_lo")]
        actb = first.place("actb", [P, GROUP, T])
        gates_at = first.end
        gate_plan = Plan(nc, gates_at)
        hot2 = gate_plan.place("hot2", [P, 2, TOK8, KEYS])
        hot1 = gate_plan.place("hot1", [P, 2, TOK8, KEYS])
        selT = gate_plan.place("selT", [P, 3, NT * P])
        gst = gate_plan.place("gst", [P, 2, KEYS, CTOK])
        sel = gate_plan.place("sel", [P, NT, 3, P])
        ret = Plan(nc, gates_at)
        sc = ret.place("sc", [P, PH, 2, NT, KEYS])
        scores_now = ret.place("scores_now", [P, 2, NT, KEYS])
        hc = ret.place("hc", [P, 2, T])
        pk = ret.place("pk", [P, 2, 2, KEYS])
        qpT = ret.place("qpT", [P, 2, T])
        assert ret.end <= gate_plan.start_of["sel"]
        ret.end = max(ret.end, gate_plan.end)
        hit = ret.place("hit", [P, PH * TOPK, TOPK])
        scr = ret.place("scr", [P, TOPK * TOPK])
        cand = ret.place("cand", [P, TOPK, TOPK])
        v16 = ret.place("v16", [P, 2, NT, TOPK])
        i16 = ret.place("i16", [P, 2, NT, TOPK], U32)
        c16 = ret.place("c16", [P, NT, TOPK])
        p16 = ret.place("p16", [P, NT, TOPK], U32)
        best = ret.place("best", [P, NT, PH, TOPK])
        pos = ret.place("pos", [P, NT, PH, TOPK], U32)
        key1 = ret.place("key1", [P, NT, PH, TOPK])
        key2 = ret.place("key2", [P, NT, PH, TOPK])
        rank = ret.place("rank", [P, 2, PH * TOPK], U32)
        rankf = ret.place("rankf", [P, 2, PH * TOPK])
        dif = ret.place("dif", [P, PH, TOPK])
        gsum = ret.place("gsum", [P, PH])

        over_first, over_gates = Plan(nc, plan.end), Plan(nc, gates_at)
        over_ret = Plan(nc, gate_plan.start_of["sel"])
        vs = [[pl.place(f"v_{n}{p}", [P, GROUP, D], F32R) for n in ("hi", "lo")]
              for p, pl in ((0, over_gates), (1, over_first))]
        wbs = [[pl.place(f"w_{n}{p}", [P, GROUP, T], F32R) for n in ("hi", "lo")]
               for p, pl in ((0, over_gates), (1, over_first))]
        aring = [over_ret.place("a0", [P, GROUP, T]), over_first.place("a1", [P, GROUP, T])]
        gring = [over_ret.place(f"g{p}", [P, NCHUNK, GROUP * CTOK]) for p in range(2)]
        wf = over_ret.place("wf", [P, 2, T])
        assert over_first.end <= gates_at and over_gates.end <= gate_plan.start_of["sel"]
        yT = Plan(nc, plan.end).place("yT", [P, C, T])

        block = whole.enter_context(nc.Block())

        def half(h):
            return slice(h * HT, (h + 1) * HT)

        def tile_cols(t):
            return slice(TILES[t][0], TILES[t][0] + TILES[t][1])

        CONSTS = [(ident, "ident"), (ones, "ones"), (eps, "eps"), (gains, "gains"), (par, "par"),
                  (iota, "iota"), (lam_in, "lam"), (dist, "dist"), (decay, "decay"),
                  (cross_scale, "cross_scale")]
        NCONST = 16 * (len(CONSTS) + 1)
        NORM_MIX, NORM_MEM, NORM_CROSS, NORM_FFN, NORM_FINAL = range(5)

        X_DONE = [1, 2, 4, 4, 6, 8]


        def results_stored(eng):
            eng.wait_ge(kd_stored, 16 * HEADS)
            eng.wait_ge(vd_stored, 32 * HEADS)
            eng.wait_ge(st_stored, 32 * HEADS)
            eng.wait_ge(mk_stored, 16 * HEADS)
            eng.wait_ge(mv_stored, 16 * HEADS)

        @block.sync
        def _(sp):
            for s in (*act_stored, *g_stored):
                sp.sem_inc(s, 16)
            sp.dma_start(xT[:], d["x"]).then_inc(x_landed, 16)
            for tile, name in CONSTS:
                sp.dma_start(tile[:], d[name]).then_inc(const_landed, 16)
            sp.dma_start(dist_s[0:TS, :], d["dist_s"]).then_inc(const_landed, 16)

            def weights(slot, src):
                sp.dma_start(wring[:, slot], src).then_inc(w_landed[slot], 16)

            for b in range(NB_IN):
                weights(b, d["w_in"][0, b])
            sp.dma_start(memT[:], d["mem"]).then_inc(mem_landed, 16)

            def head_cache(h):
                sp.dma_start(ck[:], d["cache_k"][h]).then_inc(cache_landed, 16)
                sp.dma_start(cv[:], d["cache_v"][h]).then_inc(cache_landed, 16)
                sp.dma_start(st_in[:], d["state"][h]).then_inc(cache_landed, 16)

            head_cache(0)
            with sp.Fori(0, HEADS - 1) as i:
                for b in range(NB_IN):
                    sp.wait_ge(in_done, i * 14 + 2 * (b + 1))
                    weights(b, d["w_in"][i + 1, b])
                sp.wait_ge(ro_ready, i + 1)
                head_cache(i + 1)
            for b in range(4):
                sp.wait_ge(in_done, (HEADS - 1) * 14 + 2 * (b + 1))
                weights(b, d["w_out"][b])
            for b in range(4):
                sp.wait_ge(wo_done, 2 * (b + 1))
                weights(b, d["w_out"][4 + b])
            for b in range(NB_X):
                if b < 4:
                    sp.wait_ge(wo_done, 8 + 2 * (b + 1))
                else:
                    sp.wait_ge(in_done, (HEADS - 1) * 14 + 2 * (b + 1))
                weights(b, d["w_x"][0, b])
            def head_mem(h):
                sp.dma_start(cmk[:], d["cache_mem_k"][h]).then_inc(cm_landed, 16)
                sp.dma_start(cmv[:], d["cache_mem_v"][h]).then_inc(cm_landed, 16)

            head_mem(0)
            with sp.Fori(0, HEADS - 1) as i:
                for b in range(NB_X):
                    sp.wait_ge(x_done, i * 8 + X_DONE[b])
                    weights(b, d["w_x"][i + 1, b])
                sp.wait_ge(xpv_ready, (i + 1) * NT)
                head_mem(i + 1)
            for b in range(4):
                sp.wait_ge(x_done, (HEADS - 1) * 8 + X_DONE[b])
                weights(b, d["w_xo"][b])
            for b in range(4):
                sp.wait_ge(xo_done, 2 * (b + 1))
                weights(b, d["w_xo"][4 + b])

            for b in range(4):
                sp.wait_ge(xo_done, 8 + 2 * (b + 1))
                weights(b, d["w_pq"][0, b])

            def load_keys(slot, src):
                sp.dma_start(pk[:, slot], src).then_inc(pk_landed[slot], 16)

            sp.wait_ge(h_ready, C * (NORM_FFN + 1))
            results_stored(sp)
            for j in range(2):
                load_keys(j, d["keys"][0, j])
            with sp.Fori(0, PH // 2 - 1) as i:
                for j in range(2):
                    for s in range(2):
                        b = 2 * j + s
                        sp.wait_ge(lo_ready, i * 4 + b + 1)
                        weights(b, d["w_pq"][i + 1, b])
                    sp.wait_ge(sc_ready, i * 2 + j + 1)
                    load_keys(j, d["keys"][i + 1, j])
            for b in range(4):
                sp.wait_ge(lo_ready, NPQ - 4 + b + 1)
                weights(b, d["u"][0, b])

            def first_group(g, table, nxt):
                for j in range(GROUP):
                    sp.wait_ge(lo_ready, g * GROUP + (NPQ + j + 1))
                    weights(j, table[nxt, j])
                    sp.wait_ge(unit_taken, (g * GROUP + j) * 2 + (4 + 2 * NPQ + 2))
                    sp.dma_start(d["act"][g, j], actb[:, j]).then_inc(act_stored[j], 16)

            def chunk_gates(c, p):
                sp.wait_ge(g_taken, c * 8 + 10)
                sp.sem_inc(passed, 1)
                sp.dma_start(d["gates"][c].rearrange("p g k -> p (g k)"),
                             gst[:, p].rearrange("p k t -> p (k t)")).then_inc(g_stored[p], 16)

            with sp.Fori(0, U1_GROUPS) as i:
                first_group(i, d["u"], i + 1)
            with sp.Fori(0, NCHUNK // 2) as i:
                for p in range(2):
                    first_group(i * 2 + (U1_GROUPS + p), d["u"], i * 2 + (U1_GROUPS + p + 1))
                    chunk_gates(i * 2 + p, p)
            first_group(U1_GROUPS + NCHUNK - 1, d["u"], U1_GROUPS + NCHUNK)
            chunk_gates(NCHUNK - 1, 0)
            first_group(KEYS // GROUP - 1, d["v"], 0)

            def load_group(g, p):
                sp.dma_start(aring[p][:], d["act"][g].rearrange("j p t -> p j t")).then_inc(ag_landed[p], 16)
                sp.dma_start(gring[p][:], d["gates"][:, :, g].rearrange("c p k -> p c k")).then_inc(ag_landed[p], 16)

            sp.wait_ge(g_stored[0], 16 + 16 * ((NCHUNK + 1) // 2))
            sp.wait_ge(g_stored[1], 16 + 16 * (NCHUNK // 2))
            load_group(0, 0)
            for j in range(GROUP):
                sp.wait_ge(act_stored[j], 16 + 16 * (KEYS // GROUP))
            sp.wait_ge(unit_done, 4 + 2 * (NPQ + KEYS))
            load_group(1, 1)
            vb = NPQ + KEYS

            def second_tiles(g, nxt):
                for j in range(GROUP):
                    sp.wait_ge(lo_ready, g * GROUP + (vb + j + 1))
                    sp.sem_inc(passed, 1)
                    weights(j, d["v"][nxt, j])

            with sp.Fori(0, KEYS // GROUP // 2 - 1) as i:
                for p in range(2):
                    second_tiles(i * 2 + p, i * 2 + (p + 1))
                    sp.wait_ge(wf_ready, (i * 2 + p + 1) * GROUP)
                    sp.sem_inc(passed, 1)
                    load_group(i * 2 + (2 + p), p)
            second_tiles(KEYS // GROUP - 2, KEYS // GROUP - 1)

            sp.wait_ge(h_ready, C * (NORM_FINAL + 1))
            sp.dma_start(d["y"], yT[:]).then_inc(out_stored, 16)
            sp.wait_ge(out_stored, 16)
            results_stored(sp)

        @block.gpsimd
        def _(pool):
            for s in (kd_free, vd_free, st_free, mk_free, mv_free):
                pool.sem_inc(s, 1)

            def ready(s, n):
                pool.wait_ge(s, n)
                pool.sem_inc(passed, 1)

            def stored(s, n, free):
                pool.wait_ge(s, n)
                pool.sem_inc(free, 1)

            with pool.Fori(0, HEADS) as i:
                ready(in_taken, 2 + i * 14 + 4)
                pool.dma_start(d["kd_out"][i], kdT[:]).then_inc(kd_stored, 16)
                ready(in_taken, 2 + i * 14 + 6)
                pool.dma_start(d["vd_out"][i], vd[:, 0:4]).then_inc(vd_stored, 16)
                pool.dma_start(d["vds_out"][i], vd[0:TS, 4]).then_inc(vd_stored, 16)
                stored(kd_stored, (i + 1) * 16, kd_free)
                stored(vd_stored, (i + 1) * 32, vd_free)
                ready(st_ready, i + 1)
                pool.dma_start(d["st_out"][i, 0], st[:, 3]).then_inc(st_stored, 16)
                pool.dma_start(d["st_out"][i, 1], st[:, 4]).then_inc(st_stored, 16)
                stored(st_stored, (i + 1) * 32, st_free)
            with pool.Fori(0, HEADS) as i:
                ready(x_taken, 2 + i * 8 + 2)
                pool.dma_start(d["mk_out"][i], mkT[:]).then_inc(mk_stored, 16)
                ready(x_taken, 2 + i * 8 + 4)
                pool.dma_start(d["mv_out"][i], mv[:]).then_inc(mv_stored, 16)
                stored(mk_stored, (i + 1) * 16, mk_free)
                stored(mv_stored, (i + 1) * 16, mv_free)

            def low(n, slot, dst, hi):
                pool.wait_ge(hi_ready, n + 1)
                pool.tensor_tensor(dst, wring[:, slot], hi.bitcast(F32), ALU.subtract).then_inc(lo_ready, 1)

            with pool.Fori(0, (NPQ + KEYS) // 4) as i:
                for j in range(4):
                    low(i * 4 + j, j, us[1][:, j % 2], us[0][:, j % 2])
            with pool.Fori(0, KEYS // GROUP // 2) as i:
                for p in range(2):
                    for j in range(GROUP):
                        low(i * 8 + (NPQ + KEYS + 4 * p + j), j,
                            vs[p][1][:, j].rearrange("p (c n) -> p c n", c=C),
                            vs[p][0][:, j].rearrange("p (c n) -> p c n", c=C))

        @block.tensor
        def _(pe):
            def norm_sums(k, n):
                for c in range(C):
                    pe.wait_ge(sq_ready, C * k + c + 1)
                    if c == 0 and k > 0:
                        pe.wait_ge(rms_ready, k)
                    if n == T:
                        pe.matmul(bank[6][:, 0:HT], ones[:], sq[:, c % 2, 0:HT], start=c == 0, stop=c == C - 1)
                        m = pe.matmul(bank[7][:, 0:HT], ones[:], sq[:, c % 2, HT:T], start=c == 0, stop=c == C - 1)
                    else:
                        m = pe.matmul(bank[6][:, 0:n], ones[:], sq[:, c % 2, 0:n], start=c == 0, stop=c == C - 1)
                    m.then_inc(sq_used, 1)

            pe.sem_inc(g_ready, 4)
            pe.sem_inc(y_ready, 32)
            pe.sem_inc(unit_done, 4)
            pe.wait_ge(const_landed, NCONST)
            norm_sums(NORM_MIX, T)
            norm_sums(NORM_MEM, MEM)

            def project_T(i, k, slot):
                pe.wait_ge(w_landed[slot], (i + 1) * 16)
                for h in range(2):
                    pe.wait_ge(in_taken, i * 14 + (k + h + 1))
                    for c in range(C):
                        m = pe.matmul(bank[h][:, 0:HT], wring[:, slot, c], hT[:, c, half(h)],
                                      start=c == 0, stop=c == C - 1)
                    m.then_inc(in_done, 1)

            def project_rows(i, k, slot):
                pe.wait_ge(w_landed[slot], (i + 1) * 16)
                for u, tiles in enumerate((range(4), [4])):
                    pe.wait_ge(in_taken, i * 14 + (k + u + 1))
                    for t in tiles:
                        rows = TILES[t][1]
                        for c in range(C):
                            m = pe.matmul(bank[u][0:rows, (t % 4) * P:(t % 4 + 1) * P], hT[:, c, tile_cols(t)],
                                          wring[:, slot, c], start=c == 0, stop=c == C - 1)
                    m.then_inc(in_done, 1)

            def scores(i, t):
                q0, rows = TILES[t]
                pe.wait_ge(s_taken, i * NT + t + 1)
                if t == 4:
                    pe.wait_ge(cache_landed, (i + 1) * 48)
                    pe.sem_inc(passed, 1)
                for m_ in range(2):
                    ps = slice(DK * m_, DK * m_ + DK)
                    lhs = qdT[ps, q0:q0 + rows]
                    if t < 4:
                        m = pe.matmul(bank[2 + m_][0:rows, 0:q0 + rows], lhs, kdT[ps, 0:q0 + rows],
                                      start=True, stop=True)
                    else:
                        pe.matmul(bank[2 + m_][0:rows, 0:PAST], lhs, ck[ps, :], start=True, stop=True)
                        m = pe.matmul(bank[2 + m_][0:rows, PAST:PAST + TS], lhs, kdT[ps, q0:q0 + rows],
                                      start=True, stop=True)
                m.then_inc(s_ready, 1)

            def turn(i, t):
                rows = TILES[t][1]
                pe.wait_ge(a_ready, i * NT + t + 1)
                pe.wait_ge(at_taken, i * NT + t + 1)
                if t == 4:
                    pe.sem_inc(passed, 1)
                if t < 4:
                    for k in range(t + 1):
                        m = pe.transpose(bank[4][:, k * P:(k + 1) * P], S[:, t % 2, 0, k * P:(k + 1) * P], ident[:])
                else:
                    pe.transpose(bank[4][:, 0:rows], S[0:rows, 0, 0, 0:PAST], ident[0:rows, 0:rows])
                    m = pe.transpose(bank[4][0:TS, P:P + rows], S[0:rows, 0, 0, PAST:PAST + TS],
                                     ident[0:rows, 0:rows])
                m.then_inc(at_ready, 1)

            def values(i, t):
                rows = TILES[t][1]
                pe.wait_ge(at_taken, i * NT + t + 2)
                pe.wait_ge(pv_taken, i * NT + t + 1)
                o = bank[5 + t % 2][:, 0:rows]
                if t < 4:
                    for k in range(t + 1):
                        m = pe.matmul(o, vd[:, k], aT[:, k * P:(k + 1) * P], start=k == 0, stop=k == t)
                else:
                    pe.matmul(o, cv[:], aT[:, 0:rows], start=True, stop=False)
                    m = pe.matmul(o, vd[0:TS, 4], aT[0:TS, P:P + rows], start=False, stop=True)
                m.then_inc(pv_ready, 1)

            def sums(src, ready_sem, value, done):
                pe.wait_ge(ready_sem, value)
                pe.matmul(bank[6][:, 0:HT], ones[:], src[:, 0:HT], start=True, stop=True)
                pe.matmul(bank[7][:, 0:HT], ones[:], src[:, HT:T], start=True, stop=True).then_inc(done, 1)

            pe.wait_ge(h_ready, C)
            with pe.Fori(0, HEADS) as i:
                project_T(i, 0, QD)
                project_T(i, 2, KD)
                project_rows(i, 4, VD)
                pe.wait_ge(in_taken, i * 14 + 6 + 2)
                pe.wait_ge(ro_copied, i + 1)
                scores(i, 0)
                project_T(i, 6, QR)
                scores(i, 1)
                turn(i, 0)
                project_T(i, 8, KR)
                scores(i, 2)
                values(i, 0)
                turn(i, 1)
                project_rows(i, 10, VR)
                scores(i, 3)
                values(i, 1)
                turn(i, 2)
                project_T(i, 12, GR)
                scores(i, 4)
                values(i, 2)
                turn(i, 3)
                values(i, 3)
                turn(i, 4)
                for t in range(NT):
                    rows = TILES[t][1]
                    out = bank[0][:, t * P:(t + 1) * P] if t < 4 else bank[1][0:rows, 0:P]
                    if t == 0:
                        pe.wait_ge(in_taken, i * 14 + 14 + 2)
                    m = pe.transpose(out, krT[:, tile_cols(t)], ident[:])
                m.then_inc(kt_ready, 1)
                pe.wait_ge(s_taken, i * NT + 5 + 1)
                for t in range(NT):
                    rows = TILES[t][1]
                    out = bank[2][:, t * P:(t + 1) * P] if t < 4 else bank[3][0:rows, 0:rows]
                    m = pe.matmul(out, krT[:, tile_cols(t)], qrT[:, tile_cols(t)], start=True, stop=True)
                m.then_inc(inner_ready, 1)
                values(i, 4)
                pe.wait_ge(kn_ready, i + 1)
                for t in range(NT):
                    rows = TILES[t][1]
                    out = bank[0][:, t * P:(t + 1) * P] if t < 4 else bank[1][:, 0:P]
                    m = pe.matmul(out, kn[0:rows, t], vr[0:rows, t], start=True, stop=True)
                m.then_inc(u_ready, 1)
                sums(sqo, dsq_ready, i * 2 + 1, dss_ready)
                pe.wait_ge(im_ready, i + 1)
                pe.wait_ge(st_ready, i + 1)
                for t in range(NT):
                    q0, rows = TILES[t]
                    out = bank[2][:, q0:q0 + rows] if t < 4 else bank[3][:, 0:rows]
                    m = pe.matmul(out, vr[0:rows, t], im[0:rows, q0:q0 + rows], start=True, stop=t == 0)
                    if t:
                        before = st[:, t - 1] if t < 4 else st_in[:]
                        m = pe.matmul(out, before, qs[:, q0:q0 + rows], start=False, stop=True)
                m.then_inc(ro_ready, 1)
                pe.wait_ge(drms_ready, i * 2 + 1)
                sums(ro, ro_copied, i + 2, mean_ready)
                pe.wait_ge(oc_ready, i + 1)
                pe.wait_ge(dsq_ready, i * 2 + 2)
                pe.matmul(bank[6][:, 0:HT], ones[:], sqo[:, 0:HT], start=True, stop=True)
                pe.matmul(bank[7][:, 0:HT], ones[:], sqo[:, HT:T], start=True, stop=True).then_inc(dss_ready, 1)

            def output_projection(first, taken, done):
                with pe.Fori(0, 2) as i:
                    for b in range(4):
                        pe.wait_ge(w_landed[b], i * 16 + first[b])
                        for h in range(2):
                            pe.wait_ge(taken, i * 8 + (2 * b + h + 1))
                            for c in range(C):
                                m = pe.matmul(bank[h][:, 0:HT], wring[:, b, c], mixedT[:, c, half(h)],
                                              start=c == 0, stop=c == C - 1)
                            m.then_inc(done, 1)

            pe.wait_ge(mixed_ready, 2 + 2 * HEADS)
            output_projection([16 * (HEADS + 1)] * 4, wo_taken, wo_done)
            norm_sums(NORM_CROSS, T)

            pe.wait_ge(h_ready, C * (NORM_CROSS + 1))
            xw = [16 * (HEADS + 3)] * 4 + [16 * (HEADS + 1)] * 2
            with pe.Fori(0, HEADS) as i:
                def xland(b):
                    pe.wait_ge(w_landed[b], i * 16 + xw[b])

                def xunit(k):
                    pe.wait_ge(x_taken, i * 8 + (k + 1))
                    return bank[k % 2]

                for b in range(2):
                    xland(b)
                    o = xunit(b)
                    for c in range(C):
                        m = pe.matmul(o[:, 0:MEM], wring[:, b, c], memn[:, c], start=c == 0, stop=c == C - 1)
                    m.then_inc(x_done, 1)
                xland(2)
                xland(3)
                for mt in range(2):
                    o = xunit(2 + mt)
                    for b in range(2):
                        for c in range(C):
                            m = pe.matmul(o[:, b * P:(b + 1) * P], memn[:, c, mt * P:(mt + 1) * P],
                                          wring[:, 2 + b, c], start=c == 0, stop=c == C - 1)
                    m.then_inc(x_done, 1)
                for b in range(2):
                    xland(4 + b)
                    for h in range(2):
                        o = xunit(4 + 2 * b + h)
                        for c in range(C):
                            m = pe.matmul(o[:, 0:HT], wring[:, 4 + b, c], hT[:, c, half(h)],
                                          start=c == 0, stop=c == C - 1)
                        m.then_inc(x_done, 1)
                pe.wait_ge(x_taken, i * 8 + 8 + 2)

                def xscores(t):
                    rows = TILES[t][1]
                    if t >= 2:
                        pe.wait_ge(xe_ready, i * NT + (t - 1))
                    if t == 4:
                        pe.wait_ge(cm_landed, (i + 1) * 32)
                    src = mkT if t < 4 else cmk
                    for c in range(2):
                        m = pe.matmul(bank[2 + t % 2][0:rows, 0:MEM], xqT[:, c, tile_cols(t)], src[:, c],
                                      start=c == 0, stop=c == 1)
                    m.then_inc(xs_ready, 1)

                def xturn(t):
                    rows = TILES[t][1]
                    pe.wait_ge(xp_ready, i * NT + t + 1)
                    pe.wait_ge(xt_taken, i * NT + t + 1)
                    if t == 4:
                        pe.sem_inc(passed, 1)
                    for k in range(2):
                        m = pe.transpose(bank[4][:, k * P:k * P + rows], E[0:rows, t % 2, k * P:(k + 1) * P],
                                         ident[0:rows, 0:rows])
                    m.then_inc(xt_ready, 1)

                def xvalues(t):
                    rows = TILES[t][1]
                    pe.wait_ge(xt_taken, i * NT + t + 2)
                    pe.wait_ge(xpv_taken, i * NT + t + 1)
                    src = mv if t < 4 else cmv
                    for b in range(2):
                        o = bank[5 + t % 2][:, b * P:b * P + rows]
                        for k in range(2):
                            m = pe.matmul(o, src[:, k, b * P:(b + 1) * P], eT[:, k * P:k * P + rows],
                                          start=k == 0, stop=k == 1)
                    m.then_inc(xpv_ready, 1)

                xscores(0)
                xscores(1)
                for t in range(NT):
                    xturn(t)
                    xvalues(t)
                    if t + 2 < NT:
                        xscores(t + 2)

            pe.wait_ge(xpv_taken, 2 + HEADS * NT)
            wl = [16 * (2 * HEADS + 3)] * 4
            output_projection(wl, xo_taken, xo_done)
            norm_sums(NORM_FFN, T)

            def passes(out, whi, wlo, xhi, xlo, first, last):
                pe.matmul(out, whi, xhi, start=first, stop=False)
                pe.matmul(out, whi, xlo, start=False, stop=False)
                return pe.matmul(out, wlo, xhi, start=False, stop=last)

            def unit(n, j, h):
                pe.wait_ge(unit_taken, n * 2 + (h + 1))
                out = bank[(2 * j + h) % 4][:, 0:HT]
                if h == 0:
                    pe.wait_ge(hi_ready, n + 1)
                    pe.wait_ge(lo_ready, n + 1)
                for c in range(C):
                    m = passes(out, us[0][:, j % 2, c], us[1][:, j % 2, c], hs[0][:, c, half(h)],
                               hs[1][:, c, half(h)], c == 0, c == C - 1)
                m.then_inc(unit_done, 1)

            pe.wait_ge(h_ready, C * (NORM_FFN + 1))
            with pe.Fori(0, PH // 2) as i:
                for j in range(2):
                    for s in range(2):
                        for h in range(2):
                            unit(i * 4 + (2 * j + s), 2 * j + s, h)
                    pe.wait_ge(pk_landed[j], (i + 1) * 16)
                    pe.wait_ge(unit_taken, i * 8 + (4 * j + 4 + 4))
                    pe.wait_ge(sc_taken, i * 2 + (j + 1))
                    for s in range(2):
                        for t in range(NT):
                            rows = TILES[t][1]
                            o = bank[4 + s][:, t * P:(t + 1) * P] if t < 4 else bank[6][0:rows, s * P:(s + 1) * P]
                            m = pe.matmul(o, qpT[:, s, tile_cols(t)], pk[:, j, s], start=True, stop=True)
                    m.then_inc(sc_ready, 1)

            def first_products(g, j):
                for h in range(2):
                    unit(g * GROUP + (NPQ + j), j, h)

            pe.wait_ge(sc_taken, 1 + PH)
            with pe.Fori(0, U1_GROUPS) as i:
                for j in range(GROUP):
                    first_products(i, j)

            pe.wait_ge(sel_ready, NT)
            for t in range(NT):
                for k in range(3):
                    n = t * 3 + k
                    m = pe.transpose(bank[4 + n // 4][:, (n % 4) * P:(n % 4 + 1) * P], sel[:, t, k], ident[:])
            m.then_inc(selT_ready, 1)
            pe.wait_ge(selT_taken, 1)

            def gate_products(c, j):
                pe.wait_ge(hot_ready, (c * GROUP) + j + 1)
                for b in range(2):
                    pe.wait_ge(g_taken, (c * GROUP + j) * 2 + (b + 1))
                    for k in range(4):
                        m = pe.matmul(bank[4 + b][:, k * P:(k + 1) * P], hot2[:, j % 2, 4 * b + k],
                                      hot1[:, j % 2, 4 * b + k], start=True, stop=True)
                    m.then_inc(g_ready, 1)

            with pe.Fori(0, U2_GROUPS) as i:
                for j in range(GROUP):
                    first_products(i + U1_GROUPS, j)
                    gate_products(i, j)
            for j in range(GROUP):
                first_products(KEYS // GROUP - 1, j)

            pe.wait_ge(unit_taken, 4 + 2 * (NPQ + KEYS))
            pe.wait_ge(g_taken, 2 + 2 * GROUP * NCHUNK)
            with pe.Fori(0, KEYS // GROUP // 2) as i:
                for p in range(2):
                    pe.wait_ge(lo_ready, i * 8 + (NPQ + KEYS + 4 * (p + 1)))
                    pe.wait_ge(w_ready, (i * 2 + p + 2) * GROUP)
                    for n in range(2 * C):
                        b, h = n // 2, n % 2
                        pe.wait_ge(y_taken, (i * 2 + p) * (2 * C) + (n + 1))
                        for j in range(GROUP):
                            m = passes(bank[n % 8][:, 0:HT], vs[p][0][:, j, b * P:(b + 1) * P],
                                       vs[p][1][:, j, b * P:(b + 1) * P], wbs[p][0][:, j, half(h)],
                                       wbs[p][1][:, j, half(h)], j == 0, j == GROUP - 1)
                        m.then_inc(y_ready, 1)
            pe.wait_ge(y_taken, 8 + 2 * C * KEYS // GROUP)
            norm_sums(NORM_FINAL, T)

        @block.scalar
        def _(act):
            def norm_squares(k, src, n):
                for c in range(C):
                    if C * k + c >= 2:
                        act.wait_ge(sq_used, C * k + c - 1)
                    act.activation(sq[:, c % 2, 0:n], src[:, c], ACT.Square).then_inc(sq_ready, 1)
                act.wait_ge(sq_used, C * (k + 1))
                if k:
                    act.wait_ge(h_ready, C * k)
                if n == T:
                    act.activation(rms[:, 0:HT], bank[6][:, 0:HT], ACT.Sqrt, scale=1.0 / D, bias=eps[:, 0:1])
                    act.activation(rms[:, HT:T], bank[7][:, 0:HT], ACT.Sqrt, scale=1.0 / D,
                                   bias=eps[:, 0:1]).then_inc(rms_ready, 1)
                else:
                    act.activation(rms[:, 0:n], bank[6][:, 0:n], ACT.Sqrt, scale=1.0 / D,
                                   bias=eps[:, 0:1]).then_inc(rms_ready, 1)

            for s, n in ((in_taken, 2), (at_taken, 1), (ro_copied, 1), (x_taken, 2), (xt_taken, 1),
                         (unit_taken, 4), (sc_taken, 1), (g_taken, 2)):
                act.sem_inc(s, n)
            act.wait_ge(x_landed, 16)
            act.wait_ge(const_landed, NCONST)
            norm_squares(NORM_MIX, xT, T)
            act.wait_ge(lam_ready, 1)
            act.activation(lam[:, 2:4], lam[:, 0:2], ACT.Exp).then_inc(lam_ready, 1)
            act.wait_ge(mem_landed, 16)
            norm_squares(NORM_MEM, memT, MEM)

            with act.Fori(0, HEADS) as i:
                def unit(k, dst, src, fn=ACT.Copy, scale=1.0):
                    act.wait_ge(in_done, i * 14 + (k + 1))
                    act.activation(dst, src, fn, scale=scale).then_inc(in_taken, 1)

                def unit_T(k, dst, fn=ACT.Copy, scale=1.0):
                    for h in range(2):
                        unit(k + h, dst[:, half(h)], bank[h][:, 0:HT], fn, scale)

                def unit_rows(k, dst):
                    unit(k, dst[:, 0:4].rearrange("p t n -> p (t n)"), bank[0][:])
                    unit(k + 1, dst[0:TS, 4], bank[1][0:TS, 0:P])

                def exps(t):
                    rows = TILES[t][1]
                    keys = (t + 1) * P if t < 4 else PAST + TS
                    act.wait_ge(max_ready, i * NT + (t + 1))
                    for m in range(2):
                        s = S[0:rows, t % 2, m, 0:keys]
                        a = act.activation(s, s, ACT.Exp, scale=DK ** -0.5, bias=nmx[0:rows, t % 2, m:m + 1],
                                           accum_out=rs[0:rows, t % 2, m:m + 1])
                    a.then_inc(e_ready, 1)

                def turned(t):
                    rows = TILES[t][1]
                    act.wait_ge(at_ready, i * NT + (t + 1))
                    if t < 4:
                        a = act.activation(aT[:, 0:(t + 1) * P], bank[4][:, 0:(t + 1) * P], ACT.Copy)
                    else:
                        act.activation(aT[:, 0:rows], bank[4][:, 0:rows], ACT.Copy)
                        a = act.activation(aT[0:TS, P:P + rows], bank[4][0:TS, P:P + rows], ACT.Copy)
                    a.then_inc(at_taken, 1)

                unit_T(0, qdT)
                act.wait_ge(kd_free, i + 1)
                unit_T(2, kdT)
                act.wait_ge(vd_free, i + 1)
                unit_rows(4, vd)
                exps(0)
                unit_T(6, qrT)
                exps(1)
                turned(0)
                unit_T(8, krT, scale=P ** -0.5)
                exps(2)
                turned(1)
                unit_rows(10, vr)
                exps(3)
                turned(2)
                act.wait_ge(mixed_ready, i * 2 + 2)
                unit_T(12, grT, fn=ACT.Silu)
                exps(4)
                turned(3)
                turned(4)
                act.wait_ge(kt_ready, i + 1)
                act.wait_ge(par_ready, i + 1)
                act.activation(kn[:, 0:4].rearrange("p t n -> p (t n)"), bank[0][:], ACT.Copy,
                               scale=hp[:, TAIL:TAIL + 1])
                act.activation(kn[0:TS, 4], bank[1][0:TS, 0:P], ACT.Copy,
                               scale=hp[0:TS, TAIL_S:TAIL_S + 1]).then_inc(kn_ready, 1)
                act.wait_ge(pv_taken, (i + 1) * NT + 2)
                act.activation(sqo[:], od[:], ACT.Square).then_inc(dsq_ready, 1)
                act.wait_ge(dss_ready, i * 2 + 1)
                sc2 = (1.0 - LAM_INIT) ** 2
                act.activation(rmo[:, 0:HT], bank[6][:, 0:HT], ACT.Sqrt, scale=1.0 / (P * sc2), bias=eps[:, 1:2])
                act.activation(rmo[:, HT:T], bank[7][:, 0:HT], ACT.Sqrt, scale=1.0 / (P * sc2),
                               bias=eps[:, 1:2]).then_inc(drms_ready, 1)
                act.wait_ge(ro_ready, i + 1)
                act.activation(ro[:, 0:TP], bank[2][:], ACT.Copy)
                act.activation(ro[:, TP:T], bank[3][:, 0:TS], ACT.Copy).then_inc(ro_copied, 1)
                act.wait_ge(oc_ready, i + 1)
                act.activation(sqo[:], ro[:], ACT.Square).then_inc(dsq_ready, 1)
                act.wait_ge(dss_ready, i * 2 + 2)
                act.wait_ge(mixed_ready, i * 2 + 3)
                act.activation(rmo[:, 0:HT], bank[6][:, 0:HT], ACT.Sqrt, scale=1.0 / P, bias=eps[:, 0:1])
                act.activation(rmo[:, HT:T], bank[7][:, 0:HT], ACT.Sqrt, scale=1.0 / P,
                               bias=eps[:, 0:1]).then_inc(drms_ready, 1)

            act.wait_ge(wo_taken, 2 + 16)
            norm_squares(NORM_CROSS, xT, T)

            with act.Fori(0, HEADS) as i:
                def xunit(k, dst, width):
                    act.wait_ge(x_done, i * 8 + (k + 1))
                    act.activation(dst, bank[k % 2][:, 0:width], ACT.Copy).then_inc(x_taken, 1)

                act.wait_ge(mk_free, i + 1)
                for b in range(2):
                    xunit(b, mkT[:, b], MEM)
                act.wait_ge(mv_free, i + 1)
                for mt in range(2):
                    xunit(2 + mt, mv[:, mt], MEM)
                for b in range(2):
                    for h in range(2):
                        xunit(4 + 2 * b + h, xqT[:, b, half(h)], HT)

                def xexp(t):
                    rows = TILES[t][1]
                    act.wait_ge(xmax_ready, i * NT + (t + 1))
                    act.activation(E[0:rows, t % 2], bank[2 + t % 2][0:rows, 0:MEM], ACT.Exp,
                                   scale=(D // HEADS) ** -0.5, bias=xn[0:rows, t % 2:t % 2 + 1],
                                   accum_out=xr[0:rows, t % 2:t % 2 + 1]).then_inc(xe_ready, 1)

                def xturned(t):
                    rows = TILES[t][1]
                    act.wait_ge(xt_ready, i * NT + (t + 1))
                    act.activation(eT[:].rearrange("p (k n) -> p k n", k=2)[:, :, 0:rows],
                                   bank[4][:, 0:2 * P].rearrange("p (k n) -> p k n", k=2)[:, :, 0:rows],
                                   ACT.Copy).then_inc(xt_taken, 1)

                xexp(0)
                for t in range(NT):
                    if t + 1 < NT:
                        xexp(t + 1)
                    xturned(t)

            act.wait_ge(xo_taken, 2 + 16)
            norm_squares(NORM_FFN, xT, T)

            for c in range(C):
                act.wait_ge(hc_ready, c + 1)
                act.activation(hs[0][:, c], hc[:, c % 2], ACT.Copy).then_inc(hhi_ready, 1)

            def high(n, slot, landed, dst):
                act.wait_ge(w_landed[slot], landed)
                act.wait_ge(unit_done, n * 2 + 2)
                act.activation(dst, wring[:, slot], ACT.Copy).then_inc(hi_ready, 1)

            pq0 = 2 * HEADS + 5
            high(0, 0, 16 * pq0, us[0][:, 0])
            with act.Fori(0, PH // 2) as i:
                for j in range(2):
                    for s in range(2):
                        b = 2 * j + s
                        high(i * 4 + (b + 1), (b + 1) % 4, i * 16 + 16 * (pq0 + (b == 3)), us[0][:, (b + 1) % 2])
                        for h in range(2):
                            act.wait_ge(unit_done, i * 8 + (4 + 2 * b + h + 1))
                            act.activation(qpT[:, s, half(h)], bank[(2 * b + h) % 4][:, 0:HT],
                                           ACT.Copy).then_inc(unit_taken, 1)
                    act.wait_ge(sc_ready, i * 2 + (j + 1))
                    mine = sc[:, bass.ds(i * 2 + j, 1)].rearrange("p h s t n -> p (h s) t n")
                    for s in range(2):
                        act.activation(mine[:, s, 0:4].rearrange("p t n -> p (t n)"), bank[4 + s][:], ACT.Copy)
                    act.activation(mine[0:TS, :, 4], bank[6][0:TS, 0:2 * P].rearrange("p (s n) -> p s n", s=2),
                                   ACT.Copy).then_inc(sc_taken, 1)

            def activations(g, j, more=True):
                n = g * GROUP + (NPQ + j)
                if more:
                    high(n + 1, (j + 1) % 4, g * 16 + 16 * (pq0 + NPQ // 4 + (j == 3)), us[0][:, (j + 1) % 2])
                for h in range(2):
                    act.wait_ge(unit_done, n * 2 + (4 + h + 1))
                    if h == 0:
                        act.wait_ge(act_stored[j], (g + 1) * 16)
                    act.activation(actb[:, j, half(h)], bank[(2 * j + h) % 4][:, 0:HT],
                                   ACT.Gelu).then_inc(unit_taken, 1)

            with act.Fori(0, U1_GROUPS) as i:
                for j in range(GROUP):
                    activations(i, j)

            act.wait_ge(dif_ready, 1)
            act.activation(best[:].rearrange("p t h k -> p (t h k)"), best[:].rearrange("p t h k -> p (t h k)"),
                           ACT.Exp).then_inc(gexp_ready, 1)
            act.wait_ge(selT_ready, 1)
            for t in range(NT):
                for k in range(3):
                    n = t * 3 + k
                    a = act.activation(selT[:, k, t * P:(t + 1) * P],
                                       bank[4 + n // 4][:, (n % 4) * P:(n % 4 + 1) * P], ACT.Copy)
            a.then_inc(selT_taken, 1)

            def gate_chunk(c, p, turn):
                for j in range(GROUP):
                    activations(c + U1_GROUPS, j)
                    for b in range(2):
                        act.wait_ge(g_ready, 4 + (c * GROUP + j) * 2 + (b + 1))
                        if j == 0 and b == 0:
                            act.wait_ge(g_stored[p], turn)
                        t0 = j * TOK8 + 4 * b
                        act.activation(gst[:, p, :, t0:t0 + 4].rearrange("p k t -> p t k"),
                                       bank[4 + b][:].rearrange("p (t k) -> p t k", t=4),
                                       ACT.Copy).then_inc(g_taken, 1)

            with act.Fori(0, NCHUNK // 2) as i:
                for p in range(2):
                    gate_chunk(i * 2 + p, p, (i + 1) * 16)
            gate_chunk(NCHUNK - 1, 0, (NCHUNK // 2 + 1) * 16)
            for j in range(GROUP):
                activations(KEYS // GROUP - 1, j, more=j < GROUP - 1)

            def second_group(g, p):
                for j in range(GROUP):
                    act.wait_ge(w_landed[j], g * 16 + 16 * (pq0 + NPQ // 4 + KEYS // GROUP))
                    if j == 0:
                        act.wait_ge(y_ready, g * 16 + 16)
                    act.activation(vs[p][0][:, j].rearrange("p (c n) -> p c n", c=C), wring[:, j],
                                   ACT.Copy).then_inc(hi_ready, 1)
                for j in range(GROUP):
                    act.wait_ge(wf_ready, g * GROUP + (j + 1))
                    act.activation(wbs[p][0][:, j], wf[:, j % 2], ACT.Copy).then_inc(whi_ready, 1)

            with act.Fori(0, KEYS // GROUP // 2) as i:
                for p in range(2):
                    second_group(i * 2 + p, p)

            act.wait_ge(y_taken, 8 + 2 * C * KEYS // GROUP)
            norm_squares(NORM_FINAL, xT, T)

        @block.vector
        def _(dve):
            step = Steps(dve, vec)

            def normed(k, src, dst, n):
                dve.wait_ge(rms_ready, k + 1)
                step.link(dve.reciprocal(rms[:, 0:n], rms[:, 0:n]))
                for c in range(C):
                    dve.scalar_tensor_tensor(out=dst[:, c], in0=src[:, c], scalar=gains[:, k, c:c + 1],
                                             in1=rms[:, 0:n], op0=ALU.mult, op1=ALU.mult).then_inc(h_ready, 1)

            for s, n in ((s_taken, 1), (pv_taken, 2), (mixed_ready, 2), (wo_taken, 2), (xo_taken, 2),
                         (xpv_taken, 2), (y_taken, 8), (w_ready, GROUP)):
                dve.sem_inc(s, n)
            dve.wait_ge(const_landed, NCONST)
            for m in range(2):
                a = dve.tensor_tensor_reduce(out=lam_in[:, 2 * m], in0=lam_in[:, 2 * m], in1=lam_in[:, 2 * m + 1],
                                             scale=1.0, scalar=0.0, op0=ALU.mult, op1=ALU.add,
                                             accum_out=lam[:, m:m + 1])
            a.then_inc(lam_ready, 1)
            dve.wait_ge(lam_ready, 2)
            step.link(dve.tensor_tensor(lam[:, 0:1], lam[:, 3:4], lam[:, 2:3], ALU.subtract))
            step.link(dve.tensor_scalar(lam[:, 0:1], lam[:, 0:1], -LAM_INIT, None, ALU.add))
            dve.wait_ge(x_landed, 16)
            normed(NORM_MIX, xT, hT, T)
            dve.wait_ge(mem_landed, 16)
            normed(NORM_MEM, memT, memn, MEM)

            with dve.Fori(0, HEADS) as i:
                step.restart()
                step.link(dve.tensor_copy(hp[:], par[:, i]))
                dve.sem_inc(par_ready, 1)

                def biased(t):
                    rows = TILES[t][1]
                    keys = (t + 1) * P if t < 4 else PAST + TS
                    far = dist[:, TP - keys:TP] if t < 4 else dist_s[0:rows, :]
                    dve.wait_ge(s_ready, i * NT + (t + 1))
                    for m in range(2):
                        a = dve.scalar_tensor_tensor(out=S[0:rows, t % 2, m, 0:keys], in0=far,
                                                     scalar=hp[0:rows, SLOPE8:SLOPE8 + 1],
                                                     in1=bank[2 + m][0:rows, 0:keys], op0=ALU.mult, op1=ALU.add)
                    a.then_inc(s_taken, 1)
                    dve.wait_ge(s_taken, i * NT + (t + 2))
                    step.link(dve.tensor_reduce(mx[0:rows, t % 2], S[0:rows, t % 2, :, 0:keys], AX_X, ALU.max))
                    dve.tensor_scalar(nmx[0:rows, t % 2], mx[0:rows, t % 2], -DK ** -0.5, None,
                                      ALU.mult).then_inc(max_ready, 1)

                def combined(t):
                    rows = TILES[t][1]
                    keys = (t + 1) * P if t < 4 else PAST + TS
                    dve.wait_ge(e_ready, i * NT + (t + 1))
                    r = ri[0:rows, t % 2]
                    step.link(dve.reciprocal(r, rs[0:rows, t % 2]))
                    step.link(dve.tensor_scalar(r[:, 1:2], r[:, 1:2], lam[0:rows, 0:1], None, ALU.mult))
                    s0, s1 = S[0:rows, t % 2, 0, 0:keys], S[0:rows, t % 2, 1, 0:keys]
                    step.link(dve.tensor_scalar(s0, s0, r[:, 0:1], None, ALU.mult))
                    dve.scalar_tensor_tensor(out=s0, in0=s1, scalar=r[:, 1:2], in1=s0, op0=ALU.mult,
                                             op1=ALU.add).then_inc(a_ready, 1)

                def output(t):
                    rows = TILES[t][1]
                    dve.wait_ge(pv_ready, i * NT + (t + 1))
                    dve.tensor_copy(od[:, tile_cols(t)],
                                    bank[5 + t % 2][:, 0:rows]).then_inc(pv_taken, 1)

                biased(0)
                biased(1)
                combined(0)
                biased(2)
                combined(1)
                output(0)
                biased(3)
                combined(2)
                output(1)
                biased(4)
                combined(3)
                output(2)
                combined(4)
                output(3)
                dve.wait_ge(in_taken, i * 14 + 8 + 2)
                dve.tensor_tensor(qs[:, 0:TP].rearrange("p (c n) -> p c n", c=4),
                                  qrT[:, 0:TP].rearrange("p (c n) -> p c n", c=4),
                                  cross_scale[:, i][:, None, :].to_broadcast([P, 4, P]), ALU.mult)
                dve.tensor_tensor(qs[:, TP:T], qrT[:, TP:T], cross_scale[:, i, 0:TS], ALU.mult)
                dve.wait_ge(inner_ready, i + 1)
                dve.tensor_tensor(im[:, 0:TP].rearrange("p (c n) -> p c n", c=4),
                                  bank[2][:].rearrange("p (c n) -> p c n", c=4),
                                  decay[:, i][:, None, :].to_broadcast([P, 4, P]), ALU.mult)
                dve.tensor_tensor(im[0:TS, TP:T], bank[3][0:TS, 0:TS], decay[0:TS, i, 0:TS],
                                  ALU.mult).then_inc(im_ready, 1)
                output(4)
                dve.wait_ge(u_ready, i + 1)
                dve.wait_ge(cache_landed, (i + 1) * 48)
                dve.wait_ge(st_free, i + 1)
                step.link(dve.tensor_copy(st[:, 0], bank[0][:, 0:P]))
                for t in range(1, 4):
                    step.link(dve.scalar_tensor_tensor(out=st[:, t], in0=st[:, t - 1],
                                                       scalar=hp[:, GAMMA_L:GAMMA_L + 1],
                                                       in1=bank[0][:, t * P:(t + 1) * P], op0=ALU.mult, op1=ALU.add))
                dve.scalar_tensor_tensor(out=st[:, 4], in0=st_in[:], scalar=hp[:, GAMMA_LS:GAMMA_LS + 1],
                                         in1=bank[1][:, 0:P], op0=ALU.mult, op1=ALU.add).then_inc(st_ready, 1)
                dve.wait_ge(drms_ready, i * 2 + 1)
                step.link(dve.reciprocal(rmo[:], rmo[:]))
                dve.scalar_tensor_tensor(out=mixedT[:, i], in0=od[:], scalar=hp[:, G_DA:G_DA + 1], in1=rmo[:],
                                         op0=ALU.mult, op1=ALU.mult).then_inc(mixed_ready, 1)
                dve.wait_ge(mean_ready, i + 1)
                for h in range(2):
                    a = dve.scalar_tensor_tensor(out=ro[:, half(h)], in0=bank[6 + h][:, 0:HT], scalar=-1.0 / P,
                                                 in1=ro[:, half(h)], op0=ALU.mult, op1=ALU.add)
                a.then_inc(oc_ready, 1)
                dve.wait_ge(drms_ready, i * 2 + 2)
                step.link(dve.reciprocal(rmo[:], rmo[:]))
                step.link(dve.scalar_tensor_tensor(out=ro[:], in0=ro[:], scalar=hp[:, G_RET:G_RET + 1], in1=rmo[:],
                                                   op0=ALU.mult, op1=ALU.mult))
                dve.tensor_tensor(mixedT[:, HEADS + i], ro[:], grT[:], ALU.mult).then_inc(mixed_ready, 1)

            def residual(done, taken):
                with dve.Fori(0, 2) as i:
                    for b in range(4):
                        for h in range(2):
                            dve.wait_ge(done, i * 8 + (2 * b + h + 1))
                            x = xT[:, i * 4 + b, half(h)]
                            dve.tensor_tensor(x, bank[h][:, 0:HT], x, ALU.add).then_inc(taken, 1)

            residual(wo_done, wo_taken)
            normed(NORM_CROSS, xT, hT, T)

            with dve.Fori(0, HEADS) as i:
                step.restart()

                def xmax(t):
                    rows = TILES[t][1]
                    dve.wait_ge(xs_ready, i * NT + (t + 1))
                    step.link(dve.tensor_reduce(xm[0:rows, t % 2:t % 2 + 1], bank[2 + t % 2][0:rows, 0:MEM],
                                                AX_X, ALU.max))
                    dve.tensor_scalar(xn[0:rows, t % 2:t % 2 + 1], xm[0:rows, t % 2:t % 2 + 1],
                                      -(D // HEADS) ** -0.5, None, ALU.mult).then_inc(xmax_ready, 1)

                def xnorm(t):
                    rows = TILES[t][1]
                    dve.wait_ge(xe_ready, i * NT + (t + 1))
                    r = xr[0:rows, t % 2:t % 2 + 1]
                    step.link(dve.reciprocal(r, r))
                    dve.tensor_scalar(E[0:rows, t % 2], E[0:rows, t % 2], r, None, ALU.mult).then_inc(xp_ready, 1)

                def xoutput(t):
                    rows = TILES[t][1]
                    dve.wait_ge(xpv_ready, i * NT + (t + 1))
                    dve.tensor_scalar(mixedT[:, bass.ds(i * 2, 2), tile_cols(t)],
                                      bank[5 + t % 2][:, 0:2 * P].rearrange("p (b n) -> p b n", b=2)[:, :, 0:rows],
                                      1.0, None, ALU.mult).then_inc(xpv_taken, 1)

                xmax(0)
                xmax(1)
                for t in range(NT):
                    xnorm(t)
                    xoutput(t)
                    if t + 2 < NT:
                        xmax(t + 2)

            residual(xo_done, xo_taken)
            results_stored(dve)
            dve.wait_ge(rms_ready, NORM_FFN + 1)
            step.restart()
            step.link(dve.reciprocal(rms[:], rms[:]))

            def low_half(c):
                dve.wait_ge(hhi_ready, c + 1)
                dve.tensor_tensor(hs[1][:, c], hc[:, c % 2], hs[0][:, c].bitcast(F32),
                                  ALU.subtract).then_inc(h_ready, 1)

            for c in range(C):
                if c >= 2:
                    low_half(c - 2)
                    dve.wait_ge(h_ready, C * NORM_FFN + c - 1)
                dve.scalar_tensor_tensor(out=hc[:, c % 2], in0=xT[:, c], scalar=gains[:, NORM_FFN, c:c + 1],
                                         in1=rms[:], op0=ALU.mult, op1=ALU.mult).then_inc(hc_ready, 1)
            low_half(C - 2)
            low_half(C - 1)

            for x in (v16, i16, c16, p16):
                a = step.link(dve.memset(x[:], 0))

            def top16(vals, idx, src, spare):
                step.link(dve.max(vals[:, 0:8], src))
                step.link(dve.max_index(idx[:, 0:8], vals[:, 0:8], src))
                step.link(dve.match_replace(spare, vals[:, 0:8], src, FLOOR))
                step.link(dve.max(vals[:, 8:16], spare))
                step.link(dve.max_index(idx[:, 8:16], vals[:, 8:16], spare))

            with dve.Fori(0, PH // 2) as i:
                step.restart()
                for j in range(2):
                    dve.wait_ge(sc_taken, i * 2 + (j + 2))
                    dve.sem_inc(passed, 1)
                    mine = sc[:, bass.ds(i * 2 + j, 1)].rearrange("p h s t n -> p (h s) t n")
                    dve.tensor_scalar(scores_now[:, :, 0:4], mine[:, :, 0:4], 1.0, None, ALU.mult)
                    step.link(dve.tensor_scalar(scores_now[0:TS, :, 4], mine[0:TS, :, 4], 1.0, None, ALU.mult))
                    for s in range(2):
                        for t in range(NT):
                            rows = TILES[t][1]
                            top16(v16[0:rows, s, t], i16[0:rows, s, t], scores_now[0:rows, s, t], scr[0:rows, 0:KEYS])
                    for t in range(NT):
                        rows = TILES[t][1]
                        step.link(dve.tensor_tensor(cand[0:rows],
                                                    v16[0:rows, 0, t][:, :, None].to_broadcast([rows, TOPK, TOPK]),
                                                    v16[0:rows, 1, t][:, None, :].to_broadcast([rows, TOPK, TOPK]),
                                                    ALU.add))
                        top16(c16[0:rows, t], p16[0:rows, t], cand[0:rows].rearrange("p a b -> p (a b)"),
                              scr[0:rows, :])
                    p = i * 2 + j
                    dve.tensor_copy(best[:, :, p], c16[:])
                    dve.tensor_copy(pos[:, :, p], p16[:])
                    dve.tensor_copy(key1[:, :, p], i16[:, 0])
                    step.link(dve.tensor_copy(key2[:, :, p], i16[:, 1]))

            with dve.Fori(0, NT) as i:
                step.restart()
                at = pos[:, i].rearrange("p h k -> p (h k)")
                dve.tensor_scalar(rank[:, 0], at, 4, None, ALU.logical_shift_right)
                step.link(dve.tensor_scalar(rank[:, 1], at, TOPK - 1, None, ALU.bitwise_and))
                step.link(dve.tensor_copy(rankf[:], rank[:]))
                for s, key in ((0, key1), (1, key2)):
                    step.link(dve.tensor_tensor(hit[:], rankf[:, s][:, :, None].to_broadcast([P, PH * TOPK, TOPK]),
                                                iota[:, 0:TOPK][:, None, :].to_broadcast([P, PH * TOPK, TOPK]),
                                                ALU.is_equal))
                    h4 = hit[:].rearrange("p (h k) a -> p h k a", h=PH)
                    step.link(dve.tensor_tensor(h4, h4, key[:, i][:, :, None, :].to_broadcast([P, PH, TOPK, TOPK]),
                                                ALU.mult))
                    step.link(dve.tensor_reduce(sel[:, i, s], hit[:], AX_X, ALU.add))
                step.link(dve.tensor_tensor(dif[:], best[:, i],
                                            best[:, i, :, 0:1].to_broadcast([P, PH, TOPK]), ALU.subtract))
                step.link(dve.tensor_copy(best[:, i], dif[:]))
            dve.sem_inc(dif_ready, 1)
            dve.wait_ge(gexp_ready, 1)
            for t in range(NT):
                step.link(dve.tensor_reduce(gsum[:], best[:, t], AX_X, ALU.add))
                step.link(dve.reciprocal(gsum[:], gsum[:]))
                dve.tensor_tensor(sel[:, t, 2].rearrange("p (h k) -> p h k", h=PH), best[:, t],
                                  gsum[:][:, :, None].to_broadcast([P, PH, TOPK]), ALU.mult).then_inc(sel_ready, 1)
                dve.wait_ge(sel_ready, t + 1)

            dve.wait_ge(selT_taken, 1)
            with dve.Fori(0, NCHUNK) as i:
                step.restart()
                for j in range(GROUP):
                    dve.wait_ge(g_ready, (i * GROUP + j) * 2 + 2)
                    tok = bass.ds(i * CTOK + j * TOK8, TOK8)

                    def spread(k):
                        return selT[:, k, tok][:, :, None].to_broadcast([P, TOK8, KEYS])

                    every = iota[:][:, None, :].to_broadcast([P, TOK8, KEYS])
                    step.link(dve.tensor_tensor(hot1[:, j % 2], every, spread(0), ALU.is_equal))
                    dve.tensor_tensor(hot2[:, j % 2], every, spread(1), ALU.is_equal)
                    dve.tensor_tensor(hot1[:, j % 2], hot1[:, j % 2], spread(2), ALU.mult).then_inc(hot_ready, 1)

            def weighted(g, p, turn):
                def low_half(j):
                    dve.wait_ge(whi_ready, g * GROUP + (j + 1))
                    dve.tensor_tensor(wbs[p][1][:, j], wf[:, j % 2], wbs[p][0][:, j].bitcast(F32),
                                      ALU.subtract).then_inc(w_ready, 1)

                dve.wait_ge(ag_landed[p], turn)
                dve.wait_ge(y_ready, g * 16 + 16)
                for j in range(GROUP):
                    if j >= 2:
                        low_half(j - 2)
                        dve.wait_ge(w_ready, g * GROUP + (GROUP + j - 1))
                    elif j == 0:
                        dve.wait_ge(w_ready, g * GROUP + 4)
                    dve.tensor_tensor(wf[:, j % 2].rearrange("p (c t) -> p c t", c=NCHUNK),
                                      aring[p][:, j].rearrange("p (c t) -> p c t", c=NCHUNK),
                                      gring[p][:, :, j * CTOK:(j + 1) * CTOK], ALU.mult).then_inc(wf_ready, 1)
                low_half(GROUP - 2)
                low_half(GROUP - 1)

            def add_products(g):
                for n in range(2 * C):
                    b, h = n // 2, n % 2
                    dve.wait_ge(y_ready, g * 16 + (32 + n + 1))
                    dve.tensor_tensor(xT[:, b, half(h)], bank[n % 8][:, 0:HT], xT[:, b, half(h)],
                                      ALU.add).then_inc(y_taken, 1)

            pairs = KEYS // GROUP // 2
            weighted(0, 0, 32)
            with dve.Fori(0, pairs - 1) as i:
                weighted(i * 2 + 1, 1, (i + 1) * 32)
                add_products(i * 2)
                weighted(i * 2 + 2, 0, (i + 2) * 32)
                add_products(i * 2 + 1)
            weighted(2 * pairs - 1, 1, pairs * 32)
            add_products(2 * pairs - 2)
            add_products(2 * pairs - 1)
            dve.wait_ge(y_taken, 8 + 16 * 2 * pairs)
            normed(NORM_FINAL, xT, yT, T)


def kernel(**inputs):
    import concourse.bacc as _bacc
    from concourse.bass_utils import run_bass_kernel_spmd as _run

    a = {k: np.asarray(v) for k, v in inputs.items()}

    def chunked(w):
        k, n = w.shape
        return w.reshape(k // P, P, n // P, P).transpose(2, 1, 0, 3)

    def features(x):
        return x.T.reshape(-1, P, x.shape[0]).transpose(1, 0, 2)

    x = np.concatenate([a["x_prompt"][0], a["x_sample"][0]], 0)
    w_in = a["w_in"][0].reshape(C, P, NB_IN, HEADS, P).transpose(3, 2, 1, 0, 4)
    w_x = np.stack([chunked(a[n][0]).reshape(HEADS, 2, P, C, P) for n in ("w_xk", "w_xv", "w_xq")], 1)
    host = {
        "x": features(x),
        "mem": features(a["mem_prompt"][0]),
        "gains": np.stack([g.reshape(C, P).T for g in (a["g_mix"][0], a["g_mem"][0], a["g_cross"][0],
                                                       a["g_ffn"][0], a["g_final"])], 1),
        "lam": np.broadcast_to(np.stack([a[n][0] for n in ("lam_q1", "lam_k1", "lam_q2", "lam_k2")]),
                               (P, 4, DK)),
        "w_in": w_in,
        "w_out": chunked(a["w_out"][0]),
        "w_x": w_x.reshape(HEADS, NB_X, P, C, P),
        "w_xo": chunked(a["w_xo"][0]),
        "w_pq": chunked(a["w_pq"][0]).reshape(PH // 2, 4, P, C, P),
        "keys": np.stack([a["peer_k1"][0], a["peer_k2"][0]], 1).transpose(0, 3, 1, 2).reshape(
            PH // 2, 2, P, 2, KEYS),
        "cache_k": a["cache_da_k"][0, 0].reshape(PAST, HEADS, 2 * DK).transpose(1, 2, 0),
        "cache_v": a["cache_da_v"][0, 0].transpose(1, 0, 2),
        "state": a["state_ret"][0, 0],
        "cache_mem_k": a["cache_mem_k"][0, 0].transpose(1, 2, 0).reshape(HEADS, 2, P, MEM).transpose(0, 2, 1, 3),
        "cache_mem_v": a["cache_mem_v"][0, 0].reshape(2, P, HEADS, MEM).transpose(2, 1, 0, 3),
        "u": a["peer_u"][0].reshape(KEYS // GROUP, GROUP, KEYS, C, P).transpose(0, 1, 4, 3, 2),
        "v": a["peer_v"][0].reshape(KEYS // GROUP, GROUP, KEYS, C, P),
    }
    r = np.arange(P)
    far = -np.abs(r[:, None] - (np.arange(TP)[None, :] - (TP - P))).astype(np.float64)
    ahead = (np.arange(TP)[None, :] - (TP - P)) // CHUNK > r[:, None] // CHUNK
    log_g = np.log1p(-(2.0 ** (-5.0 - np.arange(HEADS))))
    gap = r[None, None, :] - r[:, None, None]
    par = np.zeros((P, HEADS, NPAR))
    par[:, :, SLOPE8] = 2.0 ** (-8.0 * np.arange(1, HEADS + 1) / HEADS) * DK ** 0.5
    par[:, :, GAMMA_L] = np.exp(P * log_g)
    par[:, :, GAMMA_LS] = np.exp(TS * log_g)
    par[:, :, TAIL] = np.exp((P - 1 - r)[:, None] * log_g)
    par[:, :, TAIL_S] = np.exp(np.maximum(TS - 1 - r, 0)[:, None] * log_g)
    par = par.astype(np.float32)
    par[:, :, G_DA] = a["g_da"][0].T
    par[:, :, G_RET] = a["g_ret"][0].T
    host.update({
        "ident": np.eye(P), "ones": np.ones((P, P)), "iota": np.broadcast_to(r, (P, P)),
        "eps": np.broadcast_to([EPS, EPS / (1.0 - LAM_INIT) ** 2], (P, 2)),
        "par": par,
        "dist": np.where(ahead, NEG, far),
        "dist_s": -np.abs(PAST + np.arange(TS)[:, None] - np.arange(PAST + TS)[None, :]),
        "decay": np.where(gap >= 0, np.exp(np.maximum(gap, 0) * log_g[None, :, None]), 0.0),
        "cross_scale": np.broadcast_to(np.exp((r + 1) * log_g[:, None]), (P, HEADS, P)),
    })
    outs = {
        "y": (P, C, T), "kd_out": (HEADS, P, T), "vd_out": (HEADS, P, 4, P), "vds_out": (HEADS, TS, P),
        "st_out": (HEADS, 2, P, P), "mk_out": (HEADS, P, 2, MEM), "mv_out": (HEADS, P, 2, MEM),
    }
    scratch = {"act": (KEYS // GROUP, GROUP, P, T), "gates": (NCHUNK, P, KEYS // GROUP, GROUP * CTOK)}

    nc = _bacc.Bacc("TRN2", target_bir_lowering=False, num_devices=1)
    arrays, d = {}, {}
    for name, v in host.items():
        arrays["in_" + name] = np.ascontiguousarray(v, dtype=np.float32)
        d[name] = nc.dram_tensor("in_" + name, arrays["in_" + name].shape, F32, kind="ExternalInput").ap()
    for name, shape in outs.items():
        d[name] = nc.dram_tensor("out_" + name, shape, F32, kind="ExternalOutput").ap()
    for name, shape in scratch.items():
        d[name] = nc.dram_tensor("scratch_" + name, shape, F32, kind="Internal").ap()
    encoder_step(nc, d)
    res = _run(nc, [arrays], core_ids=[0]).results[0]
    o = {name: np.asarray(res["out_" + name]) for name in outs}

    y = o["y"].transpose(2, 1, 0).reshape(T, D)
    kd = o["kd_out"].reshape(HEADS, 2, DK, T).transpose(3, 0, 1, 2)
    vd = o["vd_out"].transpose(2, 1, 0, 3).reshape(TP, HEADS, P)
    mk = o["mk_out"].transpose(3, 0, 2, 1).reshape(MEM, HEADS, 2 * P)
    mv = o["mv_out"].transpose(2, 1, 0, 3).reshape(MEM, HEADS, 2 * P)
    return (y[None, :TP], y[None, TP:], kd[None, None, :TP], vd[None, None], o["st_out"][None, None, :, 0],
            mk[None, None], mv[None, None], kd[None, None, TP:],
            o["vds_out"].transpose(1, 0, 2)[None, None], o["st_out"][None, None, :, 1])
```

```python
from contextlib import ExitStack

import numpy as np

import concourse.bass as bass
from concourse import mybir

ALU = mybir.AluOpType
ACT = mybir.ActivationFunctionType
AX_X = mybir.AxisListType.X
F32 = mybir.dt.float32
F32R = mybir.dt.float32r
BF16 = mybir.dt.bfloat16
U32 = mybir.dt.uint32

P = 128
D = 1024
C = D // P
TP, TS = 512, 32
T = TP + TS
HT = T // 2
TILES = [(0, 128), (128, 128), (256, 128), (384, 128), (512, 32)]
NT = len(TILES)
HEADS = 4
DK = 64
PAST = 128
CHUNK = 64
MEM = 256
PH = 8
KEYS = 128
TOPK = 16
EPS = 1e-6
LAM_INIT = 0.8 - 0.6
NEG = -1e30
FLOOR = -3.0e38

SLOPE8, G_DA, G_RET, GAMMA_L, GAMMA_LS, TAIL, TAIL_S = range(7)
NPAR = 8
QD, KD, VD, QR, KR, VR, GR = range(7)
NB_IN = 7
MK, MV, XQ = 0, 2, 4
NB_X = 6
SLOTS = 7
(U_MK0, U_QR, U_KR, U_MK1, U_VR, U_VRT, U_GR, U_MV, U_KT, U_QD, U_KD, U_VD, U_VDT,
 TURN) = 0, 1, 3, 5, 6, 8, 10, 12, 14, 16, 18, 20, 22, 24
U_FIRST = 8


def block_number(i, b):
    return i * 7 + {QD: 0, KD: 1, VD: 2, KR: 3, QR: 4, VR: 5, GR: 6}[b]


HALF_SLOT = {QD: 0, KD: 1, VD: 0, KR: 1, QR: 0, VR: 0, GR: 1}
N_WO = 7 * HEADS
N_XQ = N_WO + C
N_XO = N_XQ + 2 * HEADS
FRONT = N_XO + C
S_QR, S_MK0, S_KR, S_MK1, S_VR, S_GR, S_MV0 = range(7)
S_MV1, S_QD, S_KD, S_VD = range(4)
RAW_SLOT = {QD: S_QD, KD: S_KD, VD: S_VD, QR: S_QR, KR: S_KR, VR: S_VR, GR: S_GR}
XO_SLOT = [4, 5, 2, 3, 0, 1, 2, 3]
XO_TURN = [HEADS + 5, HEADS + 5] + [2 * HEADS + 3] * 4 + [2 * HEADS + 4] * 2
PQ_TURN = [2 * HEADS + 4, 2 * HEADS + 4, 2 * HEADS + 5, 2 * HEADS + 5]

GROUP = 4
TOK8 = 8
CTOK = GROUP * TOK8
NCHUNK = T // CTOK
U2_GROUPS = NCHUNK
U3_GROUPS = 2
U1_GROUPS = KEYS // GROUP - U2_GROUPS - U3_GROUPS
NPQ = 2 * PH


class Plan:

    def __init__(self, nc, start):
        self.nc, self.end, self.start_of = nc, start, {}

    def place(self, name, shape, dt=F32):
        at = -(-self.end // 32) * 32
        self.start_of[name] = at
        self.end = at + (2 if dt == BF16 else 4) * int(np.prod(shape[1:]))
        return self.nc.alloc_sbuf_tensor_at(name, shape, dt, offset=at)


class Steps:

    def __init__(self, eng, sem):
        self.eng, self.sem, self.here = eng, sem, 0

    def restart(self):
        self.eng.sem_clear(self.sem)
        self.here = 0

    def link(self, ins):
        ins.then_inc(self.sem, 1)
        self.here += 1
        self.eng.wait_ge(self.sem, self.here)


def encoder_step(nc, d):
    with ExitStack() as whole:
        def sem(name):
            return whole.enter_context(nc.semaphore(name))

        plan = Plan(nc, nc.sbuf_base)
        xT = plan.place("xT", [P, C, T])
        sq = plan.place("sq", [P, 2, T])
        sq_sum = plan.place("sq_sum", [P, T])
        rms = plan.place("rms", [P, T])
        ident = plan.place("ident", [P, P])
        ones = plan.place("ones", [P, P])
        eps = plan.place("eps", [P, 2])
        gains = plan.place("gains", [P, 5, C])
        par = plan.place("par", [P, HEADS, NPAR])
        iota = plan.place("iota", [P, P])
        table = plan.place("table", [P, 1])[:]
        lam_in = plan.place("lam_in", [P, 4, DK])
        lam = plan.place("lam", [P, 4])
        wring = plan.place("wring", [P, SLOTS, C, P])
        bank = [whole.enter_context(nc.psum_tensor(f"bank{b}", [P, 512], F32)) for b in range(8)]

        x_landed = [sem(f"x_landed{p}") for p in range(4)]
        const_landed = sem("const_landed")
        w_landed = [sem(f"w_landed{s}") for s in range(SLOTS)]
        sq_ready, sq_used, rms_ready = sem("sq_ready"), sem("sq_used"), sem("rms_ready")
        sums_ready = sem("sums_ready")
        h_ready = sem("h_ready")
        vec, passed = sem("vec_steps"), sem("waits_passed")
        lam_ready = sem("lam_ready")
        out_stored = sem("out_stored")
        in_done, in_taken = sem("in_done"), sem("in_taken")
        cache_landed = sem("cache_landed")
        s_ready, s_taken, max_ready, e_ready = sem("s_ready"), sem("s_taken"), sem("max_ready"), sem("e_ready")
        a_ready, at_ready, at_taken, pv_ready, pv_taken = (
            sem("a_ready"), sem("at_ready"), sem("at_taken"), sem("pv_ready"), sem("pv_taken"))
        par_ready = sem("par_ready")
        dsq_ready, dss_ready, drms_ready, mixed_ready = (
            sem("dsq_ready"), sem("dss_ready"), sem("drms_ready"), sem("mixed_ready"))
        inner_ready, im_ready = sem("inner_ready"), sem("im_ready")
        u_ready, st_ready, ro_ready, ro_copied, mean_ready, oc_ready = (
            sem("u_ready"), sem("st_ready"), sem("ro_ready"), sem("ro_copied"), sem("mean_ready"),
            sem("oc_ready"))
        kd_stored, vd_stored, st_stored = sem("kd_stored"), sem("vd_stored"), sem("st_stored")
        wo_done, wo_taken = sem("wo_done"), sem("wo_taken")
        xo_done, xo_taken = sem("xo_done"), sem("xo_taken")
        mem_landed = sem("mem_landed")
        x_done, x_taken = sem("x_done"), sem("x_taken")
        mk_landed, cmk_landed, mv_landed, cmv_landed = (
            sem("mk_landed"), sem("cmk_landed"), sem("mv_landed"), sem("cmv_landed"))
        xq_ready = sem("xq_ready")
        xs_ready, xmax_ready, xe_ready, xp_ready, xt_ready, xt_taken, xpv_ready, xpv_taken = (
            sem("xs_ready"), sem("xmax_ready"), sem("xe_ready"), sem("xp_ready"), sem("xt_ready"),
            sem("xt_taken"), sem("xpv_ready"), sem("xpv_taken"))
        mk_stored, mv_stored = sem("mk_stored"), sem("mv_stored")
        unit_done, unit_taken = sem("unit_done"), sem("unit_taken")
        hi_ready, lo_ready = sem("hi_ready"), sem("lo_ready")
        hc_ready, hhi_ready = sem("hc_ready"), sem("hhi_ready")
        pk_landed = [sem("pk_landed0"), sem("pk_landed1")]
        sc_ready, sc_taken = sem("sc_ready"), sem("sc_taken")
        dif_ready, gexp_ready, sel_ready, selT_ready, selT_taken = (
            sem("dif_ready"), sem("gexp_ready"), sem("sel_ready"), sem("selT_ready"), sem("selT_taken"))
        act_stored = [sem(f"act_stored{j}") for j in range(GROUP)]
        hot_ready, g_ready, g_taken = sem("hot_ready"), sem("g_ready"), sem("g_taken")
        gate_ready, odd_ready = sem("gate_ready"), sem("odd_ready")
        mixed_high, mixed_low, last_low = sem("mixed_high"), sem("mixed_low"), sem("last_low")
        g_stored = [sem("g_stored0"), sem("g_stored1")]
        wf_ready, whi_ready = sem("wf_ready"), sem("whi_ready")
        ag_landed = [sem("ag_landed0"), sem("ag_landed1")]
        w_ready, y_ready, y_taken = sem("w_ready"), sem("y_ready"), sem("y_taken")

        halves = Plan(nc, plan.end)
        hs = [halves.place(n, [P, C, T], F32R) for n in ("h_hi", "h_lo")]
        us = [halves.place(n, [P, 2, C, P], F32R) for n in ("u_hi", "u_lo")]
        front = Plan(nc, halves.end)

        def fr(name, shape, dt=F32):
            return front.place(name, shape, dt)

        dist = fr("dist", [P, TP])
        dist_s = fr("dist_s", [P, PAST + TS])
        decay = fr("decay", [P, HEADS, P])
        cross_scale = fr("cross_scale", [P, HEADS, P])
        mixedT = fr("mixedT", [P, C, T])
        memT = fr("memT", [P, C, MEM])
        memn = fr("memn", [P, C, MEM])
        hp = fr("hp", [P, NPAR])
        qdT, kdT, qrT, krT, grT = (fr(n, [P, T]) for n in ("qdT", "kdT", "qrT", "krT", "grT"))
        vd, vr, kn = (fr(n, [P, NT, P]) for n in ("vd", "vr", "kn"))
        ck, cv, st_in = fr("ck", [P, PAST]), fr("cv", [P, P]), fr("st_in", [P, P])
        S = fr("S", [P, 2, 2, TP])
        mx, nmx, rs, ri = (fr(n, [P, 2, 2]) for n in ("mx", "nmx", "rs", "ri"))
        aT = fr("aT", [P, TP])
        od = fr("od", [P, T])
        sqo = fr("sqo", [P, T])
        rmo = fr("rmo", [P, T])
        qs = fr("qs", [P, T])
        im = fr("im", [P, TP + TS])
        st = fr("st", [P, NT, P])
        ro = fr("ro", [P, T])
        mkT, mv = fr("mkT", [P, 2, MEM]), fr("mv", [P, 2, MEM])
        cmk, cmv = fr("cmk", [P, 2, MEM]), fr("cmv", [P, 2, MEM])
        xqT = fr("xqT", [P, 2, T])
        E = fr("E", [P, 2, MEM])
        eT = fr("eT", [P, MEM])
        xm, xn, xr = (fr(n, [P, 2]) for n in ("xm", "xn", "xr"))

        vT = xqT[:, 0]
        assert front.end <= 229368

        first = Plan(nc, halves.end)
        actb = first.place("actb", [P, GROUP, T])
        gates_at = first.end
        gate_plan = Plan(nc, gates_at)
        hot2 = gate_plan.place("hot2", [P, 2, TOK8, KEYS], BF16)
        hot1 = gate_plan.place("hot1", [P, 2, TOK8, KEYS], BF16)
        gated = gate_plan.place("gated", [P, 2, 3, TOK8, KEYS], BF16)
        pieces = gate_plan.place("pieces", [P, 3, NT * P], BF16)
        selT = gate_plan.place("selT", [P, 3, NT * P])
        gst = gate_plan.place("gst", [P, 2, KEYS, CTOK])
        sel = gate_plan.place("sel", [P, NT, 3, P])
        ret = Plan(nc, gates_at)
        sc = ret.place("sc", [P, PH, 2, NT, KEYS])
        scores_now = ret.place("scores_now", [P, 2, NT, KEYS])
        pk = ret.place("pk", [P, 2, 2, KEYS])
        qpT = ret.place("qpT", [P, 2, T])
        hit = ret.place("hit", [P, PH * TOPK, TOPK])
        assert ret.end <= gate_plan.start_of["sel"]
        ret.end = max(ret.end, gate_plan.end)
        scr = ret.place("scr", [P, TOPK * TOPK])
        cand = ret.place("cand", [P, TOPK, TOPK])
        v16 = ret.place("v16", [P, 2, NT, TOPK])
        i16 = ret.place("i16", [P, 2, NT, TOPK], U32)
        c16 = ret.place("c16", [P, NT, TOPK])
        p16 = ret.place("p16", [P, NT, TOPK], U32)
        best = ret.place("best", [P, NT, PH, TOPK])
        pos = ret.place("pos", [P, NT, PH, TOPK], U32)
        key1 = ret.place("key1", [P, NT, PH, TOPK])
        key2 = ret.place("key2", [P, NT, PH, TOPK])
        rank = ret.place("rank", [P, 2, PH * TOPK], U32)
        rankf = ret.place("rankf", [P, 2, PH * TOPK])
        dif = ret.place("dif", [P, PH, TOPK])
        gsum = ret.place("gsum", [P, PH])

        over_first, over_gates = Plan(nc, plan.end), Plan(nc, gates_at)
        over_ret = Plan(nc, gate_plan.start_of["sel"])
        vs = [[pl.place(f"v_{n}{p}", [P, GROUP, D], F32R) for n in ("hi", "lo")]
              for p, pl in ((0, over_gates), (1, over_first))]
        wbs = [[pl.place(f"w_{n}{p}", [P, GROUP, T], F32R) for n in ("hi", "lo")]
               for p, pl in ((0, over_gates), (1, over_first))]
        aring = [over_ret.place("a0", [P, GROUP, T]), over_first.place("a1", [P, GROUP, T])]
        gring = [over_ret.place(f"g{p}", [P, NCHUNK, GROUP * CTOK]) for p in range(2)]
        wf = over_gates.place("wf", [P, 2, T])
        assert over_first.end <= gates_at and over_gates.end <= gate_plan.start_of["sel"]
        yT = Plan(nc, plan.end).place("yT", [P, C, T])

        block = whole.enter_context(nc.Block())

        def half(h):
            return slice(h * HT, (h + 1) * HT)

        def tile_cols(t):
            return slice(TILES[t][0], TILES[t][0] + TILES[t][1])

        CONSTS = [(ident, "ident"), (ones, "ones"), (eps, "eps"), (gains, "gains"), (par, "par"),
                  (iota, "iota"), (lam_in, "lam"), (dist, "dist"), (decay, "decay"),
                  (cross_scale, "cross_scale")]
        NCONST = 16 * (len(CONSTS) + 1)
        NORM_MIX, NORM_MEM, NORM_CROSS, NORM_FFN, NORM_FINAL = range(5)

        MIXED_EARLY = [c for c in range(C) if c % HEADS < HEADS - 1]
        MIXED_LAST = [HEADS - 1, 2 * HEADS - 1]
        CROSS_EARLY, CROSS_LAST = list(range(2 * (HEADS - 1))), [2 * HEADS - 2, 2 * HEADS - 1]

        def made(i, u):
            return i * TURN + (U_FIRST + u + 1)

        def room(i, u):
            return i * TURN + (U_FIRST + u + 1)

        def in_sbuf(i, u):
            return i * TURN + (U_FIRST + u + 3)


        def results_stored(eng):
            eng.wait_ge(kd_stored, 16 + 16 * HEADS)
            eng.wait_ge(vd_stored, 32 + 32 * HEADS)
            eng.wait_ge(st_stored, 32 + 32 * HEADS)
            eng.wait_ge(mk_stored, 16 + 16 * HEADS)
            eng.wait_ge(mv_stored, 16 + 16 * HEADS)

        @block.sync
        def _(sp):
            for s in (*act_stored, *g_stored, kd_stored, mk_stored, mv_stored):
                sp.sem_inc(s, 16)
            for s in (vd_stored, st_stored):
                sp.sem_inc(s, 32)
            for q in range(4):
                sp.dma_start(xT[:, 2 * q:2 * q + 2], d["x"][:, 2 * q:2 * q + 2]).then_inc(x_landed[q], 16)
            for tile, name in CONSTS:
                sp.dma_start(tile[:], d[name]).then_inc(const_landed, 16)
            sp.dma_start(dist_s[0:TS, :], d["dist_s"]).then_inc(const_landed, 16)

            def weights(slot, src):
                sp.dma_start(wring[:, slot], src).then_inc(w_landed[slot], 16)

            def turn_weights(h, b, slot):
                weights(slot, d["w_in"][h, b])

            for b, slot in ((QD, S_QD), (KD, S_KD), (VD, S_VD)):
                turn_weights(0, b, slot)
            sp.dma_start(memT[:], d["mem"]).then_inc(mem_landed, 16)
            turn_weights(0, QR, S_QR)
            turn_weights(0, VR, S_VR)
            turn_weights(0, GR, S_GR)
            weights(S_MV0, d["w_x"][0, MV])

            def head_cache(h):
                sp.dma_start(ck[:], d["cache_k"][h]).then_inc(cache_landed, 16)
                sp.dma_start(cv[:], d["cache_v"][h]).then_inc(cache_landed, 16)
                sp.dma_start(st_in[:], d["state"][h]).then_inc(cache_landed, 16)

            head_cache(0)
            def after(s, n):
                sp.wait_ge(s, n)
                sp.sem_inc(passed, 1)

            def store_differential(h, keys, values):
                after(in_taken, keys)
                sp.dma_start(d["kd_out"][h], kdT[:]).then_inc(kd_stored, 16)
                after(in_taken, values)
                sp.dma_start(d["vd_out"][h], vd[:, 0:4]).then_inc(vd_stored, 16)
                sp.dma_start(d["vds_out"][h], vd[0:TS, 4]).then_inc(vd_stored, 16)

            def store_memory_keys(i):
                after(in_taken, in_sbuf(i, U_MK1))
                sp.dma_start(d["mk_out"][i], mkT[:]).then_inc(mk_stored, 16)

            def store_memory_values(i):
                after(in_taken, in_sbuf(i, U_MV + 1))
                sp.dma_start(d["mv_out"][i], mv[:]).then_inc(mv_stored, 16)

            def store_states(i):
                after(st_ready, i + 1)
                sp.dma_start(d["st_out"][i, 0], st[:, 3]).then_inc(st_stored, 16)
                sp.dma_start(d["st_out"][i, 1], st[:, 4]).then_inc(st_stored, 16)

            def split(n):
                after(lo_ready, n + 1)

            split(block_number(0, QD))
            weights(S_MK0, d["w_x"][0, MK])
            split(block_number(0, KD))
            turn_weights(0, KR, S_KR)
            split(block_number(0, VD))
            weights(S_MK1, d["w_x"][0, MK + 1])
            store_differential(0, 2 + 4, 2 + 8)
            with sp.Fori(0, HEADS - 1) as i:
                split(block_number(i, KR))
                turn_weights(i + 1, KD, S_KD)
                split(block_number(i, QR))
                weights(S_MV1, d["w_x"][i, MV + 1])
                after(in_done, made(i, U_MK0))
                turn_weights(i + 1, QD, S_QD)
                split(block_number(i, VR))
                turn_weights(i + 1, VR, S_VR)
                split(block_number(i, GR))
                turn_weights(i + 1, GR, S_GR)
                after(in_done, made(i, U_MK1))
                turn_weights(i + 1, VD, S_VD)
                store_memory_keys(i)
                split(block_number(i + 1, QD))
                weights(S_MK0, d["w_x"][i + 1, MK])
                split(block_number(i + 1, KD))
                turn_weights(i + 1, KR, S_KR)
                after(in_done, made(i, U_MV))
                weights(S_MV0, d["w_x"][i + 1, MV])
                after(in_done, made(i, U_MV + 1))
                turn_weights(i + 1, QR, S_QR)
                store_memory_values(i)
                split(block_number(i + 1, VD))
                weights(S_MK1, d["w_x"][i + 1, MK + 1])
                store_states(i)
                after(ro_ready, i + 1)
                head_cache(i + 1)
                store_differential(i + 1, in_sbuf(i, U_KD + 1), in_sbuf(i, U_VDT + 1))
            last = HEADS - 1
            split(block_number(last, QR))
            weights(S_MV1, d["w_x"][last, MV + 1])
            split(block_number(last, KR))
            weights(2, d["w_out"][1])
            sp.wait_ge(in_done, made(last, U_MK0))
            weights(1, d["w_out"][0])
            sp.wait_ge(in_done, made(last, U_MK1))
            weights(3, d["w_out"][2])
            store_memory_keys(last)
            sp.wait_ge(in_done, made(last, U_MV + 1))
            weights(0, d["w_out"][3])
            store_memory_values(last)

            def query_weights(h, b):
                weights(XQ + b, d["w_x"][h, XQ + b])

            split(block_number(last, VR))
            query_weights(0, 0)
            split(block_number(last, GR))
            query_weights(0, 1)

            def memory_keys(h):
                sp.dma_start(mkT[:], d["mk_out"][h]).then_inc(mk_landed, 16)

            def cached_keys(h):
                sp.dma_start(cmk[:], d["cache_mem_k"][h]).then_inc(cmk_landed, 16)

            def memory_values(h):
                sp.dma_start(mv[:], d["mv_out"][h]).then_inc(mv_landed, 16)

            def cached_values(h):
                sp.dma_start(cmv[:], d["cache_mem_v"][h]).then_inc(cmv_landed, 16)

            store_states(last)
            sp.wait_ge(mk_stored, 16 + 16 * HEADS)
            sp.wait_ge(mv_stored, 16 + 16 * HEADS)
            memory_keys(0)
            cached_keys(0)
            memory_values(0)
            cached_values(0)
            for b in range(4):
                split(N_WO + b)
                weights((b + 1) % 4, d["w_out"][4 + b])
            for b in range(2):
                split(N_XQ + b)
                query_weights(1, b)
            for b, held in ((5, 4), (2, 5), (3, 6), (4, 7)):
                split(N_WO + held)
                weights(XO_SLOT[b], d["w_xo"][b])

            def next_memory(i, block):
                split(N_XQ + (i * 2 + 2))
                block(0)
                after(xs_ready, i * NT + 4)
                memory_keys(i + 1)
                after(xs_ready, i * NT + 5)
                cached_keys(i + 1)
                split(N_XQ + (i * 2 + 3))
                block(1)
                after(xpv_ready, i * NT + 4)
                memory_values(i + 1)
                after(xpv_ready, i * NT + 5)
                cached_values(i + 1)

            with sp.Fori(0, HEADS - 2) as i:
                next_memory(i, lambda b: query_weights(i + 2, b))
            next_memory(HEADS - 2, lambda b: weights(XO_SLOT[b], d["w_xo"][b]))
            for b in (6, 7):
                split(N_XO + b - 4)
                weights(XO_SLOT[b], d["w_xo"][b])

            for b in range(4):
                split(N_XO + 4 + b)
                weights(b, d["w_pq"][0, b])

            def load_keys(slot, src):
                sp.dma_start(pk[:, slot], src).then_inc(pk_landed[slot], 16)

            sp.wait_ge(h_ready, C * (NORM_FFN + 1))
            sp.wait_ge(odd_ready, 3 * C // 2)
            results_stored(sp)
            for j in range(2):
                load_keys(j, d["keys"][0, j])
            with sp.Fori(0, PH // 2 - 1) as i:
                for j in range(2):
                    for s in range(2):
                        b = 2 * j + s
                        sp.wait_ge(lo_ready, i * 4 + (FRONT + b + 1))
                        weights(b, d["w_pq"][i + 1, b])
                    sp.wait_ge(sc_ready, i * 2 + j + 1)
                    load_keys(j, d["keys"][i + 1, j])
            for b in range(4):
                sp.wait_ge(lo_ready, FRONT + NPQ - 4 + b + 1)
                weights(b, d["u"][0, b])

            def first_group(g, table, nxt):
                for j in range(GROUP):
                    sp.wait_ge(lo_ready, g * GROUP + (FRONT + NPQ + j + 1))
                    weights(j, table[nxt, j])
                    sp.wait_ge(unit_taken, (g * GROUP + j) * 2 + (4 + 2 * NPQ + 2))
                    sp.dma_start(d["act"][g, j], actb[:, j]).then_inc(act_stored[j], 16)

            def chunk_gates(c, p):
                sp.wait_ge(g_taken, c * 8 + 10)
                sp.sem_inc(passed, 1)
                sp.dma_start(d["gates"][c].rearrange("p g k -> p (g k)"),
                             gst[:, p].rearrange("p k t -> p (k t)")).then_inc(g_stored[p], 16)

            with sp.Fori(0, U1_GROUPS) as i:
                first_group(i, d["u"], i + 1)
            with sp.Fori(0, NCHUNK // 2) as i:
                for p in range(2):
                    first_group(i * 2 + (U1_GROUPS + p), d["u"], i * 2 + (U1_GROUPS + p + 1))
                    chunk_gates(i * 2 + p, p)
            first_group(U1_GROUPS + NCHUNK - 1, d["u"], U1_GROUPS + NCHUNK)
            chunk_gates(NCHUNK - 1, 0)
            for j in range(GROUP):
                sp.wait_ge(lo_ready, FRONT + NPQ + KEYS - 2 * GROUP + j + 1)
                weights(j, d["u"][KEYS // GROUP - 1, j])

            def store_activations(g):
                for j in range(GROUP):
                    sp.wait_ge(unit_taken, 4 + 2 * (NPQ + g * GROUP + j + 1))
                    sp.dma_start(d["act"][g, j], actb[:, j]).then_inc(act_stored[j], 16)

            def load_group(g, p):
                sp.dma_start(aring[p][:], d["act"][g].rearrange("j p t -> p j t")).then_inc(ag_landed[p], 16)
                sp.dma_start(gring[p][:], d["gates"][:, :, g].rearrange("c p k -> p c k")).then_inc(ag_landed[p], 16)

            sp.wait_ge(g_stored[0], 16 + 16 * ((NCHUNK + 1) // 2))
            sp.wait_ge(g_stored[1], 16 + 16 * (NCHUNK // 2))
            for j in range(GROUP):
                sp.wait_ge(act_stored[j], 32)
            load_group(0, 0)
            store_activations(KEYS // GROUP - 2)
            for j in range(GROUP):
                sp.wait_ge(lo_ready, FRONT + NPQ + KEYS - GROUP + j + 1)
                weights(j, d["v"][0, j])
            store_activations(KEYS // GROUP - 1)
            for j in range(GROUP):
                sp.wait_ge(act_stored[j], 16 + 16 * (KEYS // GROUP))
            vb = FRONT + NPQ + KEYS

            def second_tiles(g, nxt):
                for j in range(GROUP):
                    sp.wait_ge(lo_ready, g * GROUP + (vb + j + 1))
                    sp.sem_inc(passed, 1)
                    weights(j, d["v"][nxt, j])

            def reload_group(used, g, p):
                sp.wait_ge(wf_ready, used * GROUP)
                sp.sem_inc(passed, 1)
                load_group(g, p)

            second_tiles(0, 1)
            sp.wait_ge(unit_done, 4 + 2 * (NPQ + KEYS))
            load_group(1, 1)
            reload_group(1, 2, 0)
            with sp.Fori(0, KEYS // GROUP // 2 - 2) as i:
                second_tiles(i * 2 + 1, i * 2 + 2)
                reload_group(i * 2 + 2, i * 2 + 3, 1)
                second_tiles(i * 2 + 2, i * 2 + 3)
                reload_group(i * 2 + 3, i * 2 + 4, 0)
            last = KEYS // GROUP - 1
            second_tiles(last - 2, last - 1)
            reload_group(last - 1, last, 1)
            second_tiles(last - 1, last)

            for c in range(0, C, 2):
                sp.wait_ge(h_ready, C * NORM_FINAL + c + 2)
                sp.dma_start(d["y"][:, c:c + 2], yT[:, c:c + 2]).then_inc(out_stored, 16)
            sp.wait_ge(out_stored, 16 * C // 2)
            results_stored(sp)

        @block.gpsimd
        def _(pool):
            def low(n, slot, dst, hi):
                pool.wait_ge(hi_ready, n + 1)
                pool.tensor_tensor(dst, wring[:, slot], hi.bitcast(F32), ALU.subtract).then_inc(lo_ready, 1)

            def low_block(n, raw, slot):
                low(n, raw, us[1][:, slot], us[0][:, slot])

            def low_odd(before):
                for c in range(1, C, 2):
                    pool.wait_ge(hhi_ready, C * before + c + 1)
                    pool.tensor_tensor(hs[1][:, c], mixedT[:, c], hs[0][:, c].bitcast(F32),
                                       ALU.subtract).then_inc(odd_ready, 1)

            def low_mixed(first, chunks):
                for k, c in enumerate(chunks):
                    pool.wait_ge(mixed_high, first + k + 1)
                    pool.tensor_tensor(hs[1][:, c], mixedT[:, c], hs[0][:, c].bitcast(F32),
                                       ALU.subtract).then_inc(mixed_low, 1)

            def of_head(i, b):
                low_block(block_number(i, b), RAW_SLOT[b], HALF_SLOT[b])

            for b in (QD, KD, VD, KR, QR):
                of_head(0, b)
                if b == QD:
                    low_odd(0)
            with pool.Fori(0, HEADS - 1) as i:
                of_head(i, VR)
                of_head(i, GR)
                for b in (QD, KD, VD, KR, QR):
                    of_head(i + 1, b)
            of_head(HEADS - 1, VR)
            of_head(HEADS - 1, GR)
            for b in range(C):
                low_block(N_WO + b, (b + 1) % 4, b % 2)
                if b == 1:
                    low_mixed(0, MIXED_EARLY)
            low_block(N_XQ, XQ, 0)
            low_odd(1)
            low_block(N_XQ + 1, XQ + 1, 1)
            with pool.Fori(0, HEADS) as i:
                for b in range(2):
                    low_block(i * 2 + (N_XQ + 2 + b), XQ + b, b)
            low_mixed(C, CROSS_EARLY)
            for b in range(2, C):
                low_block(N_XO + b, XO_SLOT[b], b % 2)
            for j in range(4):
                low_block(FRONT + j, j, j % 2)
                if j == 0:
                    low_odd(2)
            with pool.Fori(0, (NPQ + KEYS) // 4 - 1) as i:
                for j in range(4):
                    low_block(i * 4 + (FRONT + 4 + j), j, j % 2)
            for p in range(2):
                pool.wait_ge(g_stored[p], 16 + 16 * ((NCHUNK + 1 - p) // 2))
            with pool.Fori(0, KEYS // GROUP // 2) as i:
                for p in range(2):
                    for j in range(GROUP):
                        low(i * 8 + (FRONT + NPQ + KEYS + 4 * p + j), j,
                            vs[p][1][:, j].rearrange("p (c n) -> p c n", c=C),
                            vs[p][0][:, j].rearrange("p (c n) -> p c n", c=C))

        @block.tensor
        def _(pe):
            def norm_sums(k, n):
                pe.wait_ge(sq_used, C * (k + 1) + 2)
                if k:
                    pe.wait_ge(rms_ready, k)
                if n == T:
                    pe.matmul(bank[6][:, 0:HT], ones[:], sq_sum[:, 0:HT], start=True, stop=True)
                    m = pe.matmul(bank[7][:, 0:HT], ones[:], sq_sum[:, HT:T], start=True, stop=True)
                else:
                    m = pe.matmul(bank[6][:, 0:n], ones[:], sq_sum[:, 0:n], start=True, stop=True)
                m.then_inc(sums_ready, 1)

            pe.sem_inc(g_ready, 4)
            pe.sem_inc(y_ready, 32)
            pe.sem_inc(unit_done, 4)
            pe.wait_ge(const_landed, NCONST)
            norm_sums(NORM_MIX, T)

            def passes(out, whi, wlo, xhi, xlo, first, last):
                pe.matmul(out, whi, xhi, start=first, stop=False)
                pe.matmul(out, whi, xlo, start=False, stop=False)
                return pe.matmul(out, wlo, xhi, start=False, stop=last)

            def chunk_normed(k, before, c):
                if c % 2:
                    pe.wait_ge(odd_ready, C // 2 * before + (c + 1) // 2)
                else:
                    pe.wait_ge(h_ready, C * k + c + 2)

            def halves_ready(n):
                pe.wait_ge(hi_ready, n + 1)
                pe.wait_ge(lo_ready, n + 1)

            def product(out, slot, c, h, first, last):
                return passes(out, us[0][:, slot, c], us[1][:, slot, c], hs[0][:, c, half(h)],
                              hs[1][:, c, half(h)], first, last)

            def as_normed(outs, slot, k, before, done):
                for c in range(C):
                    chunk_normed(k, before, c)
                    for h in range(2):
                        m = product(outs[h][:, 0:HT], slot, c, h, c == 0, c == C - 1)
                        if c == C - 1:
                            m.then_inc(done, 1)

            def project(i, b, free, first=0):
                halves_ready(block_number(i, b))
                for h in range(2):
                    pe.wait_ge(in_taken, free + h)
                    for c in range(C):
                        m = product(bank[(first + h) % 2][:, 0:HT], HALF_SLOT[b], c, h, c == 0, c == C - 1)
                    m.then_inc(in_done, 1)

            def turn_values(taken, free):
                pe.wait_ge(in_taken, taken)
                pe.wait_ge(in_taken, free)
                for t in range(NT):
                    rows = TILES[t][1]
                    out = bank[0][:, t * P:(t + 1) * P] if t < 4 else bank[1][0:rows, 0:P]
                    m = pe.transpose(out, vT[:, tile_cols(t)], ident[:])
                m.then_inc(in_done, 2)

            def memory_keys(i, u, slot):
                pe.wait_ge(w_landed[slot], i * 32 + 32)
                pe.wait_ge(in_taken, room(i, u))
                for c in range(C):
                    m = pe.matmul(bank[u % 2][:, 0:MEM], wring[:, slot, c], memn[:, c], start=c == 0, stop=c == C - 1)
                m.then_inc(in_done, 1)

            def memory_values(i, b, slot, turn):
                pe.wait_ge(w_landed[slot], turn)
                pe.wait_ge(in_taken, room(i, U_MV + b))
                for mt in range(2):
                    for c in range(C):
                        m = pe.matmul(bank[b][:, mt * P:(mt + 1) * P], memn[:, c, mt * P:(mt + 1) * P],
                                      wring[:, slot, c], start=c == 0, stop=c == C - 1)
                m.then_inc(in_done, 1)

            def scores(i, t):
                q0, rows = TILES[t]
                pe.wait_ge(s_taken, i * NT + t + 1)
                if t == 4:
                    pe.wait_ge(cache_landed, (i + 1) * 48)
                    pe.sem_inc(passed, 1)
                for m_ in range(2):
                    ps = slice(DK * m_, DK * m_ + DK)
                    lhs = qdT[ps, q0:q0 + rows]
                    if t < 4:
                        m = pe.matmul(bank[2 + m_][0:rows, 0:q0 + rows], lhs, kdT[ps, 0:q0 + rows],
                                      start=True, stop=True)
                    else:
                        pe.matmul(bank[2 + m_][0:rows, 0:PAST], lhs, ck[ps, :], start=True, stop=True)
                        m = pe.matmul(bank[2 + m_][0:rows, PAST:PAST + TS], lhs, kdT[ps, q0:q0 + rows],
                                      start=True, stop=True)
                m.then_inc(s_ready, 1)

            def turn(i, t):
                rows = TILES[t][1]
                pe.wait_ge(a_ready, i * NT + t + 1)
                pe.wait_ge(at_taken, i * NT + t + 1)
                if t == 4:
                    pe.sem_inc(passed, 1)
                if t < 4:
                    for k in range(t + 1):
                        m = pe.transpose(bank[4][:, k * P:(k + 1) * P], S[:, t % 2, 0, k * P:(k + 1) * P], ident[:])
                else:
                    pe.transpose(bank[4][:, 0:rows], S[0:rows, 0, 0, 0:PAST], ident[0:rows, 0:rows])
                    m = pe.transpose(bank[4][0:TS, P:P + rows], S[0:rows, 0, 0, PAST:PAST + TS],
                                     ident[0:rows, 0:rows])
                m.then_inc(at_ready, 1)

            def values(i, t):
                rows = TILES[t][1]
                pe.wait_ge(at_taken, i * NT + t + 2)
                pe.wait_ge(pv_taken, i * NT + t + 1)
                o = bank[5 + t % 2][:, 0:rows]
                if t < 4:
                    for k in range(t + 1):
                        m = pe.matmul(o, vd[:, k], aT[:, k * P:(k + 1) * P], start=k == 0, stop=k == t)
                else:
                    pe.matmul(o, cv[:], aT[:, 0:rows], start=True, stop=False)
                    m = pe.matmul(o, vd[0:TS, 4], aT[0:TS, P:P + rows], start=False, stop=True)
                m.then_inc(pv_ready, 1)

            def sums(src, ready_sem, value, done):
                pe.wait_ge(ready_sem, value)
                pe.matmul(bank[6][:, 0:HT], ones[:], src[:, 0:HT], start=True, stop=True)
                pe.matmul(bank[7][:, 0:HT], ones[:], src[:, HT:T], start=True, stop=True).then_inc(done, 1)

            def mixer_turn(i, last):
                pe.wait_ge(in_taken, in_sbuf(i, -5))
                pe.wait_ge(ro_copied, i + 1)
                scores(i, 0)
                memory_keys(i, U_MK0, S_MK0)
                project(i, QR, room(i, U_QR), first=U_QR)
                scores(i, 1)
                turn(i, 0)
                project(i, KR, room(i, U_KR), first=U_KR)
                scores(i, 2)
                values(i, 0)
                memory_keys(i, U_MK1, S_MK1)
                turn(i, 1)
                project(i, VR, room(i, U_VR))
                scores(i, 3)
                values(i, 1)
                turn(i, 2)
                turn_values(in_sbuf(i, U_VR + 1), room(i, U_VRT + 1))
                project(i, GR, room(i, U_GR))
                scores(i, 4)
                values(i, 2)
                memory_values(i, 0, S_MV0, i * 16 + 16)
                turn(i, 3)
                values(i, 3)
                memory_values(i, 1, S_MV1, i * 32 + 32)
                turn(i, 4)
                pe.wait_ge(in_taken, room(i, U_KT + 1))
                for t in range(NT):
                    rows = TILES[t][1]
                    out = bank[0][:, t * P:(t + 1) * P] if t < 4 else bank[1][0:rows, 0:P]
                    m = pe.transpose(out, krT[:, tile_cols(t)], ident[:])
                m.then_inc(in_done, 2)
                pe.wait_ge(s_taken, i * NT + 5 + 1)
                for t in range(NT):
                    rows = TILES[t][1]
                    out = bank[2][:, t * P:(t + 1) * P] if t < 4 else bank[3][0:rows, 0:rows]
                    m = pe.matmul(out, krT[:, tile_cols(t)], qrT[:, tile_cols(t)], start=True, stop=True)
                m.then_inc(inner_ready, 1)
                values(i, 4)
                pe.wait_ge(in_taken, in_sbuf(i, U_KT + 1))
                pe.wait_ge(drms_ready, i * 2 + 1)
                for t in range(NT):
                    rows = TILES[t][1]
                    out = bank[4][:, t * P:(t + 1) * P] if t < 4 else bank[7][:, 0:P]
                    m = pe.matmul(out, kn[0:rows, t], vr[0:rows, t], start=True, stop=True)
                m.then_inc(u_ready, 1)
                if not last:
                    project(i + 1, QD, room(i, U_QD))
                else:
                    begin_output(0)
                pe.wait_ge(st_ready, i + 1)
                sums(sqo, dsq_ready, i * 2 + 1, dss_ready)
                pe.wait_ge(im_ready, i + 1)
                for t in range(NT):
                    q0, rows = TILES[t]
                    out = bank[2][:, q0:q0 + rows] if t < 4 else bank[3][:, 0:rows]
                    m = pe.matmul(out, vr[0:rows, t], im[0:rows, q0:q0 + rows], start=True, stop=t == 0)
                    if t:
                        before = st[:, t - 1] if t < 4 else st_in[:]
                        m = pe.matmul(out, before, qs[:, q0:q0 + rows], start=False, stop=True)
                m.then_inc(ro_ready, 1)
                if not last:
                    project(i + 1, KD, room(i, U_KD))
                else:
                    begin_output(1)
                pe.wait_ge(drms_ready, i * 2 + 2)
                sums(ro, ro_copied, i + 2, mean_ready)
                if not last:
                    project(i + 1, VD, room(i, U_VD))
                pe.wait_ge(oc_ready, i + 1)
                sums(sqo, dsq_ready, i * 2 + 2, dss_ready)
                if not last:
                    turn_values(in_sbuf(i, U_VD + 1), room(i, U_VDT + 1))

            halves_ready(block_number(0, QD))
            pe.wait_ge(in_taken, 2)
            as_normed(bank[0:2], HALF_SLOT[QD], NORM_MIX, 0, in_done)
            project(0, KD, 3)
            norm_sums(NORM_MEM, MEM)
            project(0, VD, 5)
            turn_values(2 + 6, 8)
            pe.wait_ge(h_ready, 2 * C)

            def output_unit(n, taken, done, b, slot, h, chunks, last_ready):
                halves_ready(b + n)
                pe.wait_ge(taken, b * 2 + (h + 1))
                for c in chunks:
                    if c in last_ready:
                        pe.wait_ge(last_low, last_ready[c])
                    m = product(bank[h][:, 0:HT], slot, c, h, c == 0, c == C - 1)
                if C - 1 in chunks:
                    m.then_inc(done, 1)

            def output_projection(n, taken, done, begun, last_ready):
                for b in range(2):
                    for h in range(2):
                        chunks = [c for c in range(C) if b or c not in begun]
                        output_unit(n, taken, done, b, b, h, chunks, last_ready)
                with pe.Fori(0, C // 2 - 1) as i:
                    for slot in range(2):
                        for h in range(2):
                            output_unit(n, taken, done, i * 2 + (2 + slot), slot, h, range(C), {})

            MIXED_READY = {c: k + 1 for k, c in enumerate(MIXED_LAST)}
            CROSS_READY = {c: k + 3 for k, c in enumerate(CROSS_LAST)}

            def begin_output(h):
                pe.wait_ge(mixed_low, len(MIXED_EARLY))
                output_unit(N_WO, wo_taken, wo_done, 0, 0, h, MIXED_EARLY, {})

            with pe.Fori(0, HEADS - 1) as i:
                mixer_turn(i, False)
            mixer_turn(HEADS - 1, True)

            output_projection(N_WO, wo_taken, wo_done, MIXED_EARLY, MIXED_READY)
            norm_sums(NORM_CROSS, T)

            def query_unit(turn, k):
                b, h = k // 2, k % 2
                halves_ready(N_XQ + (turn * 2 + b))
                pe.wait_ge(x_taken, turn * 4 + (k + 1))
                for c in range(C):
                    m = product(bank[h][:, 0:HT], b, c, h, c == 0, c == C - 1)
                m.then_inc(x_done, 1)

            def begin_cross_output(h):
                pe.wait_ge(mixed_low, len(MIXED_EARLY) + len(CROSS_EARLY))
                output_unit(N_XO, xo_taken, xo_done, 0, 0, h, CROSS_EARLY, {})

            def cross_head(i, last):
                def xscores(t):
                    rows = TILES[t][1]
                    if t >= 2:
                        pe.wait_ge(xe_ready, i * NT + t)
                    if t == 0:
                        pe.wait_ge(mk_landed, i * 16 + 16)
                    if t == 4:
                        pe.wait_ge(cmk_landed, i * 16 + 16)
                    src = mkT if t < 4 else cmk
                    for c in range(2):
                        m = pe.matmul(bank[2 + t % 2][0:rows, 0:MEM], xqT[:, c, tile_cols(t)], src[:, c],
                                      start=c == 0, stop=c == 1)
                    m.then_inc(xs_ready, 1)

                def xturn(t):
                    rows = TILES[t][1]
                    pe.wait_ge(xp_ready, i * NT + t + 1)
                    pe.wait_ge(xt_taken, i * NT + t + 1)
                    if t == 4:
                        pe.sem_inc(passed, 1)
                    for k in range(2):
                        m = pe.transpose(bank[4][:, k * P:k * P + rows], E[0:rows, t % 2, k * P:(k + 1) * P],
                                         ident[0:rows, 0:rows])
                    m.then_inc(xt_ready, 1)

                def xvalues(t):
                    rows = TILES[t][1]
                    pe.wait_ge(xt_taken, i * NT + t + 2)
                    pe.wait_ge(xpv_taken, i * NT + t + 1)
                    if t == 0:
                        pe.wait_ge(mv_landed, i * 16 + 16)
                    if t == 4:
                        pe.wait_ge(cmv_landed, i * 16 + 16)
                        pe.sem_inc(passed, 1)
                    src = mv if t < 4 else cmv
                    for b in range(2):
                        o = bank[5 + t % 2][:, b * P:b * P + rows]
                        for k in range(2):
                            m = pe.matmul(o, src[:, k, b * P:(b + 1) * P], eT[:, k * P:k * P + rows],
                                          start=k == 0, stop=k == 1)
                    m.then_inc(xpv_ready, 1)

                def next_queries(k):
                    if not last:
                        query_unit(i + 1, k)
                    elif k >= 2:
                        begin_cross_output(k - 2)

                pe.wait_ge(xq_ready, i + 1)
                pe.wait_ge(xe_ready, i * NT + 1)
                xscores(0)
                xscores(1)
                next_queries(0)
                for t in range(NT):
                    xturn(t)
                    if t + 2 < NT:
                        xscores(t + 2)
                    if t == 0:
                        next_queries(1)
                    xvalues(t)
                    if t == 1:
                        next_queries(2)
                    if t == 2:
                        next_queries(3)

            halves_ready(N_XQ)
            pe.wait_ge(x_taken, 2)
            as_normed(bank[0:2], 0, NORM_CROSS, 1, x_done)
            for k in range(2, 4):
                query_unit(0, k)
            with pe.Fori(0, HEADS - 1) as i:
                cross_head(i, False)
            cross_head(HEADS - 1, True)

            output_projection(N_XO, xo_taken, xo_done, CROSS_EARLY, CROSS_READY)
            norm_sums(NORM_FFN, T)

            def unit(n, j, h):
                pe.wait_ge(unit_taken, n * 2 + (h + 1))
                out = bank[(2 * j + h) % 4][:, 0:HT]
                if h == 0:
                    halves_ready(n + FRONT)
                for c in range(C):
                    m = product(out, j % 2, c, h, c == 0, c == C - 1)
                m.then_inc(unit_done, 1)

            with pe.Fori(0, PH // 2) as i:
                for j in range(2):
                    for s in range(2):
                        if j == 0 and s == 0:
                            pe.wait_ge(unit_taken, i * 8 + 2)
                            halves_ready(i * 4 + FRONT)
                            as_normed(bank[0:2], 0, NORM_FFN, 2, unit_done)
                        else:
                            for h in range(2):
                                unit(i * 4 + (2 * j + s), 2 * j + s, h)
                    pe.wait_ge(pk_landed[j], (i + 1) * 16)
                    pe.wait_ge(unit_taken, i * 8 + (4 * j + 4 + 4))
                    pe.wait_ge(sc_taken, i * 2 + (j + 1))
                    for s in range(2):
                        for t in range(NT):
                            rows = TILES[t][1]
                            o = bank[4 + s][:, t * P:(t + 1) * P] if t < 4 else bank[6][0:rows, s * P:(s + 1) * P]
                            m = pe.matmul(o, qpT[:, s, tile_cols(t)], pk[:, j, s], start=True, stop=True)
                    m.then_inc(sc_ready, 1)

            def first_products(g, j):
                for h in range(2):
                    unit(g * GROUP + (NPQ + j), j, h)

            pe.wait_ge(sc_taken, 1 + PH)
            with pe.Fori(0, U1_GROUPS - 1) as i:
                for j in range(GROUP):
                    first_products(i, j)

            pe.wait_ge(sel_ready, NT)
            for t in range(NT):
                for k in range(3):
                    n = t * 3 + k
                    m = pe.transpose(bank[4 + n // 4][:, (n % 4) * P:(n % 4 + 1) * P], sel[:, t, k], ident[:])
            m.then_inc(selT_ready, 1)
            for j in range(GROUP):
                first_products(U1_GROUPS - 1, j)
            pe.wait_ge(selT_taken, 1)

            def gate_products(c, j):
                pe.wait_ge(hot_ready, (c * GROUP) + j + 1)
                for b in range(2):
                    pe.wait_ge(g_taken, (c * GROUP + j) * 2 + (b + 1))
                    for k in range(4):
                        for q in range(3):
                            m = pe.matmul(bank[4 + b][:, k * P:(k + 1) * P], hot2[:, j % 2, 4 * b + k],
                                          gated[:, j % 2, q, 4 * b + k], start=q == 0, stop=q == 2)
                    m.then_inc(g_ready, 1)

            with pe.Fori(0, U2_GROUPS) as i:
                for j in range(GROUP):
                    first_products(i + U1_GROUPS, j)
                    gate_products(i, j)
            with pe.Fori(0, U3_GROUPS) as i:
                for j in range(GROUP):
                    first_products(i + (KEYS // GROUP - U3_GROUPS), j)

            pe.wait_ge(unit_taken, 4 + 2 * (NPQ + KEYS))
            pe.wait_ge(g_taken, 2 + 2 * GROUP * NCHUNK)
            with pe.Fori(0, KEYS // GROUP // 2) as i:
                for p in range(2):
                    pe.wait_ge(lo_ready, i * 8 + (FRONT + NPQ + KEYS + 4 * (p + 1)))
                    pe.wait_ge(w_ready, (i * 2 + p + 2) * GROUP)
                    for n in range(2 * C):
                        b, h = n // 2, n % 2
                        pe.wait_ge(y_taken, (i * 2 + p) * (2 * C) + (n + 1))
                        for j in range(GROUP):
                            m = passes(bank[n % 8][:, 0:HT], vs[p][0][:, j, b * P:(b + 1) * P],
                                       vs[p][1][:, j, b * P:(b + 1) * P], wbs[p][0][:, j, half(h)],
                                       wbs[p][1][:, j, half(h)], j == 0, j == GROUP - 1)
                        m.then_inc(y_ready, 1)
            pe.wait_ge(y_taken, 8 + 2 * C * KEYS // GROUP)
            norm_sums(NORM_FINAL, T)

        @block.scalar
        def _(act):
            def squares(chunk, src, n, parity):
                act.wait_ge(sq_used, chunk + 1)
                act.activation(sq[:, parity, 0:n], src, ACT.Square).then_inc(sq_ready, 1)

            def roots(k, n):
                if k:
                    act.wait_ge(h_ready, C * k)
                act.wait_ge(sums_ready, k + 1)
                a = None
                for h in range(2 if n == T else 1):
                    w = min(n, HT)
                    a = act.activation(rms[:, h * HT:h * HT + w], bank[6 + h][:, 0:w], ACT.Sqrt, scale=1.0 / D,
                                       bias=eps[:, 0:1])
                a.then_inc(rms_ready, 1)

            def split_high(slot, landed, dst_slot):
                act.wait_ge(w_landed[slot], landed)
                act.activation(us[0][:, dst_slot], wring[:, slot], ACT.Copy).then_inc(hi_ready, 1)

            LOADS = {QD: (32, 16), KD: (32, 16), VD: (32, 16), QR: (32, 16), KR: (32, 32),
                     VR: (16, 16), GR: (16, 16)}

            def high_of_head(i, b):
                per_head, first = LOADS[b]
                split_high(RAW_SLOT[b], i * per_head + first, HALF_SLOT[b])

            def high_halves(k):
                for c in range(C):
                    act.wait_ge(hc_ready, C * k + c + 1)
                    act.activation(hs[0][:, c], mixedT[:, c], ACT.Copy).then_inc(hhi_ready, 1)

            def high_mixed(c):
                act.activation(hs[0][:, c], mixedT[:, c], ACT.Copy).then_inc(mixed_high, 1)

            def output_highs(k, taken, done, blocks):
                act.activation(table, eps[:, 0:1], ACT.Sqrt)
                for m in range(C):
                    if blocks[m] is not None:
                        act.wait_ge(done, 2 * (m + 1))
                        split_high(*blocks[m], m % 2)
                    act.wait_ge(taken, 2 * m + 4)
                    squares(C * k + m, xT[:, m], T, m % 2)
                roots(k, T)

            for s, n in ((in_taken, 2), (at_taken, 1), (ro_copied, 1), (drms_ready, 1), (xe_ready, 1),
                         (x_taken, 2), (xt_taken, 1),
                         (unit_taken, 4), (sc_taken, 1), (g_taken, 2)):
                act.sem_inc(s, n)
            for c in range(C):
                if c % 2 == 0:
                    act.wait_ge(x_landed[c // 2], 16)
                squares(C * NORM_MIX + c, xT[:, c], T, c % 2)
                if c == 0:
                    act.activation(table, table, ACT.Sqrt)
            act.wait_ge(const_landed, NCONST)
            roots(NORM_MIX, T)
            high_of_head(0, QD)
            high_halves(0)
            high_of_head(0, KD)
            act.wait_ge(lam_ready, 1)
            act.activation(lam[:, 2:4], lam[:, 0:2], ACT.Exp).then_inc(lam_ready, 1)

            def unit(n, dst, src, fn=ACT.Copy, scale=1.0):
                act.wait_ge(in_done, n)
                act.activation(dst, src, fn, scale=scale).then_inc(in_taken, 1)

            def unit_T(n, dst, fn=ACT.Copy, scale=1.0, first=0):
                for h in range(2):
                    unit(n + h, dst[:, half(h)], bank[(first + h) % 2][:, 0:HT], fn, scale)

            def unit_rows(n, dst):
                unit(n, dst[:, 0:4].rearrange("p t n -> p (t n)"), bank[0][:])
                unit(n + 1, dst[0:TS, 4], bank[1][0:TS, 0:P])

            def mixer_turn(i, last):
                def exps(t):
                    rows = TILES[t][1]
                    keys = (t + 1) * P if t < 4 else PAST + TS
                    act.wait_ge(max_ready, i * NT + (t + 1))
                    for m in range(2):
                        s = S[0:rows, t % 2, m, 0:keys]
                        a = act.activation(s, s, ACT.Exp, scale=DK ** -0.5, bias=nmx[0:rows, t % 2, m:m + 1],
                                           accum_out=rs[0:rows, t % 2, m:m + 1])
                    a.then_inc(e_ready, 1)

                def turned(t):
                    rows = TILES[t][1]
                    act.wait_ge(at_ready, i * NT + (t + 1))
                    if t < 4:
                        a = act.activation(aT[:, 0:(t + 1) * P], bank[4][:, 0:(t + 1) * P], ACT.Copy)
                    else:
                        act.activation(aT[:, 0:rows], bank[4][:, 0:rows], ACT.Copy)
                        a = act.activation(aT[0:TS, P:P + rows], bank[4][0:TS, P:P + rows], ACT.Copy)
                    a.then_inc(at_taken, 1)

                exps(0)
                act.wait_ge(mk_stored, i * 16 + 16)
                unit(made(i, U_MK0), mkT[:, 0], bank[U_MK0 % 2][:, 0:MEM])
                unit_T(made(i, U_QR), qrT, first=U_QR)
                high_of_head(i, VR)
                exps(1)
                turned(0)
                unit_T(made(i, U_KR), krT, scale=P ** -0.5, first=U_KR)
                high_of_head(i, GR)
                exps(2)
                unit(made(i, U_MK1), mkT[:, 1], bank[U_MK1 % 2][:, 0:MEM])
                turned(1)
                unit_T(made(i, U_VR), vT)
                if not last:
                    high_of_head(i + 1, QD)
                else:
                    split_high(1, 16 * (2 * HEADS + 1), 0)
                turned(2)
                unit_rows(made(i, U_VRT), vr)
                exps(3)
                act.wait_ge(mixed_ready, i * 2 + 2)
                unit_T(made(i, U_GR), grT)
                if not last:
                    high_of_head(i + 1, KD)
                else:
                    split_high(2, 16 * (2 * HEADS + 1), 1)
                exps(4)

                def memory_values(b):
                    unit(made(i, U_MV + b), mv[:, :, b * P:(b + 1) * P],
                         bank[b][:, 0:MEM].rearrange("p (m n) -> p m n", m=2))

                act.wait_ge(mv_stored, i * 16 + 16)
                memory_values(0)
                if last:
                    for c in MIXED_EARLY[:3]:
                        high_mixed(c)
                turned(3)
                memory_values(1)
                if last:
                    for c in MIXED_EARLY[3:]:
                        high_mixed(c)
                turned(4)
                act.wait_ge(in_done, made(i, U_KT + 1))
                act.wait_ge(par_ready, i + 1)
                act.activation(kn[:, 0:4].rearrange("p t n -> p (t n)"), bank[0][:], ACT.Copy,
                               scale=hp[:, TAIL:TAIL + 1])
                act.activation(kn[0:TS, 4], bank[1][0:TS, 0:P], ACT.Copy,
                               scale=hp[0:TS, TAIL_S:TAIL_S + 1]).then_inc(in_taken, 2)
                act.activation(grT[:], grT[:], ACT.Silu).then_inc(gate_ready, 1)
                act.activation(table, eps[:, 0:1], ACT.Sqrt)
                act.wait_ge(pv_taken, (i + 1) * NT + 2)
                act.activation(sqo[:], od[:], ACT.Square).then_inc(dsq_ready, 1)
                if not last:
                    unit_T(made(i, U_QD), qdT)
                    high_of_head(i + 1, VD)
                act.wait_ge(dss_ready, i * 2 + 1)
                sc2 = (1.0 - LAM_INIT) ** 2
                act.activation(rmo[:, 0:HT], bank[6][:, 0:HT], ACT.Sqrt, scale=1.0 / (P * sc2), bias=eps[:, 1:2])
                act.activation(rmo[:, HT:T], bank[7][:, 0:HT], ACT.Sqrt, scale=1.0 / (P * sc2),
                               bias=eps[:, 1:2]).then_inc(drms_ready, 1)
                act.wait_ge(ro_ready, i + 1)
                act.activation(ro[:, 0:TP], bank[2][:], ACT.Copy)
                act.activation(ro[:, TP:T], bank[3][:, 0:TS], ACT.Copy).then_inc(ro_copied, 1)
                if not last:
                    act.wait_ge(kd_stored, i * 16 + 32)
                    unit_T(made(i, U_KD), kdT)
                    high_of_head(i + 1, KR)
                act.wait_ge(oc_ready, i + 1)
                act.activation(sqo[:], ro[:], ACT.Square).then_inc(dsq_ready, 1)
                if not last:
                    unit_T(made(i, U_VD), vT)
                    high_of_head(i + 1, QR)
                else:
                    act.wait_ge(mixed_ready, 2 + 2 * HEADS - 1)
                    high_mixed(MIXED_LAST[0])
                act.wait_ge(dss_ready, i * 2 + 2)
                act.wait_ge(mixed_ready, i * 2 + 3)
                act.activation(rmo[:, 0:HT], bank[6][:, 0:HT], ACT.Sqrt, scale=1.0 / P, bias=eps[:, 0:1])
                act.activation(rmo[:, HT:T], bank[7][:, 0:HT], ACT.Sqrt, scale=1.0 / P,
                               bias=eps[:, 0:1]).then_inc(drms_ready, 1)
                if not last:
                    act.wait_ge(vd_stored, i * 32 + 64)
                    unit_rows(made(i, U_VDT), vd)
                    act.activation(table, eps[:, 0:1], ACT.Exp)
                else:
                    act.wait_ge(mixed_ready, 2 + 2 * HEADS)
                    high_mixed(MIXED_LAST[1])

            unit_T(1, qdT)
            high_of_head(0, VD)
            act.wait_ge(mem_landed, 16)
            for c in range(C):
                squares(C * NORM_MEM + c, memT[:, c], MEM, c % 2)
            unit_T(3, kdT)
            high_of_head(0, KR)
            roots(NORM_MEM, MEM)
            unit_T(5, vT)
            high_of_head(0, QR)
            unit_rows(7, vd)
            with act.Fori(0, HEADS - 1) as i:
                mixer_turn(i, False)
            mixer_turn(HEADS - 1, True)

            blocks = [((b + 1) % 4, 16 * (2 * HEADS + 1 + b // 4)) for b in range(2, C)]
            output_highs(NORM_CROSS, wo_taken, wo_done, blocks + [(XQ + b, 16 * (HEADS + 1)) for b in range(2)])
            high_halves(1)
            act.activation(table, eps[:, 0:1], ACT.Exp)

            xq_next = (qrT, krT)

            def query_unit(turn, k):
                b, h = k // 2, k % 2
                act.wait_ge(x_done, turn * 4 + (k + 1))
                act.activation(xq_next[b][:, half(h)], bank[h][:, 0:HT], ACT.Copy).then_inc(x_taken, 1)

            def block_after(turn, b):
                split_high(XQ + b, turn * 16 + 16 * (HEADS + 2), b)

            def cross_head(i, last):
                def xexp(t):
                    rows = TILES[t][1]
                    act.wait_ge(xmax_ready, i * NT + (t + 1))
                    act.activation(E[0:rows, t % 2], bank[2 + t % 2][0:rows, 0:MEM], ACT.Exp,
                                   scale=(D // HEADS) ** -0.5, bias=xn[0:rows, t % 2:t % 2 + 1],
                                   accum_out=xr[0:rows, t % 2:t % 2 + 1]).then_inc(xe_ready, 1)

                def xturned(t):
                    rows = TILES[t][1]
                    act.wait_ge(xt_ready, i * NT + (t + 1))
                    act.activation(eT[:].rearrange("p (k n) -> p k n", k=2)[:, :, 0:rows],
                                   bank[4][:, 0:2 * P].rearrange("p (k n) -> p k n", k=2)[:, :, 0:rows],
                                   ACT.Copy).then_inc(xt_taken, 1)

                def next_queries(k):
                    if not last:
                        query_unit(i + 1, k)
                    elif k < 3:
                        for c in CROSS_EARLY[2 * k:2 * k + 2]:
                            high_mixed(c)

                if last:
                    act.wait_ge(xpv_taken, 2 + (HEADS - 1) * NT)
                xexp(0)
                xexp(1)
                next_queries(0)
                for t in range(NT):
                    xturned(t)
                    if t + 2 < NT:
                        xexp(t + 2)
                        next_queries(t + 1)
                    if t % 2 and not last:
                        block_after(i + 1, t // 2)

            for k in range(4):
                query_unit(0, k)
                if k % 2:
                    block_after(0, k // 2)
            with act.Fori(0, HEADS - 1) as i:
                cross_head(i, False)
            cross_head(HEADS - 1, True)

            act.wait_ge(xpv_taken, 2 + HEADS * NT)
            for c in CROSS_LAST:
                high_mixed(c)
            blocks = [(XO_SLOT[b], 16 * XO_TURN[b]) for b in range(2, C)]
            output_highs(NORM_FFN, xo_taken, xo_done, blocks + [(0, 16 * PQ_TURN[0]), None])

            def high(n, slot, landed, dst):
                act.wait_ge(w_landed[slot], landed)
                act.wait_ge(unit_done, n * 2 + 2)
                act.activation(dst, wring[:, slot], ACT.Copy).then_inc(hi_ready, 1)

            high_halves(2)

            with act.Fori(0, PH // 2) as i:
                for j in range(2):
                    for s in range(2):
                        b = 2 * j + s
                        high(i * 4 + (b + 1), (b + 1) % 4, i * 16 + 16 * (PQ_TURN[(b + 1) % 4] + (b == 3)), us[0][:, (b + 1) % 2])
                        for h in range(2):
                            act.wait_ge(unit_done, i * 8 + (4 + 2 * b + h + 1))
                            act.activation(qpT[:, s, half(h)], bank[(2 * b + h) % 4][:, 0:HT],
                                           ACT.Copy).then_inc(unit_taken, 1)
                    act.wait_ge(sc_ready, i * 2 + (j + 1))
                    mine = sc[:, bass.ds(i * 2 + j, 1)].rearrange("p h s t n -> p (h s) t n")
                    for s in range(2):
                        act.activation(mine[:, s, 0:4].rearrange("p t n -> p (t n)"), bank[4 + s][:], ACT.Copy)
                    act.activation(mine[0:TS, :, 4], bank[6][0:TS, 0:2 * P].rearrange("p (s n) -> p s n", s=2),
                                   ACT.Copy).then_inc(sc_taken, 1)

            def next_high(g, j):
                high(g * GROUP + (NPQ + j + 1), (j + 1) % 4, g * 16 + 16 * (PQ_TURN[(j + 1) % 4] + NPQ // 4 + (j == 3)),
                     us[0][:, (j + 1) % 2])

            def gelu(g, j):
                for h in range(2):
                    act.wait_ge(unit_done, (g * GROUP + (NPQ + j)) * 2 + (4 + h + 1))
                    if h == 0:
                        act.wait_ge(act_stored[j], (g + 1) * 16)
                    act.activation(actb[:, j, half(h)], bank[(2 * j + h) % 4][:, 0:HT],
                                   ACT.Gelu).then_inc(unit_taken, 1)

            def activations(g, j):
                next_high(g, j)
                gelu(g, j)

            with act.Fori(0, U1_GROUPS - 2) as i:
                for j in range(GROUP):
                    activations(i, j)

            act.wait_ge(dif_ready, 1)
            act.activation(best[:].rearrange("p t h k -> p (t h k)"), best[:].rearrange("p t h k -> p (t h k)"),
                           ACT.Exp).then_inc(gexp_ready, 1)
            for j in range(GROUP):
                activations(U1_GROUPS - 2, j)
            act.wait_ge(selT_ready, 1)
            for t in range(NT):
                for k in range(3):
                    n = t * 3 + k
                    a = act.activation(selT[:, k, t * P:(t + 1) * P],
                                       bank[4 + n // 4][:, (n % 4) * P:(n % 4 + 1) * P], ACT.Copy)
            a.then_inc(selT_taken, 1)
            for j in range(GROUP):
                activations(U1_GROUPS - 1, j)

            def gate_chunk(c, p, turn):
                for j in range(GROUP):
                    activations(c + U1_GROUPS, j)
                    for b in range(2):
                        act.wait_ge(g_ready, 4 + (c * GROUP + j) * 2 + (b + 1))
                        if j == 0 and b == 0:
                            act.wait_ge(g_stored[p], turn)
                        t0 = j * TOK8 + 4 * b
                        act.activation(gst[:, p, :, t0:t0 + 4].rearrange("p k t -> p t k"),
                                       bank[4 + b][:].rearrange("p (t k) -> p t k", t=4),
                                       ACT.Copy).then_inc(g_taken, 1)

            with act.Fori(0, NCHUNK // 2) as i:
                for p in range(2):
                    gate_chunk(i * 2 + p, p, (i + 1) * 16)
            gate_chunk(NCHUNK - 1, 0, (NCHUNK // 2 + 1) * 16)
            def v_high(g, p, j):
                act.wait_ge(w_landed[j], g * 16 + 16 * (PQ_TURN[j] + NPQ // 4 + KEYS // GROUP))
                if j == 0:
                    act.wait_ge(y_ready, g * 16 + 16)
                act.activation(vs[p][0][:, j].rearrange("p (c n) -> p c n", c=C), wring[:, j],
                               ACT.Copy).then_inc(hi_ready, 1)

            def w_high(g, p, j):
                act.wait_ge(wf_ready, g * GROUP + (j + 1))
                act.activation(wbs[p][0][:, j], wf[:, j % 2], ACT.Copy).then_inc(whi_ready, 1)

            def second_group(g, p):
                for j in range(GROUP):
                    v_high(g, p, j)
                for j in range(GROUP):
                    w_high(g, p, j)

            for j in range(GROUP):
                activations(KEYS // GROUP - 2, j)
            g = KEYS // GROUP - 1
            activations(g, 0)
            activations(g, 1)
            for k in range(GROUP):
                w_high(0, 0, k)
            next_high(g, 2)
            for k in range(3):
                v_high(0, 0, k)
            gelu(g, 2)
            v_high(0, 0, 3)
            gelu(g, 3)
            with act.Fori(0, KEYS // GROUP // 2 - 1) as i:
                second_group(i * 2 + 1, 1)
                second_group(i * 2 + 2, 0)
            second_group(KEYS // GROUP - 1, 1)

            act.activation(table, eps[:, 0:1], ACT.Sqrt)
            for c in range(C):
                act.wait_ge(y_taken, 8 + 2 * C * (KEYS // GROUP - 1) + 2 * (c + 1))
                squares(C * NORM_FINAL + c, xT[:, c], T, c % 2)
            roots(NORM_FINAL, T)

        @block.vector
        def _(dve):
            step = Steps(dve, vec)

            def add_squares(chunk, n, parity):
                dve.wait_ge(sq_ready, chunk + 1)
                dve.tensor_tensor(sq_sum[:, 0:n], sq_sum[:, 0:n], sq[:, parity, 0:n], ALU.add).then_inc(sq_used, 1)
                dve.wait_ge(sq_used, chunk + 3)

            def no_squares():
                step.link(dve.memset(sq_sum[:], 0))

            def normed(k, src, dst, n):
                dve.wait_ge(rms_ready, k + 1)
                step.link(dve.reciprocal(rms[:, 0:n], rms[:, 0:n]))
                for c in range(C):
                    dve.scalar_tensor_tensor(out=dst[:, c], in0=src[:, c], scalar=gains[:, k, c:c + 1],
                                             in1=rms[:, 0:n], op0=ALU.mult, op1=ALU.mult).then_inc(h_ready, 1)
                if k != NORM_FINAL:
                    no_squares()

            def normed_halves(k, before):
                dve.wait_ge(rms_ready, k + 1)
                step.link(dve.reciprocal(rms[:], rms[:]))

                def low_half(c):
                    dve.wait_ge(hhi_ready, C * before + c + 1)
                    dve.tensor_tensor(hs[1][:, c], mixedT[:, c], hs[0][:, c].bitcast(F32),
                                      ALU.subtract).then_inc(h_ready, 2)

                for c in range(C):
                    if c >= 2 and c % 2 == 0:
                        low_half(c - 2)
                    dve.scalar_tensor_tensor(out=mixedT[:, c], in0=xT[:, c], scalar=gains[:, k, c:c + 1],
                                             in1=rms[:], op0=ALU.mult, op1=ALU.mult).then_inc(hc_ready, 1)
                low_half(C - 2)
                no_squares()

            def low_last(c, high):
                dve.wait_ge(mixed_high, high)
                dve.tensor_tensor(hs[1][:, c], mixedT[:, c], hs[0][:, c].bitcast(F32),
                                  ALU.subtract).then_inc(last_low, 1)

            for s, n in ((s_taken, 1), (pv_taken, 2), (mixed_ready, 2), (wo_taken, 2), (xo_taken, 2),
                         (xpv_taken, 2), (y_taken, 8), (w_ready, GROUP)):
                dve.sem_inc(s, n)
            step.link(dve.memset(table, 1.0))
            dve.sem_inc(sq_used, 2)
            no_squares()
            for c in range(C):
                add_squares(C * NORM_MIX + c, T, c % 2)
            dve.wait_ge(const_landed, NCONST)
            for m in range(2):
                a = dve.tensor_tensor_reduce(out=lam_in[:, 2 * m], in0=lam_in[:, 2 * m], in1=lam_in[:, 2 * m + 1],
                                             scale=1.0, scalar=0.0, op0=ALU.mult, op1=ALU.add,
                                             accum_out=lam[:, m:m + 1])
            a.then_inc(lam_ready, 1)
            normed_halves(NORM_MIX, 0)
            dve.wait_ge(lam_ready, 2)
            step.link(dve.tensor_tensor(lam[:, 0:1], lam[:, 3:4], lam[:, 2:3], ALU.subtract))
            step.link(dve.tensor_scalar(lam[:, 0:1], lam[:, 0:1], -LAM_INIT, None, ALU.add))
            dve.wait_ge(mem_landed, 16)
            for c in range(C):
                add_squares(C * NORM_MEM + c, MEM, c % 2)
            normed(NORM_MEM, memT, memn, MEM)

            def mixer_turn(i, last):
                step.restart()
                step.link(dve.tensor_copy(hp[:], par[:, i]))
                dve.sem_inc(par_ready, 1)

                def biased(t):
                    rows = TILES[t][1]
                    keys = (t + 1) * P if t < 4 else PAST + TS
                    far = dist[:, TP - keys:TP] if t < 4 else dist_s[0:rows, :]
                    dve.wait_ge(s_ready, i * NT + (t + 1))
                    for m in range(2):
                        a = dve.scalar_tensor_tensor(out=S[0:rows, t % 2, m, 0:keys], in0=far,
                                                     scalar=hp[0:rows, SLOPE8:SLOPE8 + 1],
                                                     in1=bank[2 + m][0:rows, 0:keys], op0=ALU.mult, op1=ALU.add)
                    a.then_inc(s_taken, 1)
                    dve.wait_ge(s_taken, i * NT + (t + 2))
                    step.link(dve.tensor_reduce(mx[0:rows, t % 2], S[0:rows, t % 2, :, 0:keys], AX_X, ALU.max))
                    dve.tensor_scalar(nmx[0:rows, t % 2], mx[0:rows, t % 2], -DK ** -0.5, None,
                                      ALU.mult).then_inc(max_ready, 1)

                def combined(t):
                    rows = TILES[t][1]
                    keys = (t + 1) * P if t < 4 else PAST + TS
                    dve.wait_ge(e_ready, i * NT + (t + 1))
                    r = ri[0:rows, t % 2]
                    step.link(dve.reciprocal(r, rs[0:rows, t % 2]))
                    step.link(dve.tensor_scalar(r[:, 1:2], r[:, 1:2], lam[0:rows, 0:1], None, ALU.mult))
                    s0, s1 = S[0:rows, t % 2, 0, 0:keys], S[0:rows, t % 2, 1, 0:keys]
                    step.link(dve.tensor_scalar(s0, s0, r[:, 0:1], None, ALU.mult))
                    dve.scalar_tensor_tensor(out=s0, in0=s1, scalar=r[:, 1:2], in1=s0, op0=ALU.mult,
                                             op1=ALU.add).then_inc(a_ready, 1)

                def output(t):
                    rows = TILES[t][1]
                    dve.wait_ge(pv_ready, i * NT + (t + 1))
                    dve.tensor_copy(od[:, tile_cols(t)],
                                    bank[5 + t % 2][:, 0:rows]).then_inc(pv_taken, 1)

                for t in range(NT):
                    biased(t)
                    if t >= 2:
                        output(t - 2)
                    combined(t)
                output(3)
                dve.wait_ge(in_taken, in_sbuf(i, U_QR + 1))
                dve.tensor_tensor(qs[:, 0:TP].rearrange("p (c n) -> p c n", c=4),
                                  qrT[:, 0:TP].rearrange("p (c n) -> p c n", c=4),
                                  cross_scale[:, i][:, None, :].to_broadcast([P, 4, P]), ALU.mult)
                dve.tensor_tensor(qs[:, TP:T], qrT[:, TP:T], cross_scale[:, i, 0:TS], ALU.mult)
                dve.wait_ge(inner_ready, i + 1)
                dve.tensor_tensor(im[:, 0:TP].rearrange("p (c n) -> p c n", c=4),
                                  bank[2][:].rearrange("p (c n) -> p c n", c=4),
                                  decay[:, i][:, None, :].to_broadcast([P, 4, P]), ALU.mult)
                dve.tensor_tensor(im[0:TS, TP:T], bank[3][0:TS, 0:TS], decay[0:TS, i, 0:TS],
                                  ALU.mult).then_inc(im_ready, 1)
                output(4)
                dve.wait_ge(u_ready, i + 1)
                dve.wait_ge(cache_landed, (i + 1) * 48)
                dve.wait_ge(st_stored, i * 32 + 32)
                step.link(dve.tensor_copy(st[:, 0], bank[4][:, 0:P]))
                for t in range(1, 4):
                    step.link(dve.scalar_tensor_tensor(out=st[:, t], in0=st[:, t - 1],
                                                       scalar=hp[:, GAMMA_L:GAMMA_L + 1],
                                                       in1=bank[4][:, t * P:(t + 1) * P], op0=ALU.mult, op1=ALU.add))
                dve.scalar_tensor_tensor(out=st[:, 4], in0=st_in[:], scalar=hp[:, GAMMA_LS:GAMMA_LS + 1],
                                         in1=bank[7][:, 0:P], op0=ALU.mult, op1=ALU.add).then_inc(st_ready, 1)
                dve.wait_ge(drms_ready, i * 2 + 2)
                step.link(dve.reciprocal(rmo[:], rmo[:]))
                dve.scalar_tensor_tensor(out=mixedT[:, i], in0=od[:], scalar=hp[:, G_DA:G_DA + 1], in1=rmo[:],
                                         op0=ALU.mult, op1=ALU.mult).then_inc(mixed_ready, 1)
                dve.wait_ge(mean_ready, i + 1)
                for h in range(2):
                    a = dve.scalar_tensor_tensor(out=ro[:, half(h)], in0=bank[6 + h][:, 0:HT], scalar=-1.0 / P,
                                                 in1=ro[:, half(h)], op0=ALU.mult, op1=ALU.add)
                a.then_inc(oc_ready, 1)
                if last:
                    low_last(MIXED_LAST[0], len(MIXED_EARLY) + 1)
                dve.wait_ge(drms_ready, i * 2 + 3)
                step.link(dve.reciprocal(rmo[:], rmo[:]))
                step.link(dve.scalar_tensor_tensor(out=ro[:], in0=ro[:], scalar=hp[:, G_RET:G_RET + 1], in1=rmo[:],
                                                   op0=ALU.mult, op1=ALU.mult))
                dve.wait_ge(gate_ready, i + 1)
                dve.tensor_tensor(mixedT[:, HEADS + i], ro[:], grT[:], ALU.mult).then_inc(mixed_ready, 1)
                if last:
                    low_last(MIXED_LAST[1], len(MIXED_EARLY) + 2)

            with dve.Fori(0, HEADS - 1) as i:
                mixer_turn(i, False)
            mixer_turn(HEADS - 1, True)

            def residual(k, done, taken):
                with dve.Fori(0, 2) as i:
                    for b in range(4):
                        for h in range(2):
                            dve.wait_ge(done, i * 8 + (2 * b + h + 1))
                            x = xT[:, i * 4 + b, half(h)]
                            dve.tensor_tensor(x, bank[h][:, 0:HT], x, ALU.add).then_inc(taken, 1)
                        add_squares(i * 4 + (C * k + b), T, b % 2)

            residual(NORM_CROSS, wo_done, wo_taken)
            normed_halves(NORM_CROSS, 1)

            def queries(turn):
                dve.wait_ge(x_taken, turn * 4 + 4 + 2)
                dve.tensor_copy(xqT[:, 0], qrT[:])
                dve.tensor_copy(xqT[:, 1], krT[:]).then_inc(xq_ready, 1)

            queries(0)

            def cross_head(i, last):
                step.restart()

                def xmax(t):
                    rows = TILES[t][1]
                    dve.wait_ge(xs_ready, i * NT + (t + 1))
                    step.link(dve.tensor_reduce(xm[0:rows, t % 2:t % 2 + 1], bank[2 + t % 2][0:rows, 0:MEM],
                                                AX_X, ALU.max))
                    dve.tensor_scalar(xn[0:rows, t % 2:t % 2 + 1], xm[0:rows, t % 2:t % 2 + 1],
                                      -(D // HEADS) ** -0.5, None, ALU.mult).then_inc(xmax_ready, 1)

                def xnorm(t):
                    rows = TILES[t][1]
                    dve.wait_ge(xe_ready, i * NT + (t + 2))
                    r = xr[0:rows, t % 2:t % 2 + 1]
                    step.link(dve.reciprocal(r, r))
                    dve.tensor_scalar(E[0:rows, t % 2], E[0:rows, t % 2], r, None, ALU.mult).then_inc(xp_ready, 1)

                def xoutput(t):
                    rows = TILES[t][1]
                    dve.wait_ge(xpv_ready, i * NT + (t + 1))
                    dve.tensor_scalar(mixedT[:, bass.ds(i * 2, 2), tile_cols(t)],
                                      bank[5 + t % 2][:, 0:2 * P].rearrange("p (b n) -> p b n", b=2)[:, :, 0:rows],
                                      1.0, None, ALU.mult).then_inc(xpv_taken, 1)

                xmax(0)
                xmax(1)
                for t in range(NT):
                    xnorm(t)
                    if t + 2 < NT:
                        xmax(t + 2)
                    if t >= 1:
                        xoutput(t - 1)
                if not last:
                    queries(i + 1)
                xoutput(NT - 1)

            with dve.Fori(0, HEADS - 1) as i:
                cross_head(i, False)
            cross_head(HEADS - 1, True)
            for k, c in enumerate(CROSS_LAST):
                low_last(c, C + len(CROSS_EARLY) + k + 1)

            residual(NORM_FFN, xo_done, xo_taken)
            results_stored(dve)
            step.restart()
            normed_halves(NORM_FFN, 2)

            for x in (v16, i16, c16, p16):
                a = step.link(dve.memset(x[:], 0))

            def top16(vals, idx, src, spare):
                step.link(dve.max(vals[:, 0:8], src))
                step.link(dve.max_index(idx[:, 0:8], vals[:, 0:8], src))
                step.link(dve.match_replace(spare, vals[:, 0:8], src, FLOOR))
                step.link(dve.max(vals[:, 8:16], spare))
                step.link(dve.max_index(idx[:, 8:16], vals[:, 8:16], spare))

            with dve.Fori(0, PH // 2) as i:
                step.restart()
                for j in range(2):
                    dve.wait_ge(sc_taken, i * 2 + (j + 2))
                    dve.sem_inc(passed, 1)
                    mine = sc[:, bass.ds(i * 2 + j, 1)].rearrange("p h s t n -> p (h s) t n")
                    dve.tensor_scalar(scores_now[:, :, 0:4], mine[:, :, 0:4], 1.0, None, ALU.mult)
                    step.link(dve.tensor_scalar(scores_now[0:TS, :, 4], mine[0:TS, :, 4], 1.0, None, ALU.mult))
                    for s in range(2):
                        for t in range(NT):
                            rows = TILES[t][1]
                            top16(v16[0:rows, s, t], i16[0:rows, s, t], scores_now[0:rows, s, t], scr[0:rows, 0:KEYS])
                    for t in range(NT):
                        rows = TILES[t][1]
                        step.link(dve.tensor_tensor(cand[0:rows],
                                                    v16[0:rows, 0, t][:, :, None].to_broadcast([rows, TOPK, TOPK]),
                                                    v16[0:rows, 1, t][:, None, :].to_broadcast([rows, TOPK, TOPK]),
                                                    ALU.add))
                        top16(c16[0:rows, t], p16[0:rows, t], cand[0:rows].rearrange("p a b -> p (a b)"),
                              scr[0:rows, :])
                    p = i * 2 + j
                    dve.tensor_copy(best[:, :, p], c16[:])
                    dve.tensor_copy(pos[:, :, p], p16[:])
                    dve.tensor_copy(key1[:, :, p], i16[:, 0])
                    step.link(dve.tensor_copy(key2[:, :, p], i16[:, 1]))

            with dve.Fori(0, NT) as i:
                step.restart()
                at = pos[:, i].rearrange("p h k -> p (h k)")
                dve.tensor_scalar(rank[:, 0], at, 4, None, ALU.logical_shift_right)
                step.link(dve.tensor_scalar(rank[:, 1], at, TOPK - 1, None, ALU.bitwise_and))
                step.link(dve.tensor_copy(rankf[:], rank[:]))
                for s, key in ((0, key1), (1, key2)):
                    step.link(dve.tensor_tensor(hit[:], rankf[:, s][:, :, None].to_broadcast([P, PH * TOPK, TOPK]),
                                                iota[:, 0:TOPK][:, None, :].to_broadcast([P, PH * TOPK, TOPK]),
                                                ALU.is_equal))
                    h4 = hit[:].rearrange("p (h k) a -> p h k a", h=PH)
                    step.link(dve.tensor_tensor(h4, h4, key[:, i][:, :, None, :].to_broadcast([P, PH, TOPK, TOPK]),
                                                ALU.mult))
                    step.link(dve.tensor_reduce(sel[:, i, s], hit[:], AX_X, ALU.add))
                step.link(dve.tensor_tensor(dif[:], best[:, i],
                                            best[:, i, :, 0:1].to_broadcast([P, PH, TOPK]), ALU.subtract))
                step.link(dve.tensor_copy(best[:, i], dif[:]))
            dve.sem_inc(dif_ready, 1)
            dve.wait_ge(gexp_ready, 1)
            for t in range(NT):
                step.link(dve.tensor_reduce(gsum[:], best[:, t], AX_X, ALU.add))
                step.link(dve.reciprocal(gsum[:], gsum[:]))
                dve.tensor_tensor(sel[:, t, 2].rearrange("p (h k) -> p h k", h=PH), best[:, t],
                                  gsum[:][:, :, None].to_broadcast([P, PH, TOPK]), ALU.mult).then_inc(sel_ready, 1)
                dve.wait_ge(sel_ready, t + 1)

            dve.wait_ge(selT_taken, 1)
            for q in range(3):
                step.link(dve.tensor_copy(pieces[:, q], selT[:, 2]))
                if q < 2:
                    step.link(dve.tensor_tensor(selT[:, 2], selT[:, 2], pieces[:, q], ALU.subtract))
            with dve.Fori(0, NCHUNK) as i:
                step.restart()
                for j in range(GROUP):
                    dve.wait_ge(g_ready, (i * GROUP + j) * 2 + 2)
                    tok = bass.ds(i * CTOK + j * TOK8, TOK8)

                    def spread(k):
                        return selT[:, k, tok][:, :, None].to_broadcast([P, TOK8, KEYS])

                    every = iota[:][:, None, :].to_broadcast([P, TOK8, KEYS])
                    step.link(dve.tensor_tensor(hot1[:, j % 2], every, spread(0), ALU.is_equal))
                    dve.tensor_tensor(hot2[:, j % 2], every, spread(1), ALU.is_equal)
                    for q in range(3):
                        a = dve.tensor_tensor(gated[:, j % 2, q], hot1[:, j % 2],
                                              pieces[:, q, tok][:, :, None].to_broadcast([P, TOK8, KEYS]), ALU.mult)
                    a.then_inc(hot_ready, 1)

            def weighted(g, p, turn):
                def low_half(j):
                    dve.wait_ge(whi_ready, g * GROUP + (j + 1))
                    dve.tensor_tensor(wbs[p][1][:, j], wf[:, j % 2], wbs[p][0][:, j].bitcast(F32),
                                      ALU.subtract).then_inc(w_ready, 1)

                dve.wait_ge(ag_landed[p], turn)
                dve.wait_ge(y_ready, g * 16 + 16)
                for j in range(GROUP):
                    if j >= 2:
                        low_half(j - 2)
                        dve.wait_ge(w_ready, g * GROUP + (GROUP + j - 1))
                    elif j == 0:
                        dve.wait_ge(w_ready, g * GROUP + 4)
                    dve.tensor_tensor(wf[:, j % 2].rearrange("p (c t) -> p c t", c=NCHUNK),
                                      aring[p][:, j].rearrange("p (c t) -> p c t", c=NCHUNK),
                                      gring[p][:, :, j * CTOK:(j + 1) * CTOK], ALU.mult).then_inc(wf_ready, 1)
                low_half(GROUP - 2)
                low_half(GROUP - 1)

            def add_products(g, units=range(2 * C), last=False):
                for n in units:
                    b, h = n // 2, n % 2
                    dve.wait_ge(y_ready, g * 16 + (32 + n + 1))
                    dve.tensor_tensor(xT[:, b, half(h)], bank[n % 8][:, 0:HT], xT[:, b, half(h)],
                                      ALU.add).then_inc(y_taken, 1)
                    if last and h == 1:
                        add_squares(C * NORM_FINAL + b, T, b % 2)

            pairs = KEYS // GROUP // 2
            weighted(0, 0, 32)
            add_products(0, range(8))
            weighted(1, 1, 32)
            add_products(0, range(8, 2 * C))
            with dve.Fori(0, pairs - 1) as i:
                weighted(i * 2 + 2, 0, (i + 2) * 32)
                add_products(i * 2 + 1)
                weighted(i * 2 + 3, 1, (i + 2) * 32)
                add_products(i * 2 + 2)
            add_products(2 * pairs - 1, last=True)
            dve.wait_ge(y_taken, 8 + 16 * 2 * pairs)
            normed(NORM_FINAL, xT, yT, T)


def kernel(**inputs):
    import concourse.bacc as _bacc
    from concourse.bass_utils import run_bass_kernel_spmd as _run

    a = {k: np.asarray(v) for k, v in inputs.items()}

    def chunked(w):
        k, n = w.shape
        return w.reshape(k // P, P, n // P, P).transpose(2, 1, 0, 3)

    def features(x):
        return x.T.reshape(-1, P, x.shape[0]).transpose(1, 0, 2)

    x = np.concatenate([a["x_prompt"][0], a["x_sample"][0]], 0)
    w_in = a["w_in"][0].reshape(C, P, NB_IN, HEADS, P).transpose(3, 2, 1, 0, 4)
    w_x = np.stack([chunked(a[n][0]).reshape(HEADS, 2, P, C, P) for n in ("w_xk", "w_xv", "w_xq")], 1)
    host = {
        "x": features(x),
        "mem": features(a["mem_prompt"][0]),
        "gains": np.stack([g.reshape(C, P).T for g in (a["g_mix"][0], a["g_mem"][0], a["g_cross"][0],
                                                       a["g_ffn"][0], a["g_final"])], 1),
        "lam": np.broadcast_to(np.stack([a[n][0] for n in ("lam_q1", "lam_k1", "lam_q2", "lam_k2")]),
                               (P, 4, DK)),
        "w_in": w_in,
        "w_out": chunked(a["w_out"][0]),
        "w_x": w_x.reshape(HEADS, NB_X, P, C, P),
        "w_xo": chunked(a["w_xo"][0]),
        "w_pq": chunked(a["w_pq"][0]).reshape(PH // 2, 4, P, C, P),
        "keys": np.stack([a["peer_k1"][0], a["peer_k2"][0]], 1).transpose(0, 3, 1, 2).reshape(
            PH // 2, 2, P, 2, KEYS),
        "cache_k": a["cache_da_k"][0, 0].reshape(PAST, HEADS, 2 * DK).transpose(1, 2, 0),
        "cache_v": a["cache_da_v"][0, 0].transpose(1, 0, 2),
        "state": a["state_ret"][0, 0],
        "cache_mem_k": a["cache_mem_k"][0, 0].transpose(1, 2, 0).reshape(HEADS, 2, P, MEM).transpose(0, 2, 1, 3),
        "cache_mem_v": a["cache_mem_v"][0, 0].reshape(2, P, HEADS, MEM).transpose(2, 1, 0, 3),
        "u": a["peer_u"][0].reshape(KEYS // GROUP, GROUP, KEYS, C, P).transpose(0, 1, 4, 3, 2),
        "v": a["peer_v"][0].reshape(KEYS // GROUP, GROUP, KEYS, C, P),
    }
    r = np.arange(P)
    far = -np.abs(r[:, None] - (np.arange(TP)[None, :] - (TP - P))).astype(np.float64)
    ahead = (np.arange(TP)[None, :] - (TP - P)) // CHUNK > r[:, None] // CHUNK
    log_g = np.log1p(-(2.0 ** (-5.0 - np.arange(HEADS))))
    gap = r[None, None, :] - r[:, None, None]
    par = np.zeros((P, HEADS, NPAR))
    par[:, :, SLOPE8] = 2.0 ** (-8.0 * np.arange(1, HEADS + 1) / HEADS) * DK ** 0.5
    par[:, :, GAMMA_L] = np.exp(P * log_g)
    par[:, :, GAMMA_LS] = np.exp(TS * log_g)
    par[:, :, TAIL] = np.exp((P - 1 - r)[:, None] * log_g)
    par[:, :, TAIL_S] = np.exp(np.maximum(TS - 1 - r, 0)[:, None] * log_g)
    par = par.astype(np.float32)
    par[:, :, G_DA] = a["g_da"][0].T
    par[:, :, G_RET] = a["g_ret"][0].T
    host.update({
        "ident": np.eye(P), "ones": np.ones((P, P)), "iota": np.broadcast_to(r, (P, P)),
        "eps": np.broadcast_to([EPS, EPS / (1.0 - LAM_INIT) ** 2], (P, 2)),
        "par": par,
        "dist": np.where(ahead, NEG, far),
        "dist_s": -np.abs(PAST + np.arange(TS)[:, None] - np.arange(PAST + TS)[None, :]),
        "decay": np.where(gap >= 0, np.exp(np.maximum(gap, 0) * log_g[None, :, None]), 0.0),
        "cross_scale": np.broadcast_to(np.exp((r + 1) * log_g[:, None]), (P, HEADS, P)),
    })
    outs = {
        "y": (P, C, T), "kd_out": (HEADS, P, T), "vd_out": (HEADS, P, 4, P), "vds_out": (HEADS, TS, P),
        "st_out": (HEADS, 2, P, P), "mk_out": (HEADS, P, 2, MEM), "mv_out": (HEADS, P, 2, MEM),
    }
    scratch = {"act": (KEYS // GROUP, GROUP, P, T), "gates": (NCHUNK, P, KEYS // GROUP, GROUP * CTOK)}

    nc = _bacc.Bacc("TRN2", target_bir_lowering=False, num_devices=1)
    arrays, d = {}, {}
    for name, v in host.items():
        arrays["in_" + name] = np.ascontiguousarray(v, dtype=np.float32)
        d[name] = nc.dram_tensor("in_" + name, arrays["in_" + name].shape, F32, kind="ExternalInput").ap()
    for name, shape in outs.items():
        d[name] = nc.dram_tensor("out_" + name, shape, F32, kind="ExternalOutput").ap()
    for name, shape in scratch.items():
        d[name] = nc.dram_tensor("scratch_" + name, shape, F32, kind="Internal").ap()
    encoder_step(nc, d)
    res = _run(nc, [arrays], core_ids=[0]).results[0]
    o = {name: np.asarray(res["out_" + name]) for name in outs}

    y = o["y"].transpose(2, 1, 0).reshape(T, D)
    kd = o["kd_out"].reshape(HEADS, 2, DK, T).transpose(3, 0, 1, 2)
    vd = o["vd_out"].transpose(2, 1, 0, 3).reshape(TP, HEADS, P)
    mk = o["mk_out"].transpose(3, 0, 2, 1).reshape(MEM, HEADS, 2 * P)
    mv = o["mv_out"].transpose(2, 1, 0, 3).reshape(MEM, HEADS, 2 * P)
    return (y[None, :TP], y[None, TP:], kd[None, None, :TP], vd[None, None], o["st_out"][None, None, :, 0],
            mk[None, None], mv[None, None], kd[None, None, TP:],
            o["vds_out"].transpose(1, 0, 2)[None, None], o["st_out"][None, None, :, 1])
```
